# Optimizing a Trainium2 kernel written in Bass

```python
import math
import jax
import jax.numpy as jnp
from jax import lax
import numpy as np

D_MODEL = 1024
BATCH = 1
SEQ = 256
DEPTH = 2

CHUNK = 64
N_MIXERS = 2
N_ATTN_LAYERS = (DEPTH + 1) // 2
N_HGRN_LAYERS = DEPTH // 2

A_HEADS = 8
A_HEAD_DIM = D_MODEL // (2 * A_HEADS)
A_QK_WIDTH = A_HEADS * 2 * A_HEAD_DIM
A_V_WIDTH = A_HEADS * 2 * A_HEAD_DIM
Q_BLOCK = 128
ROT_DIM = A_HEAD_DIM // 4
ROPE_THETA = 500000.0

H_EXPAND = 128
H_HEADS = D_MODEL // H_EXPAND
H_WIDTH = H_HEADS * H_EXPAND
H_VDIM = H_WIDTH // H_HEADS

N_EXPERTS = 64
N_GROUPS = 8
TOPK_GROUP = 4
TOP_K = 8
EXPERT_FF = D_MODEL // 4
ROUTED_SCALE = 2.5
MOE_BLOCK = 256

ALPHA = (2 * DEPTH) ** 0.25
BETA = (8 * DEPTH) ** -0.25
LN_EPS = 1e-5

kernel_name = "hybrid_diffattn_hgrn2_moe_deepnorm"

def layer_norm(x, g, b):
    xf = x.astype(jnp.float32)
    mu = jnp.mean(xf, axis=-1, keepdims=True)
    var = jnp.mean(jnp.square(xf - mu), axis=-1, keepdims=True)
    y = (xf - mu) * lax.rsqrt(var + LN_EPS) * g.astype(jnp.float32) + b.astype(jnp.float32)
    return y.astype(x.dtype)

def rms_norm(x, g):
    xf = x.astype(jnp.float32)
    y = xf * lax.rsqrt(jnp.mean(jnp.square(xf), axis=-1, keepdims=True) + LN_EPS)
    return y * g.astype(jnp.float32)

def rotary_tables(seq):
    pos = jnp.arange(seq, dtype=jnp.float32)
    inv_freq = ROPE_THETA ** (-jnp.arange(0, ROT_DIM, 2, dtype=jnp.float32) / ROT_DIM)
    ang = pos[:, None] * inv_freq[None, :]
    return jnp.cos(ang), jnp.sin(ang)

def partial_rotary(x, cos, sin):
    half = ROT_DIM // 2
    c = cos[None, :, None, :].astype(x.dtype)
    s = sin[None, :, None, :].astype(x.dtype)
    x1, x2, rest = x[..., :half], x[..., half:ROT_DIM], x[..., ROT_DIM:]
    return jnp.concatenate([x1 * c - x2 * s, x2 * c + x1 * s, rest], axis=-1)

def diff_attention(x, w_in, w_out, lam_params, subln_g, lambda_init, cos, sin):
    B, S, _ = x.shape
    nqb = S // Q_BLOCK
    q, k, v = jnp.split(x @ w_in, [A_QK_WIDTH, 2 * A_QK_WIDTH], axis=-1)
    q = partial_rotary(q.reshape(B, S, A_HEADS * 2, A_HEAD_DIM), cos, sin)
    k = partial_rotary(k.reshape(B, S, A_HEADS * 2, A_HEAD_DIM), cos, sin)
    q = q.reshape(B, nqb, Q_BLOCK, A_HEADS, 2, A_HEAD_DIM).transpose(1, 4, 0, 3, 2, 5)
    k = k.reshape(B, S, A_HEADS, 2, A_HEAD_DIM).transpose(3, 0, 2, 1, 4)
    v = v.reshape(B, S, A_HEADS, 2 * A_HEAD_DIM).transpose(0, 2, 1, 3)
    lp = lam_params.astype(jnp.float32)
    lam = jnp.exp(jnp.sum(lp[0] * lp[1])) - jnp.exp(jnp.sum(lp[2] * lp[3])) + lambda_init
    scale = A_HEAD_DIM ** -0.5
    key_chunk = jnp.arange(S) // CHUNK

    def attend(args):
        qb, bi = args
        q_chunk = (bi * Q_BLOCK + jnp.arange(Q_BLOCK)) // CHUNK
        mask = key_chunk[None, :] <= q_chunk[:, None]
        s = jnp.einsum("mbhqd,mbhkd->mbhqk", qb, k).astype(jnp.float32) * scale
        p = jax.nn.softmax(jnp.where(mask, s, -jnp.inf), axis=-1)
        a = (p[0] - lam * p[1]).astype(v.dtype)
        return jnp.einsum("bhqk,bhkd->bhqd", a, v)

    o = lax.map(attend, (q, jnp.arange(nqb)))
    o = o.transpose(1, 0, 3, 2, 4).reshape(B, S, A_HEADS, 2 * A_HEAD_DIM)
    o = rms_norm(o, subln_g) * (1.0 - lambda_init)
    return o.astype(x.dtype).reshape(B, S, A_V_WIDTH) @ w_out

def hgrn2(x, w_in, w_out, lower_bound, norm_g):
    B, S, _ = x.shape
    nc = S // CHUNK
    q, f, i, g = jnp.split(x @ w_in, 4, axis=-1)
    forget = lower_bound + (1.0 - lower_bound) * jax.nn.sigmoid(f.astype(jnp.float32))
    log_f = jnp.log(forget)
    k_in = 1.0 - forget
    q = jax.nn.silu(q)

    def to_chunks(t):
        d = t.shape[-1] // H_HEADS
        return t.astype(jnp.float32).reshape(B, nc, CHUNK, H_HEADS, d).transpose(1, 0, 3, 2, 4)

    causal = jnp.tril(jnp.ones((CHUNK, CHUNK), dtype=bool))[:, :, None]

    def step(state, xs):
        qc, kc, vc, gc = xs
        b = jnp.cumsum(gc, axis=2)
        diff = b[:, :, :, None, :] - b[:, :, None, :, :]
        decay = jnp.exp(jnp.where(causal, diff, -jnp.inf))
        scores = jnp.einsum("bhtd,bhtsd,bhsd->bhts", qc, decay, kc)
        b_last = b[:, :, -1:, :]
        o = jnp.einsum("bhts,bhse->bhte", scores, vc) + jnp.einsum("bhtd,bhde->bhte", qc * jnp.exp(b), state)
        state = jnp.exp(b_last[:, :, 0, :, None]) * state + jnp.einsum("bhsd,bhse->bhde", kc * jnp.exp(b_last - b), vc)
        return state, o

    state0 = jnp.zeros((B, H_HEADS, H_EXPAND, H_VDIM), jnp.float32)
    _, o = lax.scan(step, state0, (to_chunks(q), to_chunks(k_in), to_chunks(i), to_chunks(log_f)))
    o = o.transpose(1, 0, 3, 2, 4).reshape(B, S, H_HEADS, H_VDIM)
    o = rms_norm(o, norm_g).reshape(B, S, H_WIDTH) * jax.nn.silu(g.astype(jnp.float32))
    return o.astype(x.dtype) @ w_out

def swiglu(x, w_gate_up, w_down):
    gate, up = jnp.split(x @ w_gate_up, 2, axis=-1)
    return (jax.nn.silu(gate) * up) @ w_down

def route(xf, w_router, bias):
    T = xf.shape[0]
    scores = jax.nn.sigmoid(xf.astype(jnp.float32) @ w_router.astype(jnp.float32))
    choice = (scores + bias.astype(jnp.float32)).reshape(T, N_GROUPS, N_EXPERTS // N_GROUPS)
    group_score = jnp.sum(lax.top_k(choice, 2)[0], axis=-1)
    _, top_groups = lax.top_k(group_score, TOPK_GROUP)
    group_mask = jnp.any(jax.nn.one_hot(top_groups, N_GROUPS, dtype=jnp.bool_), axis=1)
    choice = jnp.where(group_mask[:, :, None], choice, -jnp.inf).reshape(T, N_EXPERTS)
    _, idx = lax.top_k(choice, TOP_K)
    w = jnp.take_along_axis(scores, idx, axis=-1)
    w = w / (jnp.sum(w, axis=-1, keepdims=True) + 1e-20) * ROUTED_SCALE
    return idx, w

def routed_experts(xf, idx, w, w_gate_up, w_down):
    T, D = xf.shape
    n_assign = T * TOP_K
    n_blocks = -(-n_assign // MOE_BLOCK) + N_EXPERTS
    flat_e = idx.reshape(-1)
    order = jnp.argsort(flat_e)
    sorted_e = flat_e[order]
    counts = jnp.zeros((N_EXPERTS,), jnp.int32).at[flat_e].add(1)
    padded = (counts + MOE_BLOCK - 1) // MOE_BLOCK * MOE_BLOCK
    pad_end = jnp.cumsum(padded)
    pad_start = pad_end - padded
    start = jnp.cumsum(counts) - counts
    dest = pad_start[sorted_e] + jnp.arange(n_assign, dtype=jnp.int32) - start[sorted_e]
    rows = jnp.full((n_blocks * MOE_BLOCK,), T, jnp.int32).at[dest].set((order // TOP_K).astype(jnp.int32))
    gates = jnp.zeros((n_blocks * MOE_BLOCK,), xf.dtype).at[dest].set(w.reshape(-1)[order].astype(xf.dtype))
    block_expert = jnp.minimum(jnp.searchsorted(pad_end // MOE_BLOCK, jnp.arange(n_blocks), side="right"), N_EXPERTS - 1)
    x_pad = jnp.concatenate([xf, jnp.zeros((1, D), xf.dtype)], axis=0)

    def block(acc, xs):
        r, gt, e = xs
        y = swiglu(x_pad[r], w_gate_up[e], w_down[e])
        return acc.at[r].add(gt[:, None] * y), None

    acc, _ = lax.scan(block, jnp.zeros((T + 1, D), xf.dtype),
                      (rows.reshape(n_blocks, MOE_BLOCK), gates.reshape(n_blocks, MOE_BLOCK), block_expert))
    return acc[:T]

def moe(x, w_router, bias, w_gate_up, w_down, ws_gate_up, ws_down):
    B, S, D = x.shape
    xf = x.reshape(B * S, D)
    idx, w = route(xf, w_router, bias)
    y = routed_experts(xf, idx, w, w_gate_up, w_down) + swiglu(xf, ws_gate_up, ws_down)
    return y.reshape(B, S, D)

def setup_inputs(seed: int = 0) -> dict:
    key = jax.random.key(seed)
    ks = jax.random.split(key, 24)

    def nrm(k, shape, scale):
        return jax.random.normal(k, shape, jnp.float32) * scale

    x = nrm(ks[0], (BATCH, SEQ, D_MODEL), 1.0)
    attn_w_in = jnp.concatenate([
        nrm(ks[1], (N_ATTN_LAYERS, D_MODEL, 2 * A_QK_WIDTH), D_MODEL ** -0.5),
        nrm(ks[2], (N_ATTN_LAYERS, D_MODEL, A_V_WIDTH), BETA * D_MODEL ** -0.5)], axis=-1)
    attn_w_out = nrm(ks[3], (N_ATTN_LAYERS, A_V_WIDTH, D_MODEL), BETA * A_V_WIDTH ** -0.5)
    attn_lambda = nrm(ks[4], (N_ATTN_LAYERS, 4, A_HEAD_DIM), 0.1)
    attn_subln = 1.0 + nrm(ks[5], (N_ATTN_LAYERS, 2 * A_HEAD_DIM), 0.02)
    hgrn_w_in = jnp.concatenate([
        nrm(ks[6], (N_HGRN_LAYERS, D_MODEL, 2 * H_WIDTH), D_MODEL ** -0.5),
        nrm(ks[7], (N_HGRN_LAYERS, D_MODEL, H_WIDTH), BETA * D_MODEL ** -0.5),
        nrm(ks[8], (N_HGRN_LAYERS, D_MODEL, H_WIDTH), D_MODEL ** -0.5)], axis=-1)
    hgrn_w_out = nrm(ks[9], (N_HGRN_LAYERS, H_WIDTH, D_MODEL), BETA * H_WIDTH ** -0.5)
    hgrn_lower_bounds = nrm(ks[10], (DEPTH, H_WIDTH), 0.1)
    hgrn_norm = 1.0 + nrm(ks[11], (N_HGRN_LAYERS, H_VDIM), 0.02)
    moe_router = nrm(ks[12], (DEPTH, D_MODEL, N_EXPERTS), D_MODEL ** -0.5)
    moe_router_bias = nrm(ks[13], (DEPTH, N_EXPERTS), 0.01)
    moe_w_gate_up = nrm(ks[14], (DEPTH, N_EXPERTS, D_MODEL, 2 * EXPERT_FF), D_MODEL ** -0.5)
    moe_w_down = nrm(ks[15], (DEPTH, N_EXPERTS, EXPERT_FF, D_MODEL), BETA * EXPERT_FF ** -0.5)
    shared_w_gate_up = nrm(ks[16], (DEPTH, D_MODEL, 2 * EXPERT_FF), D_MODEL ** -0.5)
    shared_w_down = nrm(ks[17], (DEPTH, EXPERT_FF, D_MODEL), BETA * EXPERT_FF ** -0.5)
    ln_gain = 1.0 + nrm(ks[18], (DEPTH, 2, D_MODEL), 0.02)
    ln_bias = nrm(ks[19], (DEPTH, 2, D_MODEL), 0.02)
    return {"x": x, "attn_w_in": attn_w_in, "attn_w_out": attn_w_out, "attn_lambda": attn_lambda,
            "attn_subln": attn_subln, "hgrn_w_in": hgrn_w_in, "hgrn_w_out": hgrn_w_out,
            "hgrn_lower_bounds": hgrn_lower_bounds, "hgrn_norm": hgrn_norm, "moe_router": moe_router,
            "moe_router_bias": moe_router_bias, "moe_w_gate_up": moe_w_gate_up, "moe_w_down": moe_w_down,
            "shared_w_gate_up": shared_w_gate_up, "shared_w_down": shared_w_down,
            "ln_gain": ln_gain, "ln_bias": ln_bias}

def reference(x, attn_w_in, attn_w_out, attn_lambda, attn_subln, hgrn_w_in, hgrn_w_out,
              hgrn_lower_bounds, hgrn_norm, moe_router, moe_router_bias, moe_w_gate_up, moe_w_down,
              shared_w_gate_up, shared_w_down, ln_gain, ln_bias):
    cos, sin = rotary_tables(x.shape[1])
    lb = jax.nn.softmax(hgrn_lower_bounds.astype(jnp.float32), axis=0)
    lb = jnp.cumsum(lb, axis=0) - lb[0]
    for layer in range(DEPTH):
        j = layer // N_MIXERS
        if layer % N_MIXERS == 0:
            lambda_init = 0.8 - 0.6 * math.exp(-0.3 * layer)
            h = diff_attention(x, attn_w_in[j], attn_w_out[j], attn_lambda[j], attn_subln[j], lambda_init, cos, sin)
        else:
            h = hgrn2(x, hgrn_w_in[j], hgrn_w_out[j], lb[layer], hgrn_norm[j])
        x = layer_norm(ALPHA * x + h, ln_gain[layer, 0], ln_bias[layer, 0])
        h = moe(x, moe_router[layer], moe_router_bias[layer], moe_w_gate_up[layer], moe_w_down[layer],
                shared_w_gate_up[layer], shared_w_down[layer])
        x = layer_norm(ALPHA * x + h, ln_gain[layer, 1], ln_bias[layer, 1])
    return x


_drawn_inputs = setup_inputs


def setup_inputs(seed=0):
    import zlib

    import numpy as np

    out = dict(_drawn_inputs(seed))
    spreads = {}
    factors = {'hgrn_lower_bounds': 5.786, 'hgrn_norm': 3.801}
    for name, (base, spread) in spreads.items():
        noise = np.random.default_rng([zlib.crc32(name.encode()), seed]).standard_normal(out[name].shape)
        drawn = base * np.exp(spread * noise) if base else spread * noise
        out[name] = jnp.asarray(drawn.astype(out[name].dtype))
    for name, factor in factors.items():
        out[name] = (out[name] * factor).astype(out[name].dtype)
    return out
```

```python
import math
from contextlib import ExitStack

import numpy as np

import concourse.bass as bass
from concourse import mybir

ALU = mybir.AluOpType
ACT = mybir.ActivationFunctionType
AX = mybir.AxisListType.X
F32 = mybir.dt.float32
F32R = mybir.dt.float32r
I32 = mybir.dt.int32

P = 128
SEQ, D = 256, 1024
TT = SEQ // P
J = D // P
DEPTH = 2
CHUNK = 64
BANK = 512
HALVES = D // BANK
HEADS = 8
SUB = 64
ROT = SUB // 4
RH = ROT // 2
ROPE_THETA = 500000.0
NE, NG, TOPG, TOPK = 64, 8, 4, 8
GE = NE // NG
FF = D // 4
FT = FF // P
SLOTS = 64
PAIRS = NE // 2
BLOCKS = SEQ // SLOTS
EXTRA = NE * (BLOCKS - 1)
OVF = SEQ * TOPK // SLOTS
ROUTED_SCALE = 2.5
ALPHA = (2 * DEPTH) ** 0.25
EPS = 1e-5
BIG = 3.0e38
FORGET_MIN = 1e-19
LEVELS = [128, 64, 32, 16, 8, 4, 2, 1]
NO_SLOT = 999.0
LAMBDA_INIT = 0.8 - 0.6 * math.exp(-0.3 * 0)

CONST_WIDTHS = dict(ident=P, before=P, ones=P, cos=TT * RH, sin=TT * RH, amask=P + SEQ,
                    iota=BLOCKS * SLOTS, lower=NG * NG, row=1, ovf_e=EXTRA, ovf_b=EXTRA, eps=1)
CONST_AT, _at = {}, 0
for _name, _width in CONST_WIDTHS.items():
    CONST_AT[_name] = (_at, _at + _width)
    _at += _width
CONSTS = _at
COMPACT = [m for m in LEVELS if m < 32] + [0]


def constants():
    c = np.zeros((P, CONSTS), np.float32)

    def put(name, value):
        a, b = CONST_AT[name]
        c[:, a:b] = value

    t = np.arange(P)
    put("ident", np.eye(P))
    put("before", t[:, None] < t[None, :])
    put("ones", 1.0)
    freq = np.float32(ROPE_THETA) ** (-np.arange(0, ROT, 2, dtype=np.float32) / np.float32(ROT))
    angle = np.arange(SEQ, dtype=np.float32)[:, None] * freq[None, :].astype(np.float32)
    for name, f in (("cos", np.cos), ("sin", np.sin)):
        put(name, f(angle).astype(np.float32).reshape(TT, P, RH).transpose(1, 0, 2).reshape(P, -1))
    am = np.zeros((P, P + SEQ), np.float32)
    q_chunk = t[:, None] // CHUNK
    am[:, :P] = np.where(t[None, :] // CHUNK <= q_chunk, 0, -1e30)
    am[:, P:] = np.where(np.arange(SEQ)[None, :] // CHUNK <= q_chunk + P // CHUNK, 0, -1e30)
    put("amask", am)
    put("iota", (np.arange(BLOCKS * SLOTS) - NO_SLOT)[None, :])
    g = np.arange(NG)
    put("lower", (g[None, :] < g[:, None]).reshape(1, -1))
    put("row", t[:, None])
    k = np.arange(EXTRA)
    put("ovf_e", (k % NE)[None, :])
    put("ovf_b", (k // NE + 1)[None, :])
    put("eps", EPS)
    masks = np.zeros((P, len(COMPACT), 32), np.int32)
    s, q = (t % 32)[:, None], np.arange(32)[None, :]
    for i, m in enumerate(COMPACT):
        masks[:, i] = (s == q) if m == 0 else (s // (2 * m) == q // (2 * m)) & (s % (2 * m) < m) & (q % (2 * m) >= m)
    return c, masks.reshape(P, -1)


ITEMS = []
for _layer, _chunks in ((0, 6), (1, 8)):
    ITEMS += [("in", _layer, c) for c in range(_chunks)]
    ITEMS += [("out", _layer, c) for c in range(HALVES)]
    ITEMS += [("ln", _layer, 0), ("sgu", _layer, 0), ("sdn", _layer, 0), ("ln", _layer, 1)]
ITEM = {item: k for k, item in enumerate(ITEMS)}
HGRN_COLUMNS = [1024, 1536, 0, 512, 2048, 2560, 3072, 3584]


def level_bank(i):
    return [4, 6, 4, 5, 6, 7, 4, 5, 6][i]


def build_trunk(nc, x_in, attn_w_in, attn_w_out, attn_lambda, attn_subln, hgrn_w_in, hgrn_w_out,
                hgrn_lower_bounds, hgrn_norm, moe_router, moe_router_bias, moe_w_gate_up, moe_w_down,
                shared_w_gate_up, shared_w_down, ln_gain, ln_bias, consts, level_masks, out):
    ctx = ExitStack()

    def sb(name, shape, dt=F32):
        return ctx.enter_context(nc.sbuf_tensor(name, shape, dt))

    def sem(name):
        return ctx.enter_context(nc.semaphore(name))

    with ctx:
        cst = sb("cst", [P, CONSTS])
        masks = sb("masks", [P, len(COMPACT) * 32], I32)
        x = sb("x", [P, TT, D])
        xT = sb("xT", [P, J, SEQ])
        w_gu = sb("w_gu", [P, 2, J * 2 * FF])
        w_dn = sb("w_dn", [P, 2, FT * D])
        odd = sb("odd", [P, 2 * (J * 2 * FF + FT * D)])
        stream = sb("stream", [P, 2, J * BANK])
        x_hi = sb("x_hi", [P, TT, J, P], F32R)
        x_lo = sb("x_lo", [P, TT, J, P], F32R)
        pick = sb("pick", [P, 2, TT, P], F32R)
        place = sb("place", [P, 2, SEQ], F32R)
        y_hi = sb("y_hi", [P, HALVES, BANK], F32R)
        y_lo = sb("y_lo", [P, HALVES, BANK], F32R)
        work = sb("work", [P, 5632])
        w_router = sb("w_router", [P, J, NE])
        bias_row = sb("bias_row", [P, NE])
        small = sb("small", [P, 256])
        ovf_list = sb("ovf_list", [1, 1 + 2 * OVF], I32)
        ps = ctx.enter_context(nc.psum_tensor("ps", [P, 8, BANK], F32))

        def const(name, width=None):
            a, b = CONST_AT[name]
            return cst[:, a:b]

        ident = const("ident")
        GU, DN = J * 2 * FF, FT * D

        def gate_up_of(slot):
            w = w_gu[:, slot, :] if slot < 2 else odd[:, (slot - 2) * GU:(slot - 1) * GU]
            return w

        def down_of(slot):
            return w_dn[:, slot, :] if slot < 2 else odd[:, 2 * GU + (slot - 2) * DN:2 * GU + (slot - 1) * DN]

        def part(tensor, at, *shape):
            v = tensor[:, at:at + int(np.prod(shape))]
            names = "abcd"[:len(shape)]
            return v.rearrange(f"p ({' '.join(names)}) -> p {' '.join(names)}", **dict(zip(names, shape))) if len(shape) > 1 else v

        qkv = part(odd, 0, 3, TT, D)
        q_tok, k_tok, v_tok = qkv[:, 0], qkv[:, 1], qkv[:, 2]
        a_qT, a_kT = part(odd, 6144, HEADS, SEQ), part(odd, 8192, HEADS, SEQ)
        a_o = q_tok
        masked = part(work, 0, 2, 2, P + SEQ)
        probs = part(work, 1536, 2, 2, P + SEQ)
        diff = part(work, 3072, 2, P + SEQ)
        diffT = part(work, 3840, 2, P + SEQ)
        oT = part(odd, 6144, HEADS, SEQ)
        h_b, h_qT, h_kT = (part(odd, 2048 * i, HEADS, SEQ) for i in (0, 3, 1))
        h_A = [part(odd, 2048 * i, HEADS, SEQ) for i in (2, 4)]
        scoreT = part(odd, 10240, HEADS * TT, P)
        h_o = h_A[0].rearrange("p h t -> p (h t)").rearrange("p (a n) -> p a n", a=TT)
        h_v, h_gate = part(work, 0, TT, D), part(work, 2048, TT, D)
        cross, compact = part(work, 4096, HEADS, P), part(work, 5120, HEADS * TT, 32)
        xg = part(work, 0, 2, J, P)
        silu, hid, hidT = part(work, 2048, 2, FF), part(work, 2560, 2, FF), part(work, 3072, 2, FT, P)
        R0 = 3584
        score, choice, kept, replaced = (part(work, R0 + 128 * i, TT, NE) for i in range(4))
        chosen, gate, slot = (part(work, R0 + 128 * i, TT, NE) for i in range(4, 7))
        best8 = part(work, R0 + 896, TT * NG, 8)
        rank4 = part(work, R0 + 1024, TT * NG, NG)
        tie4 = part(work, R0 + 1152, TT * NG, NG)
        flags, flags_sum = part(work, R0 + 1280, EXTRA), part(work, R0 + 1472, EXTRA)
        listed, listed_id = part(work, R0 + 1664, EXTRA), part(work, R0 + 1856, EXTRA)
        (g_sum, g_rank, g_pen) = (small[:, 16 * i:16 * i + 16] for i in range(3))
        top8 = part(small, 48, TT, 8)
        w_sum = small[:, 64:66]
        gate_slot = part(small, 66, 2)
        ovf_cols = small[:, 68:70]
        stats = part(small, 70, 2, 6)
        mean_var = part(small, 82, 2)
        rstd, nmr, eps_var = small[:, 84:85], small[:, 85:86], small[:, 86:87]
        row_max = part(small, 88, 2, 4)
        row_sum = part(small, 96, 2, 4)
        row_scale = part(small, 104, 4)
        neg_lam = small[:, 108:109]
        o_sq = small[:, 110:126]
        o_rs = small[:, 126:142]
        head_gain = small[:, 142:143]
        lam2 = small[:, 144:146]
        lb_e = part(small, 146, 2, HEADS)
        lb_rest = small[:, 162:170]
        lb_low = small[:, 170:178]
        c01 = part(small, 178, HEADS, 1)
        lb_sum = small[:, 186:194]
        lb_max = small[:, 194:202]
        norm_h = small[:, 202:203]

        lam_row = part(work, 4608, 4, SUB)
        lam_prod = part(work, 4864, 2, SUB)
        lb_raw = work[:, 5120:5120 + P]

        const_in, x_loaded, vec_in = sem("const_in"), sem("x_loaded"), sem("vec_in")
        router_in, bias_in = sem("router_in"), sem("bias_in")
        stream_in = [sem("stream_in0"), sem("stream_in1")]
        gu_in = [sem(f"gu_in{s}") for s in range(4)]
        dn_in = [sem(f"dn_in{s}") for s in range(4)]
        out_stored = sem("out_stored")
        x_ready, x_split = sem("x_ready"), sem("x_split")
        xT_ps, xT_act, xT_dve = sem("xT_ps"), sem("xT_act"), sem("xT_dve")
        proj_ps, proj_ev = sem("proj_ps"), sem("proj_ev")
        rope_ok, turn_ps, turn_act, turn_dve = sem("rope_ok"), sem("turn_ps"), sem("turn_act"), sem("turn_dve")
        sc_ps, nmax_ok, probs_ok, diff_ok = sem("sc_ps"), sem("nmax_ok"), sem("probs_ok"), sem("diff_ok")
        dT_ps, dT_ev, pv_ps, o_ev = sem("dT_ps"), sem("dT_ev"), sem("pv_ps"), sem("o_ev")
        lam_a, lam_b, lam_ok = sem("lam_a"), sem("lam_b"), sem("lam_ok")
        ms_ok, root_ok, on_ok = sem("ms_ok"), sem("root_ok"), sem("on_ok")
        oT_ps, oT_ev, outp_ps = sem("oT_ps"), sem("oT_ev"), sem("outp_ps")
        ln_var, ln_std, ln_nmr, ln_lin = sem("ln_var"), sem("ln_std"), sem("ln_nmr"), sem("ln_lin")
        xhi_ok = sem("xhi_ok")
        lb_ps, lb_exp_in, lb_exp_ok = sem("lb_ps"), sem("lb_exp_in"), sem("lb_exp_ok")
        forget_ok, logf_ok = sem("forget_ok"), sem("logf_ok")
        expo_ok, exp_ok, lev_ok, lev_ps = sem("expo_ok"), sem("exp_ok"), sem("lev_ok"), sem("lev_ps")
        lev_act, lev_dve, scores_ok, ho_ps = sem("lev_act"), sem("lev_dve"), sem("scores_ok"), sem("ho_ps")
        logit_ps, score_ok, chosen_ok, pos_ps, route_ok = sem("logit_ps"), sem("score_ok"), sem("chosen_ok"), sem("pos_ps"), sem("route_ok")
        ovf_cols_ok, ovf_row_ps, ovf_ok = sem("ovf_cols_ok"), sem("ovf_row_ps"), sem("ovf_ok")
        sh_ps, sh_silu, sh_hid, shT_ps, shT_ev = sem("sh_ps"), sem("sh_silu"), sem("sh_hid"), sem("shT_ps"), sem("shT_ev")
        pick_ok, xg_ps, xg_ev, gu_ps = sem("pick_ok"), sem("xg_ps"), sem("xg_ev"), sem("gu_ps")
        silu_ok, hid_ok, hidT_ps, hidT_ev = sem("silu_ok"), sem("hid_ok"), sem("hidT_ps"), sem("hidT_ev")
        dn_ps, yhi_ok, ylo_ok, moe_ps = sem("dn_ps"), sem("yhi_ok"), sem("ylo_ok"), sem("moe_ps")
        sdn_ps = sem("sdn_ps")
        scores_clear, sq_ok = sem("scores_clear"), sem("sq_ok")
        dve_chain, act_chain = sem("dve_chain"), sem("act_chain")
        OV = [{n: sem(f"o{layer}_{n}") for n in ("gu_in", "dn_in", "pick", "xps", "xev", "gups", "silu", "hid", "tps", "tev", "dps", "yhi", "ylo", "done")}
              for layer in range(DEPTH)]

        block = ctx.enter_context(nc.Block())

        def rows(w):
            return w.rearrange("(p j) n -> p j n", j=J)

        def expert_gu(layer, e):
            w = moe_w_gate_up[layer]
            w = w[e] if isinstance(e, int) else w[bass.ds(e, 1)].rearrange("a d n -> (a d) n")
            return w.rearrange("(p j) n -> p (j n)", j=J)

        def expert_dn(layer, e):
            w = moe_w_down[layer]
            w = w[e] if isinstance(e, int) else w[bass.ds(e, 1)].rearrange("a d n -> (a d) n")
            return w.rearrange("(p j) n -> p (j n)", j=FT)

        def last_use(k):
            name, layer, c = ITEMS[k]
            return {"in": (proj_ps, 12 * layer + 2 * c + 2), "out": (outp_ps, 4 * layer + 2 * c + 2),
                    "ln": (x_ready, 4 * layer + 2 * c + 2), "sgu": (sh_ps, TT * (layer + 1)), "sdn": (sdn_ps, layer + 1)}[name]

        @block.sync
        def _(sp):
            def load_item(k):
                name, layer, c = ITEMS[k]
                if k >= 2:
                    sp.wait_ge(*last_use(k - 2))
                buf = stream[:, k % 2, :]
                if name == "in":
                    w, col = (attn_w_in, c * BANK) if layer == 0 else (hgrn_w_in, HGRN_COLUMNS[c])
                    dst, src = buf.rearrange("p (j n) -> p j n", j=J), rows(w[0])[:, :, col:col + BANK]
                elif name == "out":
                    w = attn_w_out if layer == 0 else hgrn_w_out
                    dst = buf.rearrange("p (h n) -> p h n", h=HEADS)
                    src = w[0].rearrange("(h p) n -> p h n", p=P)[:, :, c * BANK:(c + 1) * BANK]
                elif name == "ln":
                    for i, v in enumerate((ln_gain, ln_bias)):
                        sp.dma_start(buf[:, i * D:(i + 1) * D], v[layer, c:c + 1, :].broadcast_to([P, D])).then_inc(stream_in[k % 2], 16)
                    return
                elif name == "sgu":
                    dst, src = buf, shared_w_gate_up[layer].rearrange("(p j) n -> p (j n)", j=J)
                else:
                    dst, src = buf[:, 0:DN], shared_w_down[layer].rearrange("(p j) n -> p (j n)", j=FT)
                sp.dma_start(dst, src).then_inc(stream_in[k % 2], 16)

            def load_pair(layer, p, e, u):
                g = layer * PAIRS + p
                if not isinstance(g, int) or g >= 2:
                    sp.wait_ge(gu_ps, g - 1)
                for i in range(2):
                    sp.dma_start(gate_up_of(2 * u + i), expert_gu(layer, e + i)).then_inc(gu_in[2 * u + i], 16)
                if not isinstance(g, int) or g >= 2:
                    sp.wait_ge(dn_ps, 2 * g - 2)
                for i in range(2):
                    sp.dma_start(down_of(2 * u + i), expert_dn(layer, e + i)).then_inc(dn_in[2 * u + i], 16)

            sp.dma_start(cst[:], consts).then_inc(const_in, 16)
            sp.dma_start(masks[:], level_masks).then_inc(const_in, 16)
            for tt in range(TT):
                sp.dma_start(x[:, tt, :], x_in[0, tt * P:(tt + 1) * P, :]).then_inc(x_loaded, 16)
            sp.dma_start(lam_row, attn_lambda.rearrange("a l s -> a (l s)").broadcast_to([P, 4 * SUB]).rearrange("p (l s) -> p l s", l=4)).then_inc(vec_in, 16)
            sp.dma_start(head_gain, attn_subln.rearrange("a n -> n a")).then_inc(vec_in, 16)
            sp.dma_start(norm_h, hgrn_norm.rearrange("a n -> n a")).then_inc(vec_in, 16)
            sp.dma_start(lb_raw[0:DEPTH * HEADS, :], hgrn_lower_bounds.rearrange("a (h p) -> (a h) p", p=P)).then_inc(vec_in, 16)
            load_item(0)
            load_item(1)
            k = 2
            for layer in range(DEPTH):
                if layer == 1:
                    sp.wait_ge(moe_ps, layer)
                    sp.wait_ge(route_ok, layer)
                sp.dma_start(w_router[:], rows(moe_router[layer])).then_inc(router_in, 16)
                sp.dma_start(bias_row[:], moe_router_bias[layer:layer + 1, :].broadcast_to([P, NE])).then_inc(bias_in, 16)
                prefetch_at = k + 3
                while ITEMS[k] != ("ln", layer, 1):
                    if k == prefetch_at:
                        load_pair(layer, 0, 0, 0)
                    if ITEMS[k] == ("sgu", layer, 0):
                        load_item(k)
                        k += 1
                        load_item(k)
                        k += 1
                        sp.wait_ge(x_ready, 4 * layer + 2)
                        load_pair(layer, 1, 2, 1)
                        continue
                    load_item(k)
                    k += 1
                load_item(k)
                k += 1
                with sp.Fori(1, PAIRS // 2) as it:
                    for u in range(2):
                        load_pair(layer, it * 2 + u, it * 4 + 2 * u, u)
                s = OV[layer]
                sp.wait_ge(ovf_ok, layer + 1)
                n = sp.value_load(ovf_list[0:1, 0:1], min_val=0, max_val=OVF - 1)
                with sp.If(n > 0):
                    sp.wait_ge(dn_ps, 2 * PAIRS * (layer + 1))
                    with sp.Fori(0, n) as i:
                        e = sp.value_load(ovf_list[0:1, bass.ds(i + 1, 1)], min_val=0, max_val=NE - 1)
                        sp.wait_ge(s["done"], i + 1)
                        sp.dma_start(gate_up_of(0), expert_gu(layer, e)).then_inc(s["gu_in"], 16)
                        sp.dma_start(down_of(0), expert_dn(layer, e)).then_inc(s["dn_in"], 16)
                with sp.Else():
                    sp.nop()
                if layer == 0:
                    load_item(k)
                    k += 1
            for tt in range(TT):
                sp.wait_ge(x_ready, 4 * (DEPTH - 1) + 3 + tt)
                sp.dma_start(out[0, tt * P:(tt + 1) * P, :], x[:, tt, :]).then_inc(out_stored, 16)
            sp.wait_ge(out_stored, 16 * TT)

        @block.tensor
        def _(pe):
            def item(name, layer, c):
                k = ITEM[name, layer, c]
                n = sum(2 if ITEMS[i][0] == "ln" else 1 for i in range(k % 2, k + 1, 2))
                pe.wait_ge(stream_in[k % 2], 16 * n)
                return stream[:, k % 2, :]

            def turn_x(b):
                for tt in range(TT):
                    if b == 0:
                        pe.wait_ge(x_loaded, 16 * TT)
                    else:
                        pe.wait_ge(x_ready, 2 * (b - 1) + tt + 1)
                    for j in range(J):
                        t = pe.transpose(ps[:, 2 * tt + j // 4, (j % 4) * P:(j % 4 + 1) * P],
                                         x[:, tt, j:D:J], ident)
                    t.then_inc(xT_ps, 1)

            def xT_wait(b):
                pe.wait_ge(xT_act, 2 * b + 2)
                pe.wait_ge(xT_dve, 2 * b + 2)

            def rows_unit(w, tt, n):
                if n >= 4:
                    pe.wait_ge(proj_ev, n - 3)
                for j in range(J):
                    t = pe.matmul(ps[:, n % 4, :], xT[:, j, tt * P:(tt + 1) * P], w[:, j, :],
                                  start=(j == 0), stop=(j == J - 1))
                t.then_inc(proj_ps, 1)
                return t

            def columns_unit(w, half, n):
                pe.wait_ge(proj_ev, n - 3)
                for i in range(2):
                    for j in range(J):
                        c = (2 * half + i) * P
                        t = pe.matmul(ps[:, n % 4, i * SEQ:(i + 1) * SEQ], w[:, j, c:c + P], xT[:, j, :],
                                      start=(j == 0), stop=(j == J - 1))
                t.then_inc(proj_ps, 1)
                return t

            def out_projection(layer, o):
                for r in range(4):
                    tt, hh = r // 2, r % 2
                    pe.wait_ge(on_ok, TT * layer + tt + 1)
                    for i in range(4):
                        h = 4 * hh + i
                        t = pe.transpose(ps[:, 4 + r, i * P:(i + 1) * P], o[:, tt, h * P:(h + 1) * P], ident)
                    t.then_inc(oT_ps, 1)
                for c in range(HALVES):
                    w = item("out", layer, c).rearrange("p (h n) -> p h n", h=HEADS)
                    for tt in range(TT):
                        pe.wait_ge(oT_ev, 4 * layer + 2 * tt + 2)
                        for h in range(HEADS):
                            t = pe.matmul(ps[:, tt * HALVES + c, :], oT[:, h, tt * P:(tt + 1) * P], w[:, h, :],
                                          start=(h == 0), stop=(h == HEADS - 1))
                        t.then_inc(outp_ps, 1)


            pe.wait_ge(const_in, 32)
            turn_x(0)
            pe.wait_ge(vec_in, 64)
            pe.transpose(ps[:, 6, 0:DEPTH * HEADS], lb_raw[0:DEPTH * HEADS, :], ident[0:DEPTH * HEADS, 0:DEPTH * HEADS])\
              .then_inc(lb_ps, 1)
            xT_wait(0)
            for c in range(6):
                w = item("in", 0, c).rearrange("p (j n) -> p j n", j=J)
                for tt in range(TT):
                    t = rows_unit(w, tt, 2 * c + tt)
            for r in range(8):
                src = q_tok if r < 4 else k_tok
                pe.wait_ge(rope_ok, 1 if r < 4 else 2)
                if r >= 2:
                    pe.wait_ge(turn_act if r % 2 == 0 else turn_dve, r // 2)
                for i in range(2):
                    for tt in range(TT):
                        h = 2 * (r % 4) + i
                        t = pe.transpose(ps[:, 4 + r % 2, (i * TT + tt) * P:(i * TT + tt + 1) * P],
                                         src[:, tt, h * P:(h + 1) * P], ident)
                t.then_inc(turn_ps, 1)

            def scores(h):
                if h == 0:
                    pe.wait_ge(turn_act, 4)
                    pe.wait_ge(turn_dve, 4)
                    pe.wait_ge(proj_ev, 12)
                if h >= 2:
                    pe.wait_ge(nmax_ok, h - 1)
                for m in range(2):
                    rows_m = slice(m * SUB, (m + 1) * SUB)
                    b = 2 * (h % 2) + m
                    pe.matmul(ps[:, b, 0:P], a_qT[rows_m, h, 0:P], a_kT[rows_m, h, 0:P], start=True, stop=True)
                    t = pe.matmul(ps[:, b, P:P + SEQ], a_qT[rows_m, h, P:SEQ], a_kT[rows_m, h, :],
                                  start=True, stop=True)
                t.then_inc(sc_ps, 1)

            scores(0)
            scores(1)
            for h in range(HEADS):
                pe.wait_ge(diff_ok, h + 1)
                for i in range(3):
                    t = pe.transpose(ps[:, 4 + h % 2, i * P:(i + 1) * P], diff[:, h % 2, i * P:(i + 1) * P], ident)
                t.then_inc(dT_ps, 1)
                if h + 2 < HEADS:
                    scores(h + 2)
                pe.wait_ge(dT_ev, h + 1)
                if h >= 2:
                    pe.wait_ge(o_ev, h - 1)
                v = v_tok[:, :, h * P:(h + 1) * P]
                dT = diffT[:, h % 2, :]
                pe.matmul(ps[:, 6 + h % 2, 0:P], dT[:, 0:P], v[:, 0, :], start=True, stop=True)
                pe.matmul(ps[:, 6 + h % 2, P:2 * P], dT[:, P:2 * P], v[:, 0, :], start=True, stop=False)
                pe.matmul(ps[:, 6 + h % 2, P:2 * P], dT[:, 2 * P:3 * P], v[:, 1, :], start=False, stop=True)\
                  .then_inc(pv_ps, 1)
            out_projection(0, a_o)

            def gather(g, u, r, first=False):
                if r == 0:
                    pe.wait_ge(pick_ok, g + 1)
                if not first:
                    pe.wait_ge(xg_ev, 3 * g + r)
                for i in range(4):
                    j = 4 * r + i
                    for n, (tt, half) in enumerate([(tt, half) for tt in range(TT) for half in (x_hi, x_lo)]):
                        t = pe.matmul(ps[:, 4, i * P:(i + 1) * P], half[:, tt, j, :], pick[:, u, tt, :],
                                      start=(n == 0), stop=(n == 3))
                t.then_inc(xg_ps, 1)

            def turn_pick(g, u, gates):
                pe.wait_ge(xg_ev, 3 * g + 2)
                for tt in range(TT):
                    pe.transpose(ps[:, 4, tt * P:(tt + 1) * P], pick[:, u, tt, :].bitcast(F32), ident)
                for tt in range(TT):
                    t = pe.matmul(ps[:, 4, SEQ:SEQ + 2], pick[:, u, tt, :].bitcast(F32), gates(tt),
                                  start=(tt == 0), stop=(tt == TT - 1))
                t.then_inc(xg_ps, 1)

            def gate_up(g, u, turn):
                pe.wait_ge(xg_ev, 3 * g + 2)
                for i in range(2):
                    pe.wait_ge(gu_in[2 * u + i], turn)
                for j in range(J):
                    for i in range(2):
                        a, b = i * SLOTS, (i + 1) * SLOTS
                        t = pe.matmul(ps[a:b, 5, :], xg[:, u, j, a:b],
                                      gate_up_of(2 * u + i)[:, j * BANK:(j + 1) * BANK],
                                      start=(j == 0), stop=(j == J - 1))
                t.then_inc(gu_ps, 1)

            def turn_hidden(g, u):
                pe.wait_ge(hid_ok, g + 1)
                for f in range(FT):
                    t = pe.transpose(ps[:, 6, f * P:(f + 1) * P], hid[:, u, f:FF:FT], ident)
                t.then_inc(hidT_ps, 1)

            def down(g, u, half, turn):
                if half == 0:
                    pe.wait_ge(hidT_ev, g + 1)
                    for i in range(2):
                        pe.wait_ge(dn_in[2 * u + i], turn)
                for f in range(FT):
                    for i in range(2):
                        a, b = i * SLOTS, (i + 1) * SLOTS
                        at = f * D + half * BANK
                        t = pe.matmul(ps[a:b, 5 + 2 * half, :], hidT[:, u, f, a:b],
                                      down_of(2 * u + i)[:, at:at + BANK], start=(f == 0), stop=(f == FT - 1))
                t.then_inc(dn_ps, 1)

            def scatter(g, u, half, last=False):
                pe.wait_ge(ylo_ok, 2 * g + half + 1)
                if half == 0:
                    pe.wait_ge(xg_ev, 3 * g + 3)
                for tt in range(TT):
                    for y in (y_hi, y_lo):
                        pe.matmul(ps[:, tt * HALVES + half, :], place[:, u, tt * P:(tt + 1) * P], y[:, half, :],
                                  start=False, stop=last and y is y_lo, skip_group_check=True)

            def experts(layer):
                xT_wait(2 * layer + 1)
                pe.wait_ge(router_in, 16 * (layer + 1))
                for tt in range(TT):
                    for j in range(J):
                        t = pe.matmul(ps[:, 4, tt * NE:(tt + 1) * NE], xT[:, j, tt * P:(tt + 1) * P], w_router[:, j, :],
                                      start=(j == 0), stop=(j == J - 1))
                t.then_inc(logit_ps, 1)
                w = item("sgu", layer, 0)
                for tt in range(TT):
                    for j in range(J):
                        t = pe.matmul(ps[:, 5 + 2 * tt, :], xT[:, j, tt * P:(tt + 1) * P], w[:, j * BANK:(j + 1) * BANK],
                                      start=(j == 0), stop=(j == J - 1))
                    t.then_inc(sh_ps, 1)
                pe.wait_ge(chosen_ok, layer + 1)
                pos, before, ones = ps[:, 4, P:2 * P], const("before"), const("ones")
                pe.matmul(pos[:, 0:NE], before, chosen[:, 0, :], start=True, stop=True)
                pe.matmul(pos[:, NE:2 * NE], ones, chosen[:, 0, :], start=True, stop=False)
                pe.matmul(pos[:, NE:2 * NE], before, chosen[:, 1, :], start=False, stop=True)
                count = ps[:, 4, 2 * P:2 * P + NE]
                pe.matmul(count, ones, chosen[:, 0, :], start=True, stop=False)
                pe.matmul(count, ones, chosen[:, 1, :], start=False, stop=True).then_inc(pos_ps, 1)
                for tt in range(TT):
                    pe.wait_ge(sh_hid, TT * layer + tt + 1)
                    for f in range(FT):
                        t = pe.transpose(ps[:, 6, f * SEQ + tt * P:f * SEQ + (tt + 1) * P], hid[:, tt, f:FF:FT], ident)
                t.then_inc(shT_ps, 1)
                pe.wait_ge(ovf_cols_ok, layer + 1)
                for i in range(2):
                    a = 2 * P + NE + i * OVF
                    t = pe.matmul(ps[0:1, 4, a:a + OVF], ovf_cols[:, i:i + 1], ident[:, 0:OVF], start=True, stop=True)
                t.then_inc(ovf_row_ps, 1)
                pe.wait_ge(shT_ev, layer + 1)
                w = item("sdn", layer, 0)
                for tt in range(TT):
                    for half in range(HALVES):
                        for f in range(FT):
                            t = pe.matmul(ps[:, tt * HALVES + half, :], hidT[:, :, :, :].rearrange("p a b c -> p (a b c)")[:, f * SEQ + tt * P:f * SEQ + (tt + 1) * P],
                                          w[:, f * D + half * BANK:f * D + (half + 1) * BANK],
                                          start=(f == 0), stop=False, skip_group_check=True)
                t.then_inc(sdn_ps, 1)
                pe.wait_ge(ovf_ok, layer + 1)
                pe.wait_ge(x_split, TT * (layer + 1))
                base = layer * PAIRS

                def gates(e):
                    return lambda tt: gate[:, tt, e:e + 2] if isinstance(e, int) else gate[:, tt, bass.ds(e, 2)]

                def step(p, e, u, turn, last=False, first=False):
                    g = base + p
                    gate_up(g, u, turn)
                    if not first:
                        scatter(g - 1, 1 - u, 1)
                    if not last:
                        gather(g + 1, 1 - u, 0)
                    turn_hidden(g, u)
                    if not last:
                        gather(g + 1, 1 - u, 1)
                    down(g, u, 0, turn)
                    down(g, u, 1, turn)
                    if not last:
                        turn_pick(g + 1, 1 - u, gates(e + 2))
                    scatter(g, u, 0, last)

                first_turn = 16 * (PAIRS // 2) * layer
                gather(base, 0, 0, first=(layer == 0))
                gather(base, 0, 1)
                turn_pick(base, 0, gates(0))
                for p in range(2):
                    step(p, 2 * p, p % 2, first_turn + 16, first=(p == 0))
                with pe.Fori(1, PAIRS // 2 - 1) as it:
                    for u in range(2):
                        step(it * 2 + u, it * 4 + 2 * u, u, it * 16 + (first_turn + 16))
                for p in range(PAIRS - 2, PAIRS):
                    step(p, 2 * p, p % 2, first_turn + 16 * (p // 2 + 1), last=(p == PAIRS - 1))
                scatter(base + PAIRS - 1, 1, 1, last=True)

                s = OV[layer]
                n = pe.value_load(ovf_list[0:1, 0:1], min_val=0, max_val=OVF - 1)
                with pe.If(n > 0):
                    pe.drain().then_inc(s["done"], 1)
                    with pe.Fori(0, n) as i:
                        e = pe.value_load(ovf_list[0:1, bass.ds(i + 1, 1)], min_val=0, max_val=NE - 1)
                        pe.wait_ge(s["pick"], i + 1)
                        for r in range(2):
                            pe.wait_ge(s["xev"], i * 3 + (r + 1))
                            for c in range(4):
                                j = 4 * r + c
                                for k, (tt, half) in enumerate([(tt, half) for tt in range(TT) for half in (x_hi, x_lo)]):
                                    t = pe.matmul(ps[:, 4, c * P:(c + 1) * P], half[:, tt, j, :], pick[:, 0, tt, :],
                                                  start=(k == 0), stop=(k == 3))
                            t.then_inc(s["xps"], 1)
                        pe.wait_ge(s["xev"], i * 3 + 3)
                        for tt in range(TT):
                            pe.transpose(ps[:, 4, tt * P:(tt + 1) * P], pick[:, 0, tt, :].bitcast(F32), ident)
                        for tt in range(TT):
                            t = pe.matmul(ps[:, 4, SEQ:SEQ + 1], pick[:, 0, tt, :].bitcast(F32), gate[:, tt, bass.ds(e, 1)],
                                          start=(tt == 0), stop=(tt == TT - 1))
                        t.then_inc(s["xps"], 1)
                        pe.wait_ge(s["xev"], i * 3 + 4)
                        pe.wait_ge(s["gu_in"], i * 16 + 16)
                        for j in range(J):
                            t = pe.matmul(ps[:, 5, :], xg[:, 0, j, :], gate_up_of(0)[:, j * BANK:(j + 1) * BANK],
                                          start=(j == 0), stop=(j == J - 1))
                        t.then_inc(s["gups"], 1)
                        pe.wait_ge(s["hid"], i + 1)
                        for f in range(FT):
                            t = pe.transpose(ps[:, 6, f * P:(f + 1) * P], hid[:, 0, f:FF:FT], ident)
                        t.then_inc(s["tps"], 1)
                        pe.wait_ge(s["tev"], i + 1)
                        pe.wait_ge(s["dn_in"], i * 16 + 16)
                        for half in range(HALVES):
                            for f in range(FT):
                                at = f * D + half * BANK
                                t = pe.matmul(ps[:, 5 + 2 * half, :], hidT[:, 0, f, :], down_of(0)[:, at:at + BANK],
                                              start=(f == 0), stop=(f == FT - 1))
                        t.then_inc(s["dps"], 1)
                        pe.wait_ge(s["ylo"], i + 1)
                        for half in range(HALVES):
                            for tt in range(TT):
                                for y in (y_hi, y_lo):
                                    pe.matmul(ps[:, tt * HALVES + half, :], place[:, 0, tt * P:(tt + 1) * P], y[:, half, :],
                                              start=False, stop=(y is y_lo), skip_group_check=True)
                        pe.drain().then_inc(s["done"], 1)
                with pe.Else():
                    pe.nop()
                pe.drain().then_inc(moe_ps, 1)

            turn_x(1)
            experts(0)

            turn_x(2)
            xT_wait(2)
            n = 12
            for c in range(4):
                w = item("in", 1, c).rearrange("p (j n) -> p j n", j=J)
                for half in range(2):
                    t = columns_unit(w, half, n)
                    n += 1

            def level(i):
                m = LEVELS[i] if i < len(LEVELS) else 0
                if m:
                    pe.wait_ge(lev_ok, i + 1)
                    A = h_A[i % 2]
                bank = level_bank(i)
                if 2 <= i <= 6:
                    pe.wait_ge(lev_act, {2: 1, 3: 1, 4: 2, 5: 2, 6: 3}[i])
                if i >= 7:
                    pe.wait_ge(lev_dve, i - 6)
                if m == 128:
                    for h in range(HEADS):
                        t = pe.matmul(ps[:, 4 + h // 4, (h % 4) * P:(h % 4 + 1) * P], A[:, h, 0:P], A[:, h, P:SEQ],
                                      start=True, stop=True)
                elif m == 64:
                    for h in range(HEADS):
                        for tt in range(TT):
                            k, a = h * TT + tt, tt * P
                            t = pe.matmul(ps[0:64, 6 + k // 8, (k % 8) * 64:(k % 8 + 1) * 64], A[:, h, a:a + 64],
                                          A[:, h, a + 64:a + P], start=True, stop=True)
                else:
                    for h in range(HEADS):
                        for tt in range(TT):
                            for q in range(4):
                                if m == 32 and q % 2:
                                    continue
                                k, a = h * TT + tt, tt * P + 32 * q
                                lhs = A[:, h, a:a + 32] if m else h_kT[:, h, a:a + 32]
                                rhs = A[:, h, a + 32:a + 64] if m == 32 else A[:, h, a:a + 32] if m else h_qT[:, h, a:a + 32]
                                t = pe.matmul(ps[32 * q:32 * q + 32, bank, 32 * k:32 * k + 32], lhs, rhs,
                                              start=True, stop=True)
                t.then_inc(lev_ps, 1)

            for c in range(4, 8):
                w = item("in", 1, c).rearrange("p (j n) -> p j n", j=J)
                for tt in range(TT):
                    rows_unit(w, tt, n)
                    n += 1
                    level(n - 21)
            level(8)
            pe.wait_ge(scores_ok, 1)
            pe.wait_ge(lev_act, 3)
            pe.wait_ge(proj_ev, n)
            for tt in range(TT):
                for h in range(HEADS):
                    o = ps[:, 2 * tt + h // 4, (h % 4) * P:(h % 4 + 1) * P]
                    v = h_v[:, :, h * P:(h + 1) * P]
                    if tt == 1:
                        pe.matmul(o, cross[:, h, :], v[:, 0, :], start=True, stop=False)
                    t = pe.matmul(o, scoreT[:, h * TT + tt, :], v[:, tt, :], start=(tt == 0), stop=True)
                t.then_inc(ho_ps, 1)
            out_projection(1, h_o)
            turn_x(3)
            experts(1)

        @block.scalar
        def _(act):
            links = [0]

            def link(t):
                links[0] += 1
                t.then_inc(act_chain, 1)
                act.wait_ge(act_chain, links[0])

            def f(out_, in_, func=ACT.Copy, **kw):
                return nc.scalar.activation(out_, in_, func, **kw)

            def xT_copies(b):
                for tt in range(TT):
                    act.wait_ge(xT_ps, 2 * b + tt + 1)
                    f(xT[:, 0:4, tt * P:(tt + 1) * P], ps[:, 2 * tt, :].rearrange("p (j t) -> p j t", j=4)).then_inc(xT_act, 1)

            def out_copies(layer, gain):
                for r in range(4):
                    tt, hh = r // 2, r % 2
                    act.wait_ge(oT_ps, 4 * layer + r + 1)
                    f(oT[:, 4 * hh:4 * hh + 4, tt * P:(tt + 1) * P], ps[:, 4 + r, :].rearrange("p (h t) -> p h t", h=4),
                      scale=gain).then_inc(oT_ev, 1)

            def layer_norm(n, split):
                for tt in range(TT):
                    k = 2 * n + tt
                    act.wait_ge(ln_var, k + 1)
                    f(rstd, eps_var, ACT.Sqrt).then_inc(ln_std, 1)
                    act.wait_ge(ln_nmr, k + 1)
                    f(x[:, tt, :], x[:, tt, :], ACT.Identity, scale=rstd, bias=nmr).then_inc(ln_lin, 1)

            def split_x(n):
                for tt in range(TT):
                    act.wait_ge(x_ready, 2 * n + tt + 1)
                    f(x_hi[:, tt, :, :], x[:, tt, :].rearrange("t (p j) -> t j p", j=J)).then_inc(xhi_ok, 1)

            xT_copies(0)
            act.wait_ge(lam_a, 1)
            f(lam2, lam2, ACT.Exp).then_inc(lam_b, 1)
            act.wait_ge(lb_exp_in, 1)
            f(lb_e, lb_e, ACT.Exp).then_inc(lb_exp_ok, 1)
            for n in range(12):
                c, tt = n // 2, n % 2
                act.wait_ge(proj_ps, n + 1)
                f(qkv[:, c // 2, tt, (c % 2) * BANK:(c % 2 + 1) * BANK], ps[:, n % 4, :]).then_inc(proj_ev, 1)
            for r in range(0, 8, 2):
                act.wait_ge(turn_ps, r + 1)
                dst = a_qT if r < 4 else a_kT
                f(dst[:, 2 * (r % 4):2 * (r % 4) + 2, :], ps[:, 4, :].rearrange("p (h t) -> p h t", h=2)).then_inc(turn_act, 1)

            def soften(h):
                act.wait_ge(nmax_ok, h + 1)
                for i, (tile, m) in enumerate(((0, 0), (0, 1), (1, 0), (1, 1))):
                    keys = slice(0, P) if tile == 0 else slice(P, P + SEQ)
                    t = f(probs[:, h % 2, m, keys], masked[:, h % 2, m, keys], ACT.Exp, scale=SUB ** -0.5,
                          bias=row_max[:, h % 2, i:i + 1], accum_out=row_sum[:, h % 2, i:i + 1])
                t.then_inc(probs_ok, 1)

            soften(0)
            for h in range(HEADS):
                if h + 1 < HEADS:
                    soften(h + 1)
                act.wait_ge(dT_ps, h + 1)
                f(diffT[:, h % 2, :], ps[:, 4 + h % 2, 0:P + SEQ]).then_inc(dT_ev, 1)
                act.wait_ge(pv_ps, h + 1)
                o = ps[:, 6 + h % 2, 0:SEQ].rearrange("p (a n) -> p a n", a=TT)
                for tt in range(TT):
                    f(part(work, 4608, 2, P)[:, tt, :], o[:, tt, :], ACT.Square, accum_out=o_sq[:, tt * HEADS + h:tt * HEADS + h + 1])
                f(a_o[:, :, h * P:(h + 1) * P], o).then_inc(o_ev, 1)
            act.wait_ge(ms_ok, 1)
            f(o_rs, o_sq, ACT.Sqrt).then_inc(root_ok, 1)
            out_copies(0, head_gain)
            layer_norm(0, True)
            xT_copies(1)

            def experts(layer):
                act.wait_ge(logit_ps, layer + 1)
                f(score, ps[:, 4, 0:P].rearrange("p (a e) -> p a e", a=TT), ACT.Sigmoid).then_inc(score_ok, 1)
                split_x(2 * layer)
                for tt in range(TT):
                    act.wait_ge(sh_ps, TT * layer + tt + 1)
                    f(silu[:, tt, :], ps[:, 5 + 2 * tt, 0:FF], ACT.Silu).then_inc(sh_silu, 1)
                act.wait_ge(shT_ps, layer + 1)
                f(hidT[:, :, :, :].rearrange("p a b c -> p (a b c)"), ps[:, 6, :]).then_inc(shT_ev, 1)

                def gathered(g, u, r):
                    act.wait_ge(xg_ps, 3 * g + r + 1)
                    f(xg[:, u, 4 * r:4 * r + 4, :], ps[:, 4, :].rearrange("p (j c) -> p j c", j=4)).then_inc(xg_ev, 1)

                def placed(g, u):
                    act.wait_ge(xg_ps, 3 * g + 3)
                    f(place[:, u, :], ps[:, 4, 0:SEQ])
                    f(gate_slot[0:SLOTS, u:u + 1], ps[0:SLOTS, 4, SEQ:SEQ + 1])
                    f(gate_slot[SLOTS:P, u:u + 1], ps[SLOTS:P, 4, SEQ + 1:SEQ + 2]).then_inc(xg_ev, 1)

                base = layer * PAIRS

                def step(p, u, last=False):
                    g = base + p
                    act.wait_ge(gu_ps, g + 1)
                    f(silu[:, u, :], ps[:, 5, 0:FF], ACT.Silu).then_inc(silu_ok, 1)
                    if not last:
                        gathered(g + 1, 1 - u, 0)
                    act.wait_ge(hidT_ps, g + 1)
                    f(hidT[:, u, :, :], ps[:, 6, 0:SEQ].rearrange("p (f c) -> p f c", f=FT)).then_inc(hidT_ev, 1)
                    if not last:
                        gathered(g + 1, 1 - u, 1)
                    for half in range(HALVES):
                        act.wait_ge(dn_ps, 2 * g + half + 1)
                        f(y_hi[:, half, :], ps[:, 5 + 2 * half, :]).then_inc(yhi_ok, 1)
                    if not last:
                        placed(g + 1, 1 - u)

                gathered(base, 0, 0)
                gathered(base, 0, 1)
                placed(base, 0)
                with act.Fori(0, PAIRS // 2 - 1) as it:
                    for u in range(2):
                        step(it * 2 + u, u)
                step(PAIRS - 2, 0)
                step(PAIRS - 1, 1, last=True)

                s = OV[layer]
                act.wait_ge(ovf_ok, layer + 1)
                n = act.value_load(ovf_list[0:1, 0:1], min_val=0, max_val=OVF - 1)
                with act.If(n > 0):
                    act.wait_ge(s["done"], 1)
                    act.drain().then_inc(s["xev"], 1)
                    with act.Fori(0, n) as i:
                        for r in range(2):
                            act.wait_ge(s["xps"], i * 3 + (r + 1))
                            f(xg[:, 0, 4 * r:4 * r + 4, :], ps[:, 4, :].rearrange("p (j c) -> p j c", j=4)).then_inc(s["xev"], 1)
                        act.wait_ge(s["xps"], i * 3 + 3)
                        f(place[:, 0, :], ps[:, 4, 0:SEQ])
                        f(gate_slot[:, 0:1], ps[:, 4, SEQ:SEQ + 1]).then_inc(s["xev"], 1)
                        act.wait_ge(s["gups"], i + 1)
                        f(silu[:, 0, :], ps[:, 5, 0:FF], ACT.Silu).then_inc(s["silu"], 1)
                        act.wait_ge(s["tps"], i + 1)
                        f(hidT[:, 0, :, :], ps[:, 6, 0:SEQ].rearrange("p (f c) -> p f c", f=FT)).then_inc(s["tev"], 1)
                        act.wait_ge(s["dps"], i + 1)
                        for half in range(HALVES):
                            t = f(y_hi[:, half, :], ps[:, 5 + 2 * half, :])
                        t.then_inc(s["yhi"], 1)
                with act.Else():
                    act.nop()

            experts(0)
            layer_norm(1, False)

            xT_copies(2)
            n = 12
            for i in range(4):
                act.wait_ge(proj_ps, n + 1)
                f(h_b[:, 2 * i:2 * i + 2, :], ps[:, n % 4, :].rearrange("p (h t) -> p h t", h=2), ACT.Sigmoid).then_inc(proj_ev, 1)
                n += 1
            act.wait_ge(forget_ok, 1)
            f(h_b, h_b, ACT.Ln).then_inc(logf_ok, 1)
            for i in range(4):
                act.wait_ge(proj_ps, n + 1)
                f(h_qT[:, 2 * i:2 * i + 2, :], ps[:, n % 4, :].rearrange("p (h t) -> p h t", h=2), ACT.Silu).then_inc(proj_ev, 1)
                n += 1

            def exponentials(i):
                A, m = h_A[i % 2], LEVELS[i]
                act.wait_ge(expo_ok, i + 1)
                quarter = "p h (c t) -> p h c t"
                if m == 128:
                    f(A[:, :, 2 * CHUNK:3 * CHUNK], h_b[:, :, 2 * CHUNK:3 * CHUNK], ACT.Exp)
                    f(A[:, :, 0:2 * CHUNK], A[:, :, 0:2 * CHUNK], ACT.Exp)
                    f(A[:, :, 3 * CHUNK:], A[:, :, 3 * CHUNK:], ACT.Exp).then_inc(exp_ok, 1)
                elif m == 64:
                    a, b = (v.rearrange(quarter, c=4) for v in (A, h_b))
                    f(a[:, :, 1::2, :], b[:, :, 1::2, :], ACT.Exp)
                    f(a[:, :, 0::2, :], a[:, :, 0::2, :], ACT.Exp).then_inc(exp_ok, 1)
                else:
                    f(A, A, ACT.Exp).then_inc(exp_ok, 1)

            def pieces(i):
                act.wait_ge(lev_ps, i + 1)
                if i == 0:
                    for b in range(2):
                        t = f(cross[:, 4 * b:4 * b + 4, :], ps[:, 4 + b, :].rearrange("p (h t) -> p h t", h=4))
                elif i == 1:
                    for b in range(2):
                        t = f(scoreT[0:64, 8 * b:8 * b + 8, 64:P], ps[0:64, 6 + b, :].rearrange("p (k t) -> p k t", k=8))
                else:
                    for q in (0, 2):
                        a = 32 * q
                        t = f(scoreT[a:a + 32, :, a + 32:a + 64],
                              ps[a:a + 32, level_bank(2), :].rearrange("p (k t) -> p k t", k=16))
                t.then_inc(lev_act, 1)

            exponentials(0)
            for i in range(4):
                exponentials(i + 1)
                act.wait_ge(proj_ps, n + 1)
                c, tt = i // 2, i % 2
                f(h_v[:, tt, c * BANK:(c + 1) * BANK], ps[:, n % 4, :]).then_inc(proj_ev, 1)
                n += 1
                if i < 3:
                    if i == 1:
                        act.wait_ge(scores_clear, 1)
                    pieces(i)
            for i in range(5, len(LEVELS)):
                exponentials(i)
            for i in range(4):
                act.wait_ge(proj_ps, n + 1)
                c, tt = i // 2, i % 2
                f(h_gate[:, tt, c * BANK:(c + 1) * BANK], ps[:, n % 4, :], ACT.Silu).then_inc(proj_ev, 1)
                n += 1
            for tt in range(TT):
                act.wait_ge(ho_ps, tt + 1)
                for h in range(HEADS):
                    t = f(part(odd, 6144 + (tt * HEADS + h) * P, P), ps[:, 2 * tt + h // 4, (h % 4) * P:(h % 4 + 1) * P], ACT.Square,
                          accum_out=o_sq[:, tt * HEADS + h:tt * HEADS + h + 1])
                t.then_inc(sq_ok, 1)
            act.wait_ge(ms_ok, 2)
            f(o_rs, o_sq, ACT.Sqrt).then_inc(root_ok, 1)
            out_copies(1, norm_h)
            layer_norm(2, True)
            xT_copies(3)
            experts(1)
            layer_norm(3, False)

        @block.vector
        def _(dve):
            links = [0]

            def link(t):
                links[0] += 1
                t.then_inc(dve_chain, 1)
                dve.wait_ge(dve_chain, links[0])

            tt_op = nc.vector.tensor_tensor
            ts_op = nc.vector.tensor_scalar
            stt = nc.vector.scalar_tensor_tensor

            def wait_item(name, layer, c):
                k = ITEM[name, layer, c]
                n = sum(2 if ITEMS[i][0] == "ln" else 1 for i in range(k % 2, k + 1, 2))
                dve.wait_ge(stream_in[k % 2], 16 * n)
                return stream[:, k % 2, :]

            def xT_copies(b):
                for tt in range(TT):
                    dve.wait_ge(xT_ps, 2 * b + tt + 1)
                    nc.vector.tensor_copy(xT[:, 4:8, tt * P:(tt + 1) * P],
                                          ps[:, 2 * tt + 1, :].rearrange("p (j t) -> p j t", j=4)).then_inc(xT_dve, 1)

            def layer_norm(n, ready):
                w = wait_item("ln", n // 2, n % 2)
                for tt in range(TT):
                    k = 2 * n + tt
                    ready(tt)
                    for half in range(HALVES):
                        cols = slice(half * BANK, (half + 1) * BANK)
                        t = stt(out=x[:, tt, cols], in0=x[:, tt, cols], scalar=ALPHA, in1=ps[:, tt * HALVES + half, :],
                                op0=ALU.mult, op1=ALU.add)
                    link(t)
                    for half in range(HALVES):
                        t = nc.vector.bn_stats(stats[:, half, :], x[:, tt, half * BANK:(half + 1) * BANK])
                    link(t)
                    link(nc.vector.bn_aggr(mean_var, stats.rearrange("p a b -> p (a b)")))
                    ts_op(eps_var, mean_var[:, 1:2], EPS, None, ALU.add).then_inc(ln_var, 1)
                    dve.wait_ge(ln_std, k + 1)
                    link(nc.vector.reciprocal(rstd, rstd))
                    ts_op(nmr, mean_var[:, 0:1], rstd, -1.0, ALU.mult, ALU.mult).then_inc(ln_nmr, 1)
                    dve.wait_ge(ln_lin, k + 1)
                    link(tt_op(x[:, tt, :], x[:, tt, :], w[:, 0:D], ALU.mult))
                    tt_op(x[:, tt, :], x[:, tt, :], w[:, D:2 * D], ALU.add).then_inc(x_ready, 1)

            def split_x(layer):
                for tt in range(TT):
                    dve.wait_ge(xhi_ok, TT * layer + tt + 1)
                    tt_op(x_lo[:, tt, :, :], x[:, tt, :].rearrange("t (p j) -> t j p", j=J),
                          x_hi[:, tt, :, :].bitcast(F32), ALU.subtract).then_inc(x_split, 1)

            dve.wait_ge(vec_in, 64)
            dve.wait_ge(const_in, 32)
            link(tt_op(lam_prod, lam_row[:, 0::2, :], lam_row[:, 1::2, :], ALU.mult))
            nc.vector.tensor_reduce(lam2, lam_prod, AX, ALU.add).then_inc(lam_a, 1)
            xT_copies(0)
            dve.wait_ge(lam_b, 1)
            link(tt_op(neg_lam, lam2[:, 1:2], lam2[:, 0:1], ALU.subtract))
            link(ts_op(neg_lam, neg_lam, -LAMBDA_INIT, None, ALU.add))

            dve.wait_ge(lb_ps, 1)
            link(nc.vector.tensor_copy(lb_e.rearrange("p a h -> p (a h)"), ps[:, 6, 0:DEPTH * HEADS]))
            link(tt_op(lb_max, lb_e[:, 0, :], lb_e[:, 1, :], ALU.max))
            tt_op(lb_e, lb_e, lb_max[:, None, :].broadcast_to([P, DEPTH, HEADS]), ALU.subtract).then_inc(lb_exp_in, 1)
            dve.wait_ge(lb_exp_ok, 1)
            link(tt_op(lb_sum, lb_e[:, 0, :], lb_e[:, 1, :], ALU.add))
            link(nc.vector.reciprocal(lb_sum, lb_sum))
            link(tt_op(lb_e, lb_e, lb_sum[:, None, :].broadcast_to([P, DEPTH, HEADS]), ALU.mult))
            link(tt_op(lb_low, lb_e[:, 0, :], lb_e[:, 1, :], ALU.add))
            link(tt_op(lb_low, lb_low, lb_e[:, 0, :], ALU.subtract))
            link(ts_op(lb_rest, lb_low, -1.0, 1.0, ALU.mult, ALU.add))

            rope_tmp = [part(work, 256 * i, TT, 16, RH) for i in range(4)]
            cos = const("cos").rearrange("p (a r) -> p a r", a=TT)[:, :, None, :].broadcast_to([P, TT, 16, RH])
            sin = const("sin").rearrange("p (a r) -> p a r", a=TT)[:, :, None, :].broadcast_to([P, TT, 16, RH])
            for i, tok in enumerate((q_tok, k_tok)):
                dve.wait_ge(proj_ev, 4 * i + 4)
                if i:
                    dve.wait_ge(rope_ok, i)
                v = tok.rearrange("p a (h s) -> p a h s", s=SUB)
                x1, x2 = v[:, :, :, 0:RH], v[:, :, :, RH:ROT]
                for t_, a_, b_ in zip(rope_tmp, (x1, x2, x2, x1), (cos, sin, cos, sin)):
                    t = tt_op(t_, a_, b_, ALU.mult)
                link(t)
                link(tt_op(x1, rope_tmp[0], rope_tmp[1], ALU.subtract))
                tt_op(x2, rope_tmp[2], rope_tmp[3], ALU.add).then_inc(rope_ok, 1)
            for r in range(1, 8, 2):
                dve.wait_ge(turn_ps, r + 1)
                dst = a_qT if r < 4 else a_kT
                nc.vector.tensor_copy(dst[:, 2 * (r % 4):2 * (r % 4) + 2, :],
                                      ps[:, 5, :].rearrange("p (h t) -> p h t", h=2)).then_inc(turn_dve, 1)

            def front(h):
                u = h % 2
                dve.wait_ge(sc_ps, h + 1)
                mask = const("amask")[:, None, :].broadcast_to([P, 2, P + SEQ])
                link(tt_op(masked[:, u, :, :], ps[:, 2 * u:2 * u + 2, 0:P + SEQ], mask, ALU.add))
                nc.vector.tensor_reduce(row_max[:, u, 0:2], masked[:, u, :, 0:P], AX, ALU.max)
                link(nc.vector.tensor_reduce(row_max[:, u, 2:4], masked[:, u, :, P:P + SEQ], AX, ALU.max))
                ts_op(row_max[:, u, :], row_max[:, u, :], -SUB ** -0.5, None, ALU.mult).then_inc(nmax_ok, 1)

            def back(h):
                u = h % 2
                dve.wait_ge(probs_ok, h + 1)
                if h:
                    dve.wait_ge(diff_ok, h)
                link(nc.vector.reciprocal(row_scale, row_sum[:, u, :]))
                link(ts_op(row_scale[:, 1:4:2], row_scale[:, 1:4:2], neg_lam, None, ALU.mult))
                keys = (slice(0, P), slice(P, P + SEQ))
                for tile in range(2):
                    t = ts_op(probs[:, u, 1, keys[tile]], probs[:, u, 1, keys[tile]], row_scale[:, 2 * tile + 1:2 * tile + 2], None, ALU.mult)
                link(t)
                for tile in range(2):
                    t = stt(out=diff[:, u, keys[tile]], in0=probs[:, u, 0, keys[tile]], scalar=row_scale[:, 2 * tile:2 * tile + 1],
                            in1=probs[:, u, 1, keys[tile]], op0=ALU.mult, op1=ALU.add)
                t.then_inc(diff_ok, 1)

            front(0)
            for h in range(HEADS):
                if h + 1 < HEADS:
                    front(h + 1)
                back(h)
            dve.wait_ge(o_ev, HEADS)
            ts_op(o_sq, o_sq, 1.0 / P, EPS, ALU.mult, ALU.add).then_inc(ms_ok, 1)
            dve.wait_ge(root_ok, 1)
            link(nc.vector.reciprocal(o_rs, o_rs))
            link(ts_op(o_rs, o_rs, 1.0 - LAMBDA_INIT, None, ALU.mult))
            for tt in range(TT):
                v = a_o[:, tt, :].rearrange("p (h n) -> p h n", h=HEADS)
                r = o_rs[:, tt * HEADS:(tt + 1) * HEADS][:, :, None].broadcast_to([P, HEADS, P])
                tt_op(v, v, r, ALU.mult).then_inc(on_ok, 1)
            layer_norm(0, lambda tt: dve.wait_ge(outp_ps, 3 + tt))
            xT_copies(1)

            def route(layer):
                dve.wait_ge(bias_in, 16 * (layer + 1))
                dve.wait_ge(score_ok, layer + 1)
                link(tt_op(choice, score, bias_row[:, None, :].broadcast_to([P, TT, NE]), ALU.add))
                groups = choice.rearrange("p a (g e) -> p (a g) e", e=GE)
                for i in range(TT * NG):
                    t = nc.vector.max(best8[:, i, :], groups[:, i, :])
                link(t)
                link(tt_op(g_sum, best8[:, :, 0], best8[:, :, 1], ALU.add))
                gv = g_sum.rearrange("p (a g) -> p a g", a=TT)
                r4, t4 = (v.rearrange("p (a g) k -> p a g k", a=TT) for v in (rank4, tie4))
                other = gv[:, :, None, :].broadcast_to([P, TT, NG, NG])
                own = gv[:, :, :, None].broadcast_to([P, TT, NG, NG])
                tt_op(r4, other, own, ALU.is_gt)
                link(tt_op(t4, other, own, ALU.is_equal))
                lower = const("lower").rearrange("p (g k) -> p g k", g=NG)[:, None, :, :].broadcast_to([P, TT, NG, NG])
                link(tt_op(t4, t4, lower, ALU.mult))
                link(tt_op(rank4, rank4, tie4, ALU.add))
                link(nc.vector.tensor_reduce(g_rank, rank4, AX, ALU.add))
                link(ts_op(g_rank, g_rank, float(TOPG), None, ALU.is_lt))
                link(ts_op(g_pen, g_rank, -1.0, BIG, ALU.add, ALU.mult))
                kg = kept.rearrange("p a (g e) -> p (a g) e", e=GE)
                link(tt_op(kg, groups, g_rank[:, :, None].broadcast_to([P, TT * NG, GE]), ALU.mult))
                link(tt_op(kg, kg, g_pen[:, :, None].broadcast_to([P, TT * NG, GE]), ALU.add))
                for tt in range(TT):
                    t = nc.vector.max(top8[:, tt, :], kept[:, tt, :])
                link(t)
                for tt in range(TT):
                    t = nc.vector.match_replace(out=replaced[:, tt, :], in_to_replace=top8[:, tt, :],
                                                in_values=kept[:, tt, :], imm_value=-3.3e38)
                link(t)
                tt_op(chosen, replaced, kept, ALU.not_equal).then_inc(chosen_ok, 1)
                dve.wait_ge(chosen_ok, layer + 1)
                link(tt_op(gate, score, chosen, ALU.mult))
                link(nc.vector.tensor_reduce(w_sum, gate, AX, ALU.add))
                link(ts_op(w_sum, w_sum, 1e-20, None, ALU.add))
                link(nc.vector.reciprocal(w_sum, w_sum))
                link(ts_op(w_sum, w_sum, ROUTED_SCALE, None, ALU.mult))
                link(tt_op(gate, gate, w_sum[:, :, None].broadcast_to([P, TT, NE]), ALU.mult))
                dve.wait_ge(pos_ps, layer + 1)
                stt(out=slot, in0=ps[:, 4, P:2 * P].rearrange("p (a e) -> p a e", a=TT), scalar=-NO_SLOT, in1=chosen,
                    op0=ALU.add, op1=ALU.mult).then_inc(route_ok, 1)
                for b in range(1, BLOCKS):
                    t = ts_op(flags[:, (b - 1) * NE:b * NE], ps[:, 4, 2 * P:2 * P + NE], float(b * SLOTS), None, ALU.is_gt)
                link(t)
                ones = const("ones")[:, 0:1].broadcast_to([P, EXTRA])
                link(nc.vector.tensor_tensor_scan(flags_sum, ones, flags, 0.0, ALU.mult, ALU.add))
                link(tt_op(listed, flags_sum, flags, ALU.subtract))
                link(stt(out=listed, in0=listed, scalar=const("row"), in1=flags, op0=ALU.is_equal, op1=ALU.mult))
                for i, name in enumerate(("ovf_e", "ovf_b")):
                    link(tt_op(listed_id, listed, const(name), ALU.mult))
                    t = nc.vector.tensor_reduce(ovf_cols[:, i:i + 1], listed_id, AX, ALU.add)
                    if i == 0:
                        link(t)
                t.then_inc(ovf_cols_ok, 1)

            def read_list(layer):
                dve.wait_ge(ovf_row_ps, layer + 1)
                nc.vector.tensor_copy(ovf_list[:, 0:1], flags_sum[0:1, EXTRA - 1:EXTRA])
                nc.vector.tensor_copy(ovf_list[:, 1:1 + 2 * OVF], ps[0:1, 4, 2 * P + NE:2 * P + NE + 2 * OVF]).then_inc(ovf_ok, 1)

            def shared(layer):
                for tt in range(TT):
                    dve.wait_ge(sh_silu, TT * layer + tt + 1)
                    tt_op(hid[:, tt, :], silu[:, tt, :], ps[:, 5 + 2 * tt, FF:2 * FF], ALU.mult).then_inc(sh_hid, 1)

            def experts(layer):
                route(layer)
                shared(layer)
                read_list(layer)
                split_x(layer)
                dve.wait_ge(route_ok, layer + 1)
                base = layer * PAIRS
                iota = const("iota")[:, 0:SLOTS][:, None, None, :].broadcast_to([P, TT, 2, SLOTS])

                def one_hot(g, e, u):
                    if not isinstance(g, int) or g >= 2:
                        dve.wait_ge(xg_ps, 3 * g - 3)
                    s = slot[:, :, e:e + 2] if isinstance(e, int) else slot[:, :, bass.ds(e, 2)]
                    tt_op(pick[:, u, :, :].rearrange("p a (e c) -> p a e c", e=2), iota,
                          s[:, :, :, None].broadcast_to([P, TT, 2, SLOTS]), ALU.is_equal).then_inc(pick_ok, 1)

                def step(p, e, u, more=True):
                    g = base + p
                    dve.wait_ge(silu_ok, g + 1)
                    dve.wait_ge(xg_ev, 3 * g + 3)
                    stt(out=hid[:, u, :], in0=silu[:, u, :], scalar=gate_slot[:, u:u + 1], in1=ps[:, 5, FF:2 * FF],
                        op0=ALU.mult, op1=ALU.mult).then_inc(hid_ok, 1)
                    if more:
                        one_hot(g + 2, e + 4, u)
                    for half in range(HALVES):
                        dve.wait_ge(yhi_ok, 2 * g + half + 1)
                        tt_op(y_lo[:, half, :], ps[:, 5 + 2 * half, :], y_hi[:, half, :].bitcast(F32),
                              ALU.subtract).then_inc(ylo_ok, 1)

                one_hot(base, 0, 0)
                one_hot(base + 1, 2, 1)
                with dve.Fori(0, PAIRS // 2 - 1) as it:
                    for u in range(2):
                        step(it * 2 + u, it * 4 + 2 * u, u)
                step(PAIRS - 2, 0, 0, more=False)
                step(PAIRS - 1, 0, 1, more=False)

                s = OV[layer]
                n = dve.value_load(ovf_list[0:1, 0:1], min_val=0, max_val=OVF - 1)
                with dve.If(n > 0):
                    nc.vector.memset(pick[:, 0, :, SLOTS:P].bitcast(F32), 0.0)
                    with dve.Fori(0, n) as i:
                        e = dve.value_load(ovf_list[0:1, bass.ds(i + 1, 1)], min_val=0, max_val=NE - 1)
                        b = dve.value_load(ovf_list[0:1, bass.ds(i + (1 + OVF), 1)], min_val=0, max_val=BLOCKS - 1)
                        dve.wait_ge(s["done"], i + 1)
                        sl = slot[:, :, bass.ds(e, 1)].broadcast_to([P, TT, SLOTS])
                        io = cst[:, bass.ds(b * SLOTS + CONST_AT["iota"][0], SLOTS)][:, None, :].broadcast_to([P, TT, SLOTS])
                        tt_op(pick[:, 0, :, 0:SLOTS], io, sl, ALU.is_equal).then_inc(s["pick"], 1)
                        dve.wait_ge(s["silu"], i + 1)
                        stt(out=hid[:, 0, :], in0=silu[:, 0, :], scalar=gate_slot[:, 0:1], in1=ps[:, 5, FF:2 * FF],
                            op0=ALU.mult, op1=ALU.mult).then_inc(s["hid"], 1)
                        dve.wait_ge(s["yhi"], i + 1)
                        for half in range(HALVES):
                            t = tt_op(y_lo[:, half, :], ps[:, 5 + 2 * half, :], y_hi[:, half, :].bitcast(F32), ALU.subtract)
                        t.then_inc(s["ylo"], 1)
                with dve.Else():
                    dve.nop()

            experts(0)
            layer_norm(1, lambda tt: dve.wait_ge(moe_ps, 1))

            xT_copies(2)
            dve.wait_ge(proj_ev, 16)
            for h in range(HEADS):
                t = ts_op(h_b[:, h, :], h_b[:, h, :], lb_rest[:, h:h + 1], lb_low[:, h:h + 1], ALU.mult, ALU.add)
            link(t)
            link(ts_op(h_kT, h_b, -1.0, 1.0, ALU.mult, ALU.add))
            ts_op(h_b, h_b, FORGET_MIN, None, ALU.max).then_inc(forget_ok, 1)
            nc.vector.memset(scoreT, 0.0)
            nc.vector.memset(compact, 0.0).then_inc(scores_clear, 1)
            dve.wait_ge(logf_ok, 1)
            for h in range(HEADS):
                for c in range(SEQ // CHUNK):
                    v = h_b[:, h, c * CHUNK:(c + 1) * CHUNK]
                    t = nc.vector.tensor_tensor_scan(v, const("ones")[:, 0:CHUNK], v, 0.0, ALU.mult, ALU.add)
            link(t)
            b4 = h_b.rearrange("p h (c t) -> p h c t", c=4)

            def exponents(i):
                m, A = LEVELS[i], h_A[i % 2]
                if i >= 2:
                    dve.wait_ge(lev_ps, i - 1)
                last = b4[:, :, :, CHUNK - 1:CHUNK]
                A4 = A.rearrange("p h (c t) -> p h c t", c=4)
                wide = [P, HEADS, CHUNK]
                if m == 128:
                    link(tt_op(c01, last[:, :, 0], last[:, :, 1], ALU.add))
                    tt_op(A4[:, :, 0], c01.broadcast_to(wide), b4[:, :, 0], ALU.subtract)
                    tt_op(A4[:, :, 1], last[:, :, 1].broadcast_to(wide), b4[:, :, 1], ALU.subtract)
                    t = tt_op(A4[:, :, 3], b4[:, :, 3], last[:, :, 2].broadcast_to(wide), ALU.add)
                elif m == 64:
                    t = tt_op(A4[:, :, 0::2], last[:, :, 0::2].broadcast_to([P, HEADS, 2, CHUNK]), b4[:, :, 0::2], ALU.subtract)
                else:
                    a, b = (v.rearrange("p h t -> p (h t)").rearrange("p (n s m) -> p n s m", s=2, m=m) for v in (A, h_b))
                    mid = b[:, :, 0, m - 1:m].broadcast_to([P, HEADS * SEQ // (2 * m), m])
                    tt_op(a[:, :, 1], b[:, :, 1], mid, ALU.subtract)
                    t = tt_op(a[:, :, 0], mid, b[:, :, 0], ALU.subtract)
                t.then_inc(expo_ok, 1)

            def factors(i):
                m, A = LEVELS[i], h_A[i % 2]
                dve.wait_ge(exp_ok, i + 1)
                if i == 0:
                    dve.wait_ge(proj_ev, 20)
                a, q, k = (v.rearrange("p h t -> p (h t)").rearrange("p (n s m) -> p n s m", s=2, m=m) for v in (A, h_qT, h_kT))
                tt_op(a[:, :, 1], a[:, :, 1], q[:, :, 1], ALU.mult)
                tt_op(a[:, :, 0], a[:, :, 0], k[:, :, 0], ALU.mult).then_inc(lev_ok, 1)

            def merge(i):
                dve.wait_ge(lev_ps, i + 1)
                if i > 3:
                    dve.wait_ge(lev_dve, i - 3)
                which = masks[:, (i - 3) * 32:(i - 2) * 32][:, None, :].broadcast_to([P, HEADS * TT, 32])
                nc.vector.copy_predicated(compact, which, ps[:, level_bank(i), :].rearrange("p (k t) -> p k t", k=HEADS * TT))\
                  .then_inc(lev_dve, 1)

            dve.wait_ge(scores_clear, 1)
            exponents(0)
            for i in range(len(LEVELS)):
                if i + 1 < len(LEVELS):
                    exponents(i + 1)
                factors(i)
                if i > 3:
                    merge(i - 1)
            merge(7)
            merge(8)
            dve.wait_ge(lev_dve, 6)
            for q in range(4):
                a = 32 * q
                t = nc.vector.tensor_copy(scoreT[a:a + 32, :, a:a + 32], compact[a:a + 32, :, :])
            t.then_inc(scores_ok, 1)
            dve.wait_ge(sq_ok, 2)
            ts_op(o_sq, o_sq, 1.0 / P, EPS, ALU.mult, ALU.add).then_inc(ms_ok, 1)
            dve.wait_ge(root_ok, 2)
            link(nc.vector.reciprocal(o_rs, o_rs))
            for tt in range(TT):
                for h in range(HEADS):
                    cols = slice(h * P, (h + 1) * P)
                    t = stt(out=h_o[:, tt, cols], in0=ps[:, 2 * tt + h // 4, (h % 4) * P:(h % 4 + 1) * P],
                            scalar=o_rs[:, tt * HEADS + h:tt * HEADS + h + 1], in1=h_gate[:, tt, cols], op0=ALU.mult, op1=ALU.mult)
                t.then_inc(on_ok, 1)
            layer_norm(2, lambda tt: dve.wait_ge(outp_ps, 4 + 3 + tt))
            xT_copies(3)
            experts(1)
            layer_norm(3, lambda tt: dve.wait_ge(moe_ps, 2))


_INS = ["x", "attn_w_in", "attn_w_out", "attn_lambda", "attn_subln", "hgrn_w_in", "hgrn_w_out",
        "hgrn_lower_bounds", "hgrn_norm", "moe_router", "moe_router_bias", "moe_w_gate_up", "moe_w_down",
        "shared_w_gate_up", "shared_w_down", "ln_gain", "ln_bias"]


def kernel(**inputs):
    import concourse.bacc as bacc
    from concourse.bass_utils import run_bass_kernel_spmd

    nc = bacc.Bacc("TRN2", target_bir_lowering=False, num_devices=1)
    floats, masks = constants()
    arrays = {f"in_{name}": np.ascontiguousarray(inputs[name]) for name in _INS}
    arrays["in_constants"], arrays["in_level_masks"] = floats, masks
    args = [nc.dram_tensor(name, a.shape, mybir.dt.from_np(a.dtype), kind="ExternalInput").ap() for name, a in arrays.items()]
    out = nc.dram_tensor("out", (1, SEQ, D), F32, kind="ExternalOutput").ap()
    build_trunk(nc, *args, out)
    return run_bass_kernel_spmd(nc, [arrays], core_ids=[0]).results[0]["out"]
```

```python
import math
from contextlib import ExitStack

import numpy as np

import concourse.bass as bass
from concourse import mybir

ALU = mybir.AluOpType
ACT = mybir.ActivationFunctionType
AX = mybir.AxisListType.X
F32 = mybir.dt.float32
F32R = mybir.dt.float32r
I32 = mybir.dt.int32

P = 128
SEQ, D = 256, 1024
TT = SEQ // P
J = D // P
DEPTH = 2
CHUNK = 64
BANK = 512
HALVES = D // BANK
HEADS = 8
SUB = 64
ROT = SUB // 4
RH = ROT // 2
ROPE_THETA = 500000.0
NE, NG, TOPG, TOPK = 64, 8, 4, 8
GE = NE // NG
FF = D // 4
FT = FF // P
SLOTS = 64
PAIRS = NE // 2
BLOCKS = SEQ // SLOTS
EXTRA = NE * (BLOCKS - 1)
OVF = SEQ * TOPK // SLOTS
ROUTED_SCALE = 2.5
ALPHA = (2 * DEPTH) ** 0.25
EPS = 1e-5
BIG = 3.0e38
FORGET_MIN = 1e-19
LEVELS = [128, 64, 32, 16, 8, 4, 2, 1]
NO_SLOT = 999.0
LAMBDA_INIT = 0.8 - 0.6 * math.exp(-0.3 * 0)

CONST_WIDTHS = dict(ident=P, before=P, ones=P, cos=TT * RH, sin=TT * RH, amask=P + SEQ,
                    iota=BLOCKS * SLOTS, lower=NG * NG, row=1, ovf_e=EXTRA, ovf_b=EXTRA, eps=1)
CONST_AT, _at = {}, 0
for _name, _width in CONST_WIDTHS.items():
    CONST_AT[_name] = (_at, _at + _width)
    _at += _width
CONSTS = _at
COMPACT = [m for m in LEVELS if m < 32] + [0]


def constants():
    c = np.zeros((P, CONSTS), np.float32)

    def put(name, value):
        a, b = CONST_AT[name]
        c[:, a:b] = value

    t = np.arange(P)
    put("ident", np.eye(P))
    put("before", t[:, None] < t[None, :])
    put("ones", 1.0)
    freq = np.float32(ROPE_THETA) ** (-np.arange(0, ROT, 2, dtype=np.float32) / np.float32(ROT))
    angle = np.arange(SEQ, dtype=np.float32)[:, None] * freq[None, :].astype(np.float32)
    for name, f in (("cos", np.cos), ("sin", np.sin)):
        put(name, f(angle).astype(np.float32).reshape(TT, P, RH).transpose(1, 0, 2).reshape(P, -1))
    am = np.zeros((P, P + SEQ), np.float32)
    q_chunk = t[:, None] // CHUNK
    am[:, :P] = np.where(t[None, :] // CHUNK <= q_chunk, 0, -1e30)
    am[:, P:] = np.where(np.arange(SEQ)[None, :] // CHUNK <= q_chunk + P // CHUNK, 0, -1e30)
    put("amask", am)
    put("iota", (np.arange(BLOCKS * SLOTS) - NO_SLOT)[None, :])
    g = np.arange(NG)
    put("lower", (g[None, :] < g[:, None]).reshape(1, -1))
    put("row", t[:, None])
    k = np.arange(EXTRA)
    put("ovf_e", (k % NE)[None, :])
    put("ovf_b", (k // NE + 1)[None, :])
    put("eps", EPS)
    masks = np.zeros((P, len(COMPACT), 32), np.int32)
    s, q = (t % 32)[:, None], np.arange(32)[None, :]
    for i, m in enumerate(COMPACT):
        masks[:, i] = (s == q) if m == 0 else (s // (2 * m) == q // (2 * m)) & (s % (2 * m) < m) & (q % (2 * m) >= m)
    return c, masks.reshape(P, -1)


ITEMS = []
for _layer, _chunks in ((0, 6), (1, 8)):
    ITEMS += [("in", _layer, c) for c in range(_chunks)]
    ITEMS += [("out", _layer, c) for c in range(HALVES)]
    ITEMS += [("ln", _layer, 0), ("sgu", _layer, 0), ("sdn", _layer, 0), ("ln", _layer, 1)]
ITEM = {item: k for k, item in enumerate(ITEMS)}
ATTN_COLUMNS = [0, 1024, 2048, 512, 1536, 2560]
HGRN_COLUMNS = [1024, 1536, 0, 512, 2048, 2560, 3072, 3584]


TURN_BANK = [4, 5, 4, 5, 0, 1, 2, 3]


def unit_bank(n):
    return n % 4 if n < 4 or n >= 12 else 6 + n % 2


def level_bank(i):
    return [4, 6, 4, 5, 6, 7, 4, 5, 6][i]


def build_trunk(nc, x_in, attn_w_in, attn_w_out, attn_lambda, attn_subln, hgrn_w_in, hgrn_w_out,
                hgrn_lower_bounds, hgrn_norm, moe_router, moe_router_bias, moe_w_gate_up, moe_w_down,
                shared_w_gate_up, shared_w_down, ln_gain, ln_bias, consts, level_masks, out):
    ctx = ExitStack()

    def sb(name, shape, dt=F32):
        return ctx.enter_context(nc.sbuf_tensor(name, shape, dt))

    def sem(name):
        return ctx.enter_context(nc.semaphore(name))

    with ctx:
        cst = sb("cst", [P, CONSTS])
        masks = sb("masks", [P, len(COMPACT) * 32], I32)
        x = sb("x", [P, TT, D])
        xT = sb("xT", [P, J, SEQ])
        w_gu = sb("w_gu", [P, 2, J * 2 * FF])
        w_dn = sb("w_dn", [P, 2, FT * D])
        odd = sb("odd", [P, 2 * (J * 2 * FF + FT * D)])
        stream = sb("stream", [P, 2, J * BANK])
        x_hi = sb("x_hi", [P, TT, J, P], F32R)
        x_lo = sb("x_lo", [P, TT, J, P], F32R)
        pick = sb("pick", [P, 2, TT, P], F32R)
        place = sb("place", [P, 2, SEQ], F32R)
        y_hi = sb("y_hi", [P, HALVES, BANK], F32R)
        y_lo = sb("y_lo", [P, HALVES, BANK], F32R)
        work = sb("work", [P, 6144])
        w_router = sb("w_router", [P, J, NE])
        bias_row = sb("bias_row", [P, NE])
        small = sb("small", [P, 256])
        ovf_list = sb("ovf_list", [1, 1 + 2 * OVF], I32)
        ps = ctx.enter_context(nc.psum_tensor("ps", [P, 8, BANK], F32))

        def const(name, width=None):
            a, b = CONST_AT[name]
            return cst[:, a:b]

        ident = const("ident")
        GU, DN = J * 2 * FF, FT * D

        def gate_up_of(slot):
            w = w_gu[:, slot, :] if slot < 2 else odd[:, (slot - 2) * GU:(slot - 1) * GU]
            return w

        def down_of(slot):
            return w_dn[:, slot, :] if slot < 2 else odd[:, 2 * GU + (slot - 2) * DN:2 * GU + (slot - 1) * DN]

        def part(tensor, at, *shape):
            v = tensor[:, at:at + int(np.prod(shape))]
            names = "abcd"[:len(shape)]
            return v.rearrange(f"p ({' '.join(names)}) -> p {' '.join(names)}", **dict(zip(names, shape))) if len(shape) > 1 else v

        qkv = part(odd, 0, 3, TT, D)
        q_tok, k_tok, v_tok = qkv[:, 0], qkv[:, 1], qkv[:, 2]
        a_qT, a_kT = part(odd, 6144, HEADS, SEQ), part(odd, 8192, HEADS, SEQ)
        a_o = q_tok
        probs = part(work, 1536, 2, 2, P + SEQ)
        mask_r, ident_r = y_hi[:, 0, 0:P + SEQ], y_hi[:, 1, 0:P]
        diff = part(work, 3072, 2, P + SEQ)
        diffT = part(work, 3840, 2, P + SEQ)
        oT = part(odd, 6144, HEADS, SEQ)
        h_b, h_qT, h_kT = (part(odd, 2048 * i, HEADS, SEQ) for i in (0, 3, 1))
        h_A = [part(odd, 2048 * i, HEADS, SEQ) for i in (2, 4)]
        scoreT = part(odd, 10240, HEADS * TT, P)
        h_o = h_A[0].rearrange("p h t -> p (h t)").rearrange("p (a n) -> p a n", a=TT)
        h_v, h_gate = part(work, 0, TT, D), part(work, 2048, TT, D)
        cross, compact = part(work, 4096, HEADS, P), part(work, 5120, HEADS * TT, 32)
        xg = part(work, 0, 2, J, P)
        sh_hidT = part(work, 5632, FT * SEQ)
        silu, hid, hidT = part(work, 2048, 2, FF), part(work, 2560, 2, FF), part(work, 3072, 2, FT, P)
        R0 = 3584
        score, choice, kept, replaced = (part(work, R0 + 128 * i, TT, NE) for i in range(4))
        chosen, gate, slot = (part(work, R0 + 128 * i, TT, NE) for i in range(4, 7))
        best8 = part(work, R0 + 896, TT * NG, 8)
        rank4 = part(work, R0 + 1024, TT * NG, NG)
        tie4 = part(work, R0 + 1152, TT * NG, NG)
        flags, flags_sum = part(work, R0 + 1280, EXTRA), part(work, R0 + 1472, EXTRA)
        listed, listed_id = part(work, R0 + 1664, EXTRA), part(work, R0 + 1856, EXTRA)
        (g_sum, g_rank, g_pen) = (small[:, 16 * i:16 * i + 16] for i in range(3))
        top8 = part(small, 48, TT, 8)
        w_sum = small[:, 64:66]
        gate_slot = part(small, 66, 2)
        ovf_cols = small[:, 68:70]
        stats = part(small, 203, TT, HALVES, 6)
        mean_var = part(small, 227, TT, 2)
        rstd, eps_var = part(small, 231, TT), part(small, 233, TT)
        row_max = part(small, 88, 2, 4)
        row_sum = part(small, 96, 2, 4)
        row_scale = part(small, 104, 4)
        neg_lam = small[:, 108:109]
        o_sq = small[:, 110:126]
        o_rs = small[:, 126:142]
        head_gain = small[:, 142:143]
        lam2 = small[:, 144:146]
        lb_e = part(small, 146, 2, HEADS)
        lb_rest = small[:, 162:170]
        lb_low = small[:, 170:178]
        c01 = part(small, 178, HEADS, 1)
        lb_sum = small[:, 186:194]
        lb_max = small[:, 194:202]
        norm_h = small[:, 202:203]

        lam_row = part(work, 4608, 4, SUB)
        lam_prod = part(work, 4864, 2, SUB)
        lb_raw = work[:, 5120:5120 + P]

        const_in, x_loaded, vec_in = sem("const_in"), sem("x_loaded"), sem("vec_in")
        router_in, bias_in = sem("router_in"), sem("bias_in")
        stream_in = [sem("stream_in0"), sem("stream_in1")]
        gu_in = [sem(f"gu_in{s}") for s in range(4)]
        dn_in = [sem(f"dn_in{s}") for s in range(4)]
        out_stored = sem("out_stored")
        x_ready, x_split = sem("x_ready"), sem("x_split")
        xT_ps, xT_act, xT_dve = sem("xT_ps"), sem("xT_act"), sem("xT_dve")
        proj_ps, proj_ev = sem("proj_ps"), sem("proj_ev")
        rope_ok, turn_ps, turn_act, turn_dve = sem("rope_ok"), sem("turn_ps"), sem("turn_act"), sem("turn_dve")
        sc_ps, nmax_ok, probs_ok, diff_ok = sem("sc_ps"), sem("nmax_ok"), sem("probs_ok"), sem("diff_ok")
        dT_ps, dT_ev, pv_ps, o_ev = sem("dT_ps"), sem("dT_ev"), sem("pv_ps"), sem("o_ev")
        lam_a, lam_b, lam_ok = sem("lam_a"), sem("lam_b"), sem("lam_ok")
        ms_ok, root_ok, on_ok = sem("ms_ok"), sem("root_ok"), sem("on_ok")
        oT_ps, oT_ev, outp_ps = sem("oT_ps"), sem("oT_ev"), sem("outp_ps")
        ln_var, ln_std = sem("ln_var"), sem("ln_std")
        xhi_ok = sem("xhi_ok")
        lb_ps, lb_exp_in, lb_exp_ok = sem("lb_ps"), sem("lb_exp_in"), sem("lb_exp_ok")
        forget_ok, logf_ok = sem("forget_ok"), sem("logf_ok")
        expo_ok, exp_ok, lev_ok, lev_ps = sem("expo_ok"), sem("exp_ok"), sem("lev_ok"), sem("lev_ps")
        lev_act, lev_dve, scores_ok, ho_ps = sem("lev_act"), sem("lev_dve"), sem("scores_ok"), sem("ho_ps")
        logit_ps, score_ok, chosen_ok, pos_ps, route_ok = sem("logit_ps"), sem("score_ok"), sem("chosen_ok"), sem("pos_ps"), sem("route_ok")
        ovf_cols_ok, ovf_row_ps, ovf_ok = sem("ovf_cols_ok"), sem("ovf_row_ps"), sem("ovf_ok")
        sh_ps, sh_silu, sh_hid, shT_ps, shT_ev = sem("sh_ps"), sem("sh_silu"), sem("sh_hid"), sem("shT_ps"), sem("shT_ev")
        pick_ok, xg_ps, xg_ev, gu_ps = sem("pick_ok"), sem("xg_ps"), sem("xg_ev"), sem("gu_ps")
        silu_ok, hid_ok, hidT_ps, hidT_ev = sem("silu_ok"), sem("hid_ok"), sem("hidT_ps"), sem("hidT_ev")
        dn_ps, yhi_ok, ylo_ok, moe_ps = sem("dn_ps"), sem("yhi_ok"), sem("ylo_ok"), sem("moe_ps")
        sdn_ps = sem("sdn_ps")
        mask_ok = sem("mask_ok")
        scores_clear, sq_ok = sem("scores_clear"), sem("sq_ok")
        dve_chain, act_chain = sem("dve_chain"), sem("act_chain")
        OV = [{n: sem(f"o{layer}_{n}") for n in ("gu_in", "dn_in", "pick", "xps", "xev", "gups", "silu", "hid", "tps", "tev", "dps", "yhi", "ylo", "done")}
              for layer in range(DEPTH)]

        block = ctx.enter_context(nc.Block())

        def rows(w):
            return w.rearrange("(p j) n -> p j n", j=J)

        def expert_gu(layer, e):
            w = moe_w_gate_up[layer]
            w = w[e] if isinstance(e, int) else w[bass.ds(e, 1)].rearrange("a d n -> (a d) n")
            return w.rearrange("(p j) n -> p (j n)", j=J)

        def expert_dn(layer, e):
            w = moe_w_down[layer]
            w = w[e] if isinstance(e, int) else w[bass.ds(e, 1)].rearrange("a d n -> (a d) n")
            return w.rearrange("(p j) n -> p (j n)", j=FT)

        def last_use(k):
            name, layer, c = ITEMS[k]
            return {"in": (proj_ps, 12 * layer + 2 * c + 2), "out": (outp_ps, 4 * layer + 2 * c + 2),
                    "ln": (x_ready, 4 * layer + 2 * c + 2), "sgu": (sh_ps, TT * (layer + 1)), "sdn": (sdn_ps, layer + 1)}[name]

        @block.sync
        def _(sp):
            def load_item(k):
                name, layer, c = ITEMS[k]
                if k >= 2:
                    sp.wait_ge(*last_use(k - 2))
                buf = stream[:, k % 2, :]
                if name == "in":
                    w, col = (attn_w_in, ATTN_COLUMNS[c]) if layer == 0 else (hgrn_w_in, HGRN_COLUMNS[c])
                    dst, src = buf.rearrange("p (j n) -> p j n", j=J), rows(w[0])[:, :, col:col + BANK]
                elif name == "out":
                    w = attn_w_out if layer == 0 else hgrn_w_out
                    dst = buf.rearrange("p (h n) -> p h n", h=HEADS)
                    src = w[0].rearrange("(h p) n -> p h n", p=P)[:, :, c * BANK:(c + 1) * BANK]
                elif name == "ln":
                    for i, v in enumerate((ln_gain, ln_bias)):
                        sp.dma_start(buf[:, i * D:(i + 1) * D], v[layer, c:c + 1, :].broadcast_to([P, D])).then_inc(stream_in[k % 2], 16)
                    return
                elif name == "sgu":
                    dst, src = buf, shared_w_gate_up[layer].rearrange("(p j) n -> p (j n)", j=J)
                else:
                    dst, src = buf[:, 0:DN], shared_w_down[layer].rearrange("(p j) n -> p (j n)", j=FT)
                sp.dma_start(dst, src).then_inc(stream_in[k % 2], 16)

            def load_pair(layer, p, e, u):
                g = layer * PAIRS + p
                if not isinstance(g, int) or g >= 2:
                    sp.wait_ge(gu_ps, g - 1)
                for i in range(2):
                    sp.dma_start(gate_up_of(2 * u + i), expert_gu(layer, e + i)).then_inc(gu_in[2 * u + i], 16)
                if not isinstance(g, int) or g >= 2:
                    sp.wait_ge(dn_ps, 2 * g - 2)
                for i in range(2):
                    sp.dma_start(down_of(2 * u + i), expert_dn(layer, e + i)).then_inc(dn_in[2 * u + i], 16)

            sp.dma_start(cst[:], consts).then_inc(const_in, 16)
            sp.dma_start(masks[:], level_masks).then_inc(const_in, 16)
            for tt in range(TT):
                sp.dma_start(x[:, tt, :], x_in[0, tt * P:(tt + 1) * P, :]).then_inc(x_loaded, 16)
            sp.dma_start(lam_row, attn_lambda.rearrange("a l s -> a (l s)").broadcast_to([P, 4 * SUB]).rearrange("p (l s) -> p l s", l=4)).then_inc(vec_in, 16)
            sp.dma_start(head_gain, attn_subln.rearrange("a n -> n a")).then_inc(vec_in, 16)
            sp.dma_start(norm_h, hgrn_norm.rearrange("a n -> n a")).then_inc(vec_in, 16)
            sp.dma_start(lb_raw[0:DEPTH * HEADS, :], hgrn_lower_bounds.rearrange("a (h p) -> (a h) p", p=P)).then_inc(vec_in, 16)
            load_item(0)
            load_item(1)
            k = 2
            for layer in range(DEPTH):
                if layer == 1:
                    sp.wait_ge(moe_ps, layer)
                    sp.wait_ge(route_ok, layer)
                sp.dma_start(w_router[:], rows(moe_router[layer])).then_inc(router_in, 16)
                sp.dma_start(bias_row[:], moe_router_bias[layer:layer + 1, :].broadcast_to([P, NE])).then_inc(bias_in, 16)
                prefetch_at = k + 3
                while ITEMS[k] != ("ln", layer, 1):
                    if k == prefetch_at:
                        load_pair(layer, 0, 0, 0)
                    if ITEMS[k] == ("sgu", layer, 0):
                        load_item(k)
                        k += 1
                        load_item(k)
                        k += 1
                        sp.wait_ge(x_ready, 4 * layer + 2)
                        load_pair(layer, 1, 2, 1)
                        continue
                    load_item(k)
                    k += 1
                load_item(k)
                k += 1
                with sp.Fori(1, PAIRS // 2) as it:
                    for u in range(2):
                        load_pair(layer, it * 2 + u, it * 4 + 2 * u, u)
                s = OV[layer]
                sp.wait_ge(ovf_ok, layer + 1)
                n = sp.value_load(ovf_list[0:1, 0:1], min_val=0, max_val=OVF - 1)
                with sp.If(n > 0):
                    sp.wait_ge(dn_ps, 2 * PAIRS * (layer + 1))
                    with sp.Fori(0, n) as i:
                        e = sp.value_load(ovf_list[0:1, bass.ds(i + 1, 1)], min_val=0, max_val=NE - 1)
                        sp.wait_ge(s["done"], i + 1)
                        sp.dma_start(gate_up_of(0), expert_gu(layer, e)).then_inc(s["gu_in"], 16)
                        sp.dma_start(down_of(0), expert_dn(layer, e)).then_inc(s["dn_in"], 16)
                with sp.Else():
                    sp.nop()
                if layer == 0:
                    load_item(k)
                    k += 1
            for tt in range(TT):
                sp.wait_ge(x_ready, 4 * (DEPTH - 1) + 3 + tt)
                sp.dma_start(out[0, tt * P:(tt + 1) * P, :], x[:, tt, :]).then_inc(out_stored, 16)
            sp.wait_ge(out_stored, 16 * TT)

        @block.tensor
        def _(pe):
            def item(name, layer, c):
                k = ITEM[name, layer, c]
                n = sum(2 if ITEMS[i][0] == "ln" else 1 for i in range(k % 2, k + 1, 2))
                pe.wait_ge(stream_in[k % 2], 16 * n)
                return stream[:, k % 2, :]

            def turn_x(b):
                for tt in range(TT):
                    if b == 0:
                        pe.wait_ge(x_loaded, 16 * TT)
                    else:
                        pe.wait_ge(x_ready, 2 * (b - 1) + tt + 1)
                    for j in range(J):
                        t = pe.transpose(ps[:, 2 * tt + j // 4, (j % 4) * P:(j % 4 + 1) * P],
                                         x[:, tt, j:D:J], ident)
                    t.then_inc(xT_ps, 1)

            def xT_wait(b):
                pe.wait_ge(xT_act, 2 * b + 2)
                pe.wait_ge(xT_dve, 2 * b + 2)

            def rows_unit(w, tt, n):
                if n >= 4:
                    pe.wait_ge(proj_ev, n - 3 if n >= 12 else max(n - 1, 4))
                for j in range(J):
                    t = pe.matmul(ps[:, unit_bank(n), :], xT[:, j, tt * P:(tt + 1) * P], w[:, j, :],
                                  start=(j == 0), stop=(j == J - 1))
                t.then_inc(proj_ps, 1)
                return t

            def columns_unit(w, half, n):
                pe.wait_ge(proj_ev, n - 3)
                for i in range(2):
                    for j in range(J):
                        c = (2 * half + i) * P
                        t = pe.matmul(ps[:, n % 4, i * SEQ:(i + 1) * SEQ], w[:, j, c:c + P], xT[:, j, :],
                                      start=(j == 0), stop=(j == J - 1))
                t.then_inc(proj_ps, 1)
                return t

            def turn_heads(o, tt, hh, bank):
                for i in range(4):
                    h = 4 * hh + i
                    t = pe.transpose(ps[:, bank, i * P:(i + 1) * P], o[:, tt, h * P:(h + 1) * P], ident)
                t.then_inc(oT_ps, 1)

            def out_unit(layer, c, tt, heads):
                w = item("out", layer, c).rearrange("p (h n) -> p h n", h=HEADS)
                for h in heads:
                    t = pe.matmul(ps[:, tt * HALVES + c, :], oT[:, h, tt * P:(tt + 1) * P], w[:, h, :],
                                  start=(h == 0), stop=(h == HEADS - 1))
                if heads[-1] == HEADS - 1:
                    t.then_inc(outp_ps, 1)

            pe.wait_ge(const_in, 32)
            turn_x(0)
            pe.wait_ge(vec_in, 64)
            pe.transpose(ps[:, 6, 0:DEPTH * HEADS], lb_raw[0:DEPTH * HEADS, :], ident[0:DEPTH * HEADS, 0:DEPTH * HEADS])\
              .then_inc(lb_ps, 1)
            xT_wait(0)

            def unit(n):
                rows_unit(item("in", 0, n // 2).rearrange("p (j n) -> p j n", j=J), n % 2, n)

            def turn(r):
                group, src = r // 4, (q_tok if r % 4 < 2 else k_tok)
                pe.wait_ge(rope_ok, r // 2 + 1)
                if r in (2, 3):
                    pe.wait_ge(turn_act if r == 2 else turn_dve, 1)
                if r == 4:
                    pe.wait_ge(probs_ok, 4)
                for i in range(2):
                    for tt in range(TT):
                        h = 4 * group + 2 * (r % 2) + i
                        t = pe.transpose(ps[:, TURN_BANK[r], (i * TT + tt) * P:(i * TT + tt + 1) * P],
                                         src[:, tt, h * P:(h + 1) * P], ident)
                t.then_inc(turn_ps, 1)

            def scores(h):
                if h in (0, 4):
                    pe.wait_ge(turn_act, 2 + h // 2)
                    pe.wait_ge(turn_dve, 2 + h // 2)
                if h == 0:
                    pe.wait_ge(proj_ev, 4)
                    pe.wait_ge(mask_ok, 2)
                if h >= 2:
                    pe.wait_ge(probs_ok, h - 1)
                for m in range(2):
                    rows_m = slice(m * SUB, (m + 1) * SUB)
                    b = 2 * (h % 2) + m
                    pe.matmul(ps[:, b, 0:P + SEQ], ident_r, mask_r, start=True, stop=False, skip_group_check=True)
                    pe.matmul(ps[:, b, 0:P], a_qT[rows_m, h, 0:P], a_kT[rows_m, h, 0:P], start=False, stop=True,
                              skip_group_check=True)
                    t = pe.matmul(ps[:, b, P:P + SEQ], a_qT[rows_m, h, P:SEQ], a_kT[rows_m, h, :],
                                  start=False, stop=True, skip_group_check=True)
                t.then_inc(sc_ps, 1)

            def turn_diff(h):
                pe.wait_ge(diff_ok, h + 1)
                if h:
                    pe.wait_ge(dT_ev, h)
                for i in range(3):
                    t = pe.transpose(ps[:, 4, i * P:(i + 1) * P], diff[:, h % 2, i * P:(i + 1) * P], ident)
                t.then_inc(dT_ps, 1)

            def values(h):
                pe.wait_ge(dT_ev, h + 1)
                pe.wait_ge(proj_ev, 6 if h < 4 else 12)
                if h >= 2:
                    pe.wait_ge(o_ev, h - 1)
                v, dT, a = v_tok[:, :, h * P:(h + 1) * P], diffT[:, h % 2, :], SEQ * (h % 2)
                pe.matmul(ps[:, 5, a:a + P], dT[:, 0:P], v[:, 0, :], start=True, stop=True)
                pe.matmul(ps[:, 5, a + P:a + SEQ], dT[:, P:2 * P], v[:, 0, :], start=True, stop=False)
                pe.matmul(ps[:, 5, a + P:a + SEQ], dT[:, 2 * P:3 * P], v[:, 1, :], start=False, stop=True)\
                  .then_inc(pv_ps, 1)

            for n in range(4):
                unit(n)
            turn(0)
            turn(1)
            unit(4)
            turn(2)
            turn(3)
            scores(0)
            scores(1)
            for h in range(3):
                unit(5 + h)
                turn_diff(h)
                if h < 2:
                    scores(h + 2)
                values(h)
            unit(8)
            turn(4)
            turn(5)
            unit(9)
            turn_diff(3)
            values(3)
            turn(6)
            turn(7)
            scores(4)
            scores(5)
            unit(10)
            turn_diff(4)
            scores(6)
            unit(11)
            values(4)
            turn_diff(5)
            scores(7)
            values(5)
            pe.wait_ge(on_ok, 1)
            pe.wait_ge(proj_ev, 12)
            for tt in range(TT):
                turn_heads(a_o, tt, 0, 6 + tt)
            turn_diff(6)
            values(6)
            pe.wait_ge(probs_ok, HEADS)
            pe.wait_ge(oT_ev, 2)
            out_unit(0, 0, 0, range(4))
            turn_diff(7)
            out_unit(0, 0, 1, range(4))
            values(7)
            for tt in range(TT):
                out_unit(0, 1, tt, range(4))
            pe.wait_ge(on_ok, 2)
            for tt in range(TT):
                turn_heads(a_o, tt, 1, 6 + tt)
            for c in range(HALVES):
                for tt in range(TT):
                    pe.wait_ge(oT_ev, 3 + tt)
                    out_unit(0, c, tt, range(4, HEADS))

            def gather(g, u, r, first=False):
                if r == 0:
                    pe.wait_ge(pick_ok, g + 1)
                if not first:
                    pe.wait_ge(xg_ev, 3 * g + r)
                for i in range(4):
                    j = 4 * r + i
                    for n, (tt, half) in enumerate([(tt, half) for tt in range(TT) for half in (x_hi, x_lo)]):
                        t = pe.matmul(ps[:, 4, i * P:(i + 1) * P], half[:, tt, j, :], pick[:, u, tt, :],
                                      start=(n == 0), stop=(n == 3))
                t.then_inc(xg_ps, 1)

            def turn_pick(g, u, gates):
                pe.wait_ge(xg_ev, 3 * g + 2)
                for tt in range(TT):
                    pe.transpose(ps[:, 4, tt * P:(tt + 1) * P], pick[:, u, tt, :].bitcast(F32), ident)
                for tt in range(TT):
                    t = pe.matmul(ps[:, 4, SEQ:SEQ + 2], pick[:, u, tt, :].bitcast(F32), gates(tt),
                                  start=(tt == 0), stop=(tt == TT - 1))
                t.then_inc(xg_ps, 1)

            def gate_up(g, u, turn):
                pe.wait_ge(xg_ev, 3 * g + 2)
                for i in range(2):
                    pe.wait_ge(gu_in[2 * u + i], turn)
                for j in range(J):
                    for i in range(2):
                        a, b = i * SLOTS, (i + 1) * SLOTS
                        t = pe.matmul(ps[a:b, 5, :], xg[:, u, j, a:b],
                                      gate_up_of(2 * u + i)[:, j * BANK:(j + 1) * BANK],
                                      start=(j == 0), stop=(j == J - 1))
                t.then_inc(gu_ps, 1)

            def turn_hidden(g, u, layer, first):
                pe.wait_ge(hid_ok, g + 1)
                if first:
                    pe.wait_ge(shT_ev, layer + 1)
                for f in range(FT):
                    t = pe.transpose(ps[:, 6, f * P:(f + 1) * P], hid[:, u, f:FF:FT], ident)
                t.then_inc(hidT_ps, 1)

            def down(g, u, half, turn):
                if half == 0:
                    pe.wait_ge(hidT_ev, g + 1)
                    for i in range(2):
                        pe.wait_ge(dn_in[2 * u + i], turn)
                for f in range(FT):
                    for i in range(2):
                        a, b = i * SLOTS, (i + 1) * SLOTS
                        at = f * D + half * BANK
                        t = pe.matmul(ps[a:b, 5 + 2 * half, :], hidT[:, u, f, a:b],
                                      down_of(2 * u + i)[:, at:at + BANK], start=(f == 0), stop=(f == FT - 1))
                t.then_inc(dn_ps, 1)

            def scatter(g, u, half, last=False):
                pe.wait_ge(ylo_ok, 2 * g + half + 1)
                if half == 0:
                    pe.wait_ge(xg_ev, 3 * g + 3)
                for tt in range(TT):
                    for y in (y_hi, y_lo):
                        pe.matmul(ps[:, tt * HALVES + half, :], place[:, u, tt * P:(tt + 1) * P], y[:, half, :],
                                  start=False, stop=last and y is y_lo, skip_group_check=True)

            def experts(layer):
                xT_wait(2 * layer + 1)
                pe.wait_ge(router_in, 16 * (layer + 1))
                for tt in range(TT):
                    for j in range(J):
                        t = pe.matmul(ps[:, 4, tt * NE:(tt + 1) * NE], xT[:, j, tt * P:(tt + 1) * P], w_router[:, j, :],
                                      start=(j == 0), stop=(j == J - 1))
                t.then_inc(logit_ps, 1)
                w = item("sgu", layer, 0)
                for tt in range(TT):
                    for j in range(J):
                        t = pe.matmul(ps[:, 5 + 2 * tt, :], xT[:, j, tt * P:(tt + 1) * P], w[:, j * BANK:(j + 1) * BANK],
                                      start=(j == 0), stop=(j == J - 1))
                    t.then_inc(sh_ps, 1)
                pe.wait_ge(chosen_ok, layer + 1)
                pos, before, ones = ps[:, 0, 0:P], const("before"), const("ones")
                pe.matmul(pos[:, 0:NE], before, chosen[:, 0, :], start=True, stop=True)
                pe.matmul(pos[:, NE:2 * NE], ones, chosen[:, 0, :], start=True, stop=False)
                pe.matmul(pos[:, NE:2 * NE], before, chosen[:, 1, :], start=False, stop=True)
                count = ps[:, 0, P:P + NE]
                pe.matmul(count, ones, chosen[:, 0, :], start=True, stop=False)
                pe.matmul(count, ones, chosen[:, 1, :], start=False, stop=True).then_inc(pos_ps, 1)
                pe.wait_ge(x_split, TT * (layer + 1))
                base = layer * PAIRS

                def turn_shared():
                    for tt in range(TT):
                        pe.wait_ge(sh_hid, TT * layer + tt + 1)
                        for f in range(FT):
                            t = pe.transpose(ps[:, 6, f * SEQ + tt * P:f * SEQ + (tt + 1) * P], hid[:, tt, f:FF:FT], ident)
                    t.then_inc(shT_ps, 1)

                def turn_list():
                    pe.wait_ge(ovf_cols_ok, layer + 1)
                    for i in range(2):
                        a = P + NE + i * OVF
                        t = pe.matmul(ps[0:1, 0, a:a + OVF], ovf_cols[:, i:i + 1], ident[:, 0:OVF], start=True, stop=True)
                    t.then_inc(ovf_row_ps, 1)

                def shared_down():
                    pe.wait_ge(shT_ev, layer + 1)
                    pe.wait_ge(ovf_ok, layer + 1)
                    w = item("sdn", layer, 0)
                    for tt in range(TT):
                        for half in range(HALVES):
                            for f in range(FT):
                                t = pe.matmul(ps[:, tt * HALVES + half, :], sh_hidT[:, f * SEQ + tt * P:f * SEQ + (tt + 1) * P],
                                              w[:, f * D + half * BANK:f * D + (half + 1) * BANK],
                                              start=(f == 0), stop=False, skip_group_check=True)
                    t.then_inc(sdn_ps, 1)

                def gates(e):
                    return lambda tt: gate[:, tt, e:e + 2] if isinstance(e, int) else gate[:, tt, bass.ds(e, 2)]

                def step(p, e, u, turn, last=False, first=False):
                    g = base + p
                    gate_up(g, u, turn)
                    if not last:
                        gather(g + 1, 1 - u, 0)
                    if first:
                        turn_list()
                    else:
                        scatter(g - 1, 1 - u, 1)
                    turn_hidden(g, u, layer, first)
                    if not last:
                        gather(g + 1, 1 - u, 1)
                    down(g, u, 0, turn)
                    down(g, u, 1, turn)
                    if not last:
                        turn_pick(g + 1, 1 - u, gates(e + 2))
                    if first:
                        shared_down()
                    scatter(g, u, 0, last)

                first_turn = 16 * (PAIRS // 2) * layer
                gather(base, 0, 0, first=(layer == 0))
                gather(base, 0, 1)
                turn_pick(base, 0, gates(0))
                turn_shared()
                for p in range(2):
                    step(p, 2 * p, p % 2, first_turn + 16, first=(p == 0))
                with pe.Fori(1, PAIRS // 2 - 1) as it:
                    for u in range(2):
                        step(it * 2 + u, it * 4 + 2 * u, u, it * 16 + (first_turn + 16))
                for p in range(PAIRS - 2, PAIRS):
                    step(p, 2 * p, p % 2, first_turn + 16 * (p // 2 + 1), last=(p == PAIRS - 1))
                scatter(base + PAIRS - 1, 1, 1, last=True)

                s = OV[layer]
                n = pe.value_load(ovf_list[0:1, 0:1], min_val=0, max_val=OVF - 1)
                with pe.If(n > 0):
                    pe.drain().then_inc(s["done"], 1)
                    with pe.Fori(0, n) as i:
                        e = pe.value_load(ovf_list[0:1, bass.ds(i + 1, 1)], min_val=0, max_val=NE - 1)
                        pe.wait_ge(s["pick"], i + 1)
                        for r in range(2):
                            pe.wait_ge(s["xev"], i * 3 + (r + 1))
                            for c in range(4):
                                j = 4 * r + c
                                for k, (tt, half) in enumerate([(tt, half) for tt in range(TT) for half in (x_hi, x_lo)]):
                                    t = pe.matmul(ps[:, 4, c * P:(c + 1) * P], half[:, tt, j, :], pick[:, 0, tt, :],
                                                  start=(k == 0), stop=(k == 3))
                            t.then_inc(s["xps"], 1)
                        pe.wait_ge(s["xev"], i * 3 + 3)
                        for tt in range(TT):
                            pe.transpose(ps[:, 4, tt * P:(tt + 1) * P], pick[:, 0, tt, :].bitcast(F32), ident)
                        for tt in range(TT):
                            t = pe.matmul(ps[:, 4, SEQ:SEQ + 1], pick[:, 0, tt, :].bitcast(F32), gate[:, tt, bass.ds(e, 1)],
                                          start=(tt == 0), stop=(tt == TT - 1))
                        t.then_inc(s["xps"], 1)
                        pe.wait_ge(s["xev"], i * 3 + 4)
                        pe.wait_ge(s["gu_in"], i * 16 + 16)
                        for j in range(J):
                            t = pe.matmul(ps[:, 5, :], xg[:, 0, j, :], gate_up_of(0)[:, j * BANK:(j + 1) * BANK],
                                          start=(j == 0), stop=(j == J - 1))
                        t.then_inc(s["gups"], 1)
                        pe.wait_ge(s["hid"], i + 1)
                        for f in range(FT):
                            t = pe.transpose(ps[:, 6, f * P:(f + 1) * P], hid[:, 0, f:FF:FT], ident)
                        t.then_inc(s["tps"], 1)
                        pe.wait_ge(s["tev"], i + 1)
                        pe.wait_ge(s["dn_in"], i * 16 + 16)
                        for half in range(HALVES):
                            for f in range(FT):
                                at = f * D + half * BANK
                                t = pe.matmul(ps[:, 5 + 2 * half, :], hidT[:, 0, f, :], down_of(0)[:, at:at + BANK],
                                              start=(f == 0), stop=(f == FT - 1))
                        t.then_inc(s["dps"], 1)
                        pe.wait_ge(s["ylo"], i + 1)
                        for half in range(HALVES):
                            for tt in range(TT):
                                for y in (y_hi, y_lo):
                                    pe.matmul(ps[:, tt * HALVES + half, :], place[:, 0, tt * P:(tt + 1) * P], y[:, half, :],
                                              start=False, stop=(y is y_lo), skip_group_check=True)
                        pe.drain().then_inc(s["done"], 1)
                with pe.Else():
                    pe.nop()
                pe.drain().then_inc(moe_ps, 1)

            turn_x(1)
            experts(0)

            turn_x(2)
            xT_wait(2)
            n = 12
            for c in range(4):
                w = item("in", 1, c).rearrange("p (j n) -> p j n", j=J)
                for half in range(2):
                    t = columns_unit(w, half, n)
                    n += 1

            def level(i):
                m = LEVELS[i] if i < len(LEVELS) else 0
                if m:
                    pe.wait_ge(lev_ok, i + 1)
                    A = h_A[i % 2]
                bank = level_bank(i)
                if 2 <= i <= 6:
                    pe.wait_ge(lev_act, {2: 1, 3: 1, 4: 2, 5: 2, 6: 3}[i])
                if i >= 7:
                    pe.wait_ge(lev_dve, i - 6)
                if m == 128:
                    for h in range(HEADS):
                        t = pe.matmul(ps[:, 4 + h // 4, (h % 4) * P:(h % 4 + 1) * P], A[:, h, 0:P], A[:, h, P:SEQ],
                                      start=True, stop=True)
                elif m == 64:
                    for h in range(HEADS):
                        for tt in range(TT):
                            k, a = h * TT + tt, tt * P
                            t = pe.matmul(ps[0:64, 6 + k // 8, (k % 8) * 64:(k % 8 + 1) * 64], A[:, h, a:a + 64],
                                          A[:, h, a + 64:a + P], start=True, stop=True)
                else:
                    for h in range(HEADS):
                        for tt in range(TT):
                            for q in range(4):
                                if m == 32 and q % 2:
                                    continue
                                k, a = h * TT + tt, tt * P + 32 * q
                                lhs = A[:, h, a:a + 32] if m else h_kT[:, h, a:a + 32]
                                rhs = A[:, h, a + 32:a + 64] if m == 32 else A[:, h, a:a + 32] if m else h_qT[:, h, a:a + 32]
                                t = pe.matmul(ps[32 * q:32 * q + 32, bank, 32 * k:32 * k + 32], lhs, rhs,
                                              start=True, stop=True)
                t.then_inc(lev_ps, 1)

            for c in range(4, 8):
                w = item("in", 1, c).rearrange("p (j n) -> p j n", j=J)
                for tt in range(TT):
                    rows_unit(w, tt, n)
                    n += 1
                    level(n - 21)
            level(8)
            pe.wait_ge(scores_ok, 1)
            pe.wait_ge(lev_act, 3)
            pe.wait_ge(proj_ev, n)
            for tt in range(TT):
                for h in range(HEADS):
                    o = ps[:, 2 * tt + h // 4, (h % 4) * P:(h % 4 + 1) * P]
                    v = h_v[:, :, h * P:(h + 1) * P]
                    if tt == 1:
                        pe.matmul(o, cross[:, h, :], v[:, 0, :], start=True, stop=False)
                    t = pe.matmul(o, scoreT[:, h * TT + tt, :], v[:, tt, :], start=(tt == 0), stop=True)
                t.then_inc(ho_ps, 1)
            for tt in range(TT):
                pe.wait_ge(on_ok, 2 + tt + 1)
                for hh in range(2):
                    turn_heads(h_o, tt, hh, 4 + 2 * tt + hh)
            for c in range(HALVES):
                for tt in range(TT):
                    pe.wait_ge(oT_ev, 4 + 2 * tt + 2)
                    out_unit(1, c, tt, range(HEADS))
            turn_x(3)
            experts(1)

        @block.scalar
        def _(act):
            links = [0]

            def link(t):
                links[0] += 1
                t.then_inc(act_chain, 1)
                act.wait_ge(act_chain, links[0])

            def f(out_, in_, func=ACT.Copy, **kw):
                return nc.scalar.activation(out_, in_, func, **kw)

            def xT_copies(b):
                for tt in range(TT):
                    act.wait_ge(xT_ps, 2 * b + tt + 1)
                    f(xT[:, 0:4, tt * P:(tt + 1) * P], ps[:, 2 * tt, :].rearrange("p (j t) -> p j t", j=4)).then_inc(xT_act, 1)

            def out_copy(n, tt, hh, bank, gain):
                act.wait_ge(oT_ps, n + 1)
                f(oT[:, 4 * hh:4 * hh + 4, tt * P:(tt + 1) * P], ps[:, bank, :].rearrange("p (h t) -> p h t", h=4),
                  scale=gain).then_inc(oT_ev, 1)

            def layer_norm(n):
                for tt in range(TT):
                    act.wait_ge(ln_var, 2 * n + tt + 1)
                    f(rstd[:, tt:tt + 1], eps_var[:, tt:tt + 1], ACT.Sqrt).then_inc(ln_std, 1)

            def split_x(n):
                for tt in range(TT):
                    act.wait_ge(x_ready, 2 * n + tt + 1)
                    f(x_hi[:, tt, :, :], x[:, tt, :].rearrange("t (p j) -> t j p", j=J)).then_inc(xhi_ok, 1)

            xT_copies(0)
            act.wait_ge(lam_a, 1)
            f(lam2, lam2, ACT.Exp).then_inc(lam_b, 1)
            act.wait_ge(lb_exp_in, 1)
            f(lb_e, lb_e, ACT.Exp).then_inc(lb_exp_ok, 1)

            def project(n):
                c, tt = n // 2, n % 2
                act.wait_ge(proj_ps, n + 1)
                f(qkv[:, c % 3, tt, (c // 3) * BANK:(c // 3 + 1) * BANK], ps[:, unit_bank(n), :]).then_inc(proj_ev, 1)

            def turned(r):
                act.wait_ge(turn_ps, r + 1)
                h = 4 * (r // 4)
                dst = a_qT if r % 4 < 2 else a_kT
                f(dst[:, h:h + 2, :], ps[:, TURN_BANK[r], :].rearrange("p (h t) -> p h t", h=2)).then_inc(turn_act, 1)

            def soften(h):
                act.wait_ge(nmax_ok, h + 1)
                for i, (tile, m) in enumerate(((0, 0), (0, 1), (1, 0), (1, 1))):
                    keys = slice(0, P) if tile == 0 else slice(P, P + SEQ)
                    t = f(probs[:, h % 2, m, keys], ps[:, 2 * (h % 2) + m, keys], ACT.Exp, scale=SUB ** -0.5,
                          bias=row_max[:, h % 2, i:i + 1], accum_out=row_sum[:, h % 2, i:i + 1])
                t.then_inc(probs_ok, 1)

            def weights(h):
                act.wait_ge(dT_ps, h + 1)
                f(diffT[:, h % 2, :], ps[:, 4, 0:P + SEQ]).then_inc(dT_ev, 1)

            def head_out(h):
                act.wait_ge(pv_ps, h + 1)
                o = ps[:, 5, SEQ * (h % 2):SEQ * (h % 2 + 1)].rearrange("p (a n) -> p a n", a=TT)
                f(a_o[:, :, h * P:(h + 1) * P], o)
                for tt in range(TT):
                    t = f(part(work, 4608, 2, P)[:, tt, :], o[:, tt, :], ACT.Square, accum_out=o_sq[:, tt * HEADS + h:tt * HEADS + h + 1])
                t.then_inc(o_ev, 1)

            def root(hh):
                act.wait_ge(ms_ok, hh + 1)
                v = o_sq.rearrange("p (a h) -> p a h", a=TT)[:, :, 4 * hh:4 * hh + 4]
                r = o_rs.rearrange("p (a h) -> p a h", a=TT)[:, :, 4 * hh:4 * hh + 4]
                f(r, v, ACT.Sqrt).then_inc(root_ok, 1)

            f(ident_r, ident).then_inc(mask_ok, 1)
            f(mask_r, const("amask")).then_inc(mask_ok, 1)
            for n in range(4):
                project(n)
            turned(0)
            project(4)
            turned(2)
            soften(0)
            soften(1)
            for h in range(3):
                project(5 + h)
                weights(h)
                head_out(h)
                if h < 2:
                    soften(h + 2)
            project(8)
            turned(4)
            project(9)
            weights(3)
            head_out(3)
            turned(6)
            root(0)
            soften(4)
            soften(5)
            project(10)
            weights(4)
            soften(6)
            project(11)
            head_out(4)
            weights(5)
            soften(7)
            head_out(5)
            for tt in range(TT):
                out_copy(tt, tt, 0, 6 + tt, head_gain)
            weights(6)
            head_out(6)
            weights(7)
            head_out(7)
            root(1)
            for tt in range(TT):
                out_copy(2 + tt, tt, 1, 6 + tt, head_gain)
            layer_norm(0)
            xT_copies(1)

            def experts(layer):
                split_x(2 * layer)
                act.wait_ge(logit_ps, layer + 1)
                f(score, ps[:, 4, 0:P].rearrange("p (a e) -> p a e", a=TT), ACT.Sigmoid).then_inc(score_ok, 1)
                for tt in range(TT):
                    act.wait_ge(sh_ps, TT * layer + tt + 1)
                    f(silu[:, tt, :], ps[:, 5 + 2 * tt, 0:FF], ACT.Silu).then_inc(sh_silu, 1)
                def gathered(g, u, r):
                    act.wait_ge(xg_ps, 3 * g + r + 1)
                    f(xg[:, u, 4 * r:4 * r + 4, :], ps[:, 4, :].rearrange("p (j c) -> p j c", j=4)).then_inc(xg_ev, 1)

                def placed(g, u):
                    act.wait_ge(xg_ps, 3 * g + 3)
                    f(place[:, u, :], ps[:, 4, 0:SEQ])
                    f(gate_slot[0:SLOTS, u:u + 1], ps[0:SLOTS, 4, SEQ:SEQ + 1])
                    f(gate_slot[SLOTS:P, u:u + 1], ps[SLOTS:P, 4, SEQ + 1:SEQ + 2]).then_inc(xg_ev, 1)

                base = layer * PAIRS

                def step(p, u, last=False):
                    g = base + p
                    act.wait_ge(gu_ps, g + 1)
                    f(silu[:, u, :], ps[:, 5, 0:FF], ACT.Silu).then_inc(silu_ok, 1)
                    if not last:
                        gathered(g + 1, 1 - u, 0)
                    act.wait_ge(hidT_ps, g + 1)
                    f(hidT[:, u, :, :], ps[:, 6, 0:SEQ].rearrange("p (f c) -> p f c", f=FT)).then_inc(hidT_ev, 1)
                    if not last:
                        gathered(g + 1, 1 - u, 1)
                    for half in range(HALVES):
                        act.wait_ge(dn_ps, 2 * g + half + 1)
                        f(y_hi[:, half, :], ps[:, 5 + 2 * half, :]).then_inc(yhi_ok, 1)
                    if not last:
                        placed(g + 1, 1 - u)

                gathered(base, 0, 0)
                gathered(base, 0, 1)
                placed(base, 0)
                act.wait_ge(shT_ps, layer + 1)
                f(sh_hidT, ps[:, 6, :]).then_inc(shT_ev, 1)
                with act.Fori(0, PAIRS // 2 - 1) as it:
                    for u in range(2):
                        step(it * 2 + u, u)
                step(PAIRS - 2, 0)
                step(PAIRS - 1, 1, last=True)

                s = OV[layer]
                act.wait_ge(ovf_ok, layer + 1)
                n = act.value_load(ovf_list[0:1, 0:1], min_val=0, max_val=OVF - 1)
                with act.If(n > 0):
                    act.wait_ge(s["done"], 1)
                    act.drain().then_inc(s["xev"], 1)
                    with act.Fori(0, n) as i:
                        for r in range(2):
                            act.wait_ge(s["xps"], i * 3 + (r + 1))
                            f(xg[:, 0, 4 * r:4 * r + 4, :], ps[:, 4, :].rearrange("p (j c) -> p j c", j=4)).then_inc(s["xev"], 1)
                        act.wait_ge(s["xps"], i * 3 + 3)
                        f(place[:, 0, :], ps[:, 4, 0:SEQ])
                        f(gate_slot[:, 0:1], ps[:, 4, SEQ:SEQ + 1]).then_inc(s["xev"], 1)
                        act.wait_ge(s["gups"], i + 1)
                        f(silu[:, 0, :], ps[:, 5, 0:FF], ACT.Silu).then_inc(s["silu"], 1)
                        act.wait_ge(s["tps"], i + 1)
                        f(hidT[:, 0, :, :], ps[:, 6, 0:SEQ].rearrange("p (f c) -> p f c", f=FT)).then_inc(s["tev"], 1)
                        act.wait_ge(s["dps"], i + 1)
                        for half in range(HALVES):
                            t = f(y_hi[:, half, :], ps[:, 5 + 2 * half, :])
                        t.then_inc(s["yhi"], 1)
                with act.Else():
                    act.nop()

            experts(0)
            layer_norm(1)

            xT_copies(2)
            n = 12
            for i in range(4):
                act.wait_ge(proj_ps, n + 1)
                f(h_b[:, 2 * i:2 * i + 2, :], ps[:, n % 4, :].rearrange("p (h t) -> p h t", h=2), ACT.Sigmoid).then_inc(proj_ev, 1)
                n += 1
            act.wait_ge(forget_ok, 1)
            f(h_b, h_b, ACT.Ln).then_inc(logf_ok, 1)
            for i in range(4):
                act.wait_ge(proj_ps, n + 1)
                f(h_qT[:, 2 * i:2 * i + 2, :], ps[:, n % 4, :].rearrange("p (h t) -> p h t", h=2), ACT.Silu).then_inc(proj_ev, 1)
                n += 1

            def exponentials(i):
                A, m = h_A[i % 2], LEVELS[i]
                act.wait_ge(expo_ok, i + 1)
                quarter = "p h (c t) -> p h c t"
                if m == 128:
                    f(A[:, :, 2 * CHUNK:3 * CHUNK], h_b[:, :, 2 * CHUNK:3 * CHUNK], ACT.Exp)
                    f(A[:, :, 0:2 * CHUNK], A[:, :, 0:2 * CHUNK], ACT.Exp)
                    f(A[:, :, 3 * CHUNK:], A[:, :, 3 * CHUNK:], ACT.Exp).then_inc(exp_ok, 1)
                elif m == 64:
                    a, b = (v.rearrange(quarter, c=4) for v in (A, h_b))
                    f(a[:, :, 1::2, :], b[:, :, 1::2, :], ACT.Exp)
                    f(a[:, :, 0::2, :], a[:, :, 0::2, :], ACT.Exp).then_inc(exp_ok, 1)
                else:
                    f(A, A, ACT.Exp).then_inc(exp_ok, 1)

            def pieces(i):
                act.wait_ge(lev_ps, i + 1)
                if i == 0:
                    for b in range(2):
                        t = f(cross[:, 4 * b:4 * b + 4, :], ps[:, 4 + b, :].rearrange("p (h t) -> p h t", h=4))
                elif i == 1:
                    for b in range(2):
                        t = f(scoreT[0:64, 8 * b:8 * b + 8, 64:P], ps[0:64, 6 + b, :].rearrange("p (k t) -> p k t", k=8))
                else:
                    for q in (0, 2):
                        a = 32 * q
                        t = f(scoreT[a:a + 32, :, a + 32:a + 64],
                              ps[a:a + 32, level_bank(2), :].rearrange("p (k t) -> p k t", k=16))
                t.then_inc(lev_act, 1)

            exponentials(0)
            for i in range(4):
                exponentials(i + 1)
                act.wait_ge(proj_ps, n + 1)
                c, tt = i // 2, i % 2
                f(h_v[:, tt, c * BANK:(c + 1) * BANK], ps[:, n % 4, :]).then_inc(proj_ev, 1)
                n += 1
                if i < 3:
                    if i == 1:
                        act.wait_ge(scores_clear, 1)
                    pieces(i)
            for i in range(5, len(LEVELS)):
                exponentials(i)
            for i in range(4):
                act.wait_ge(proj_ps, n + 1)
                c, tt = i // 2, i % 2
                f(h_gate[:, tt, c * BANK:(c + 1) * BANK], ps[:, n % 4, :], ACT.Silu).then_inc(proj_ev, 1)
                n += 1
            for tt in range(TT):
                act.wait_ge(ho_ps, tt + 1)
                for h in range(HEADS):
                    t = f(part(odd, 6144 + (tt * HEADS + h) * P, P), ps[:, 2 * tt + h // 4, (h % 4) * P:(h % 4 + 1) * P], ACT.Square,
                          accum_out=o_sq[:, tt * HEADS + h:tt * HEADS + h + 1])
                t.then_inc(sq_ok, 1)
            act.wait_ge(ms_ok, 3)
            f(o_rs, o_sq, ACT.Sqrt).then_inc(root_ok, 1)
            for r in range(4):
                out_copy(4 + r, r // 2, r % 2, 4 + r, norm_h)
            layer_norm(2)
            xT_copies(3)
            experts(1)
            layer_norm(3)

        @block.vector
        def _(dve):
            links = [0]

            def link(t):
                links[0] += 1
                t.then_inc(dve_chain, 1)
                dve.wait_ge(dve_chain, links[0])

            tt_op = nc.vector.tensor_tensor
            ts_op = nc.vector.tensor_scalar
            stt = nc.vector.scalar_tensor_tensor

            def wait_item(name, layer, c):
                k = ITEM[name, layer, c]
                n = sum(2 if ITEMS[i][0] == "ln" else 1 for i in range(k % 2, k + 1, 2))
                dve.wait_ge(stream_in[k % 2], 16 * n)
                return stream[:, k % 2, :]

            def xT_copies(b):
                for tt in range(TT):
                    dve.wait_ge(xT_ps, 2 * b + tt + 1)
                    nc.vector.tensor_copy(xT[:, 4:8, tt * P:(tt + 1) * P],
                                          ps[:, 2 * tt + 1, :].rearrange("p (j t) -> p j t", j=4)).then_inc(xT_dve, 1)

            def layer_norm(n, outp=None):
                w = wait_item("ln", n // 2, n % 2)
                def add(tt, half):
                    cols = slice(half * BANK, (half + 1) * BANK)
                    link(stt(out=x[:, tt, cols], in0=x[:, tt, cols], scalar=ALPHA, in1=ps[:, tt * HALVES + half, :],
                             op0=ALU.mult, op1=ALU.add))
                    return nc.vector.bn_stats(stats[:, tt, half, :], x[:, tt, cols])

                def variance(tt, t):
                    link(t)
                    link(nc.vector.bn_aggr(mean_var[:, tt, :], stats[:, tt, :, :].rearrange("p a b -> p (a b)")))
                    ts_op(eps_var[:, tt:tt + 1], mean_var[:, tt, 1:2], EPS, None, ALU.add).then_inc(ln_var, 1)

                def finish(tt):
                    link(stt(out=x[:, tt, :], in0=x[:, tt, :], scalar=mean_var[:, tt, 0:1], in1=w[:, 0:D],
                             op0=ALU.subtract, op1=ALU.mult))
                    dve.wait_ge(ln_std, 2 * n + tt + 1)
                    link(nc.vector.reciprocal(rstd[:, tt:tt + 1], rstd[:, tt:tt + 1]))
                    stt(out=x[:, tt, :], in0=x[:, tt, :], scalar=rstd[:, tt:tt + 1], in1=w[:, D:2 * D],
                        op0=ALU.mult, op1=ALU.add).then_inc(x_ready, 1)

                if outp is None:
                    dve.wait_ge(moe_ps, n // 2 + 1)
                    for tt in range(TT):
                        add(tt, 0)
                        variance(tt, add(tt, 1))
                        finish(tt)
                else:
                    for half in range(HALVES):
                        for tt in range(TT):
                            dve.wait_ge(outp_ps, outp + half * TT + tt + 1)
                            t = add(tt, half)
                            if half:
                                variance(tt, t)
                                finish(tt)

            def split_x(layer):
                for tt in range(TT):
                    dve.wait_ge(xhi_ok, TT * layer + tt + 1)
                    tt_op(x_lo[:, tt, :, :], x[:, tt, :].rearrange("t (p j) -> t j p", j=J),
                          x_hi[:, tt, :, :].bitcast(F32), ALU.subtract).then_inc(x_split, 1)

            dve.wait_ge(vec_in, 64)
            dve.wait_ge(const_in, 32)
            link(tt_op(lam_prod, lam_row[:, 0::2, :], lam_row[:, 1::2, :], ALU.mult))
            nc.vector.tensor_reduce(lam2, lam_prod, AX, ALU.add).then_inc(lam_a, 1)
            xT_copies(0)
            dve.wait_ge(lam_b, 1)
            link(tt_op(neg_lam, lam2[:, 1:2], lam2[:, 0:1], ALU.subtract))
            link(ts_op(neg_lam, neg_lam, -LAMBDA_INIT, None, ALU.add))

            dve.wait_ge(lb_ps, 1)
            link(nc.vector.tensor_copy(lb_e.rearrange("p a h -> p (a h)"), ps[:, 6, 0:DEPTH * HEADS]))
            link(tt_op(lb_max, lb_e[:, 0, :], lb_e[:, 1, :], ALU.max))
            tt_op(lb_e, lb_e, lb_max[:, None, :].broadcast_to([P, DEPTH, HEADS]), ALU.subtract).then_inc(lb_exp_in, 1)
            dve.wait_ge(lb_exp_ok, 1)
            link(tt_op(lb_sum, lb_e[:, 0, :], lb_e[:, 1, :], ALU.add))
            link(nc.vector.reciprocal(lb_sum, lb_sum))
            link(tt_op(lb_e, lb_e, lb_sum[:, None, :].broadcast_to([P, DEPTH, HEADS]), ALU.mult))
            link(tt_op(lb_low, lb_e[:, 0, :], lb_e[:, 1, :], ALU.add))
            link(tt_op(lb_low, lb_low, lb_e[:, 0, :], ALU.subtract))
            link(ts_op(lb_rest, lb_low, -1.0, 1.0, ALU.mult, ALU.add))

            rope_tmp = [part(work, 128 * i, TT, HEADS, RH) for i in range(4)]
            cos = const("cos").rearrange("p (a r) -> p a r", a=TT)[:, :, None, :].broadcast_to([P, TT, HEADS, RH])
            sin = const("sin").rearrange("p (a r) -> p a r", a=TT)[:, :, None, :].broadcast_to([P, TT, HEADS, RH])

            def rope(i):
                dve.wait_ge(proj_ev, (2, 4, 8, 10)[i])
                if i:
                    dve.wait_ge(rope_ok, i)
                v = (q_tok, k_tok)[i % 2].rearrange("p a (h s) -> p a h s", s=SUB)[:, :, HEADS * (i // 2):HEADS * (i // 2 + 1), :]
                x1, x2 = v[:, :, :, 0:RH], v[:, :, :, RH:ROT]
                for t_, a_, b_ in zip(rope_tmp, (x1, x2, x2, x1), (cos, sin, cos, sin)):
                    t = tt_op(t_, a_, b_, ALU.mult)
                link(t)
                tt_op(x1, rope_tmp[0], rope_tmp[1], ALU.subtract)
                tt_op(x2, rope_tmp[2], rope_tmp[3], ALU.add).then_inc(rope_ok, 1)

            def turned(r):
                dve.wait_ge(turn_ps, r + 1)
                h = 4 * (r // 4) + 2
                dst = a_qT if r % 4 < 2 else a_kT
                nc.vector.tensor_copy(dst[:, h:h + 2, :],
                                      ps[:, TURN_BANK[r], :].rearrange("p (h t) -> p h t", h=2)).then_inc(turn_dve, 1)

            def front(h):
                u = h % 2
                dve.wait_ge(sc_ps, h + 1)
                nc.vector.tensor_reduce(row_max[:, u, 0:2], ps[:, 2 * u:2 * u + 2, 0:P], AX, ALU.max)
                link(nc.vector.tensor_reduce(row_max[:, u, 2:4], ps[:, 2 * u:2 * u + 2, P:P + SEQ], AX, ALU.max))
                ts_op(row_max[:, u, :], row_max[:, u, :], -SUB ** -0.5, None, ALU.mult).then_inc(nmax_ok, 1)

            def back(h):
                u = h % 2
                dve.wait_ge(probs_ok, h + 1)
                if h:
                    dve.wait_ge(diff_ok, h)
                link(nc.vector.reciprocal(row_scale, row_sum[:, u, :]))
                link(ts_op(row_scale[:, 1:4:2], row_scale[:, 1:4:2], neg_lam, None, ALU.mult))
                keys = (slice(0, P), slice(P, P + SEQ))
                for tile in range(2):
                    t = ts_op(probs[:, u, 1, keys[tile]], probs[:, u, 1, keys[tile]], row_scale[:, 2 * tile + 1:2 * tile + 2], None, ALU.mult)
                link(t)
                if h >= 2:
                    dve.wait_ge(dT_ps, h - 1)
                for tile in range(2):
                    t = stt(out=diff[:, u, keys[tile]], in0=probs[:, u, 0, keys[tile]], scalar=row_scale[:, 2 * tile:2 * tile + 1],
                            in1=probs[:, u, 1, keys[tile]], op0=ALU.mult, op1=ALU.add)
                t.then_inc(diff_ok, 1)

            def of_heads(v, hh):
                return v.rearrange("p (a h) -> p a h", a=TT)[:, :, 4 * hh:4 * hh + 4]

            def mean_square(hh):
                dve.wait_ge(o_ev, 4 * hh + 4)
                ts_op(of_heads(o_sq, hh), of_heads(o_sq, hh), 1.0 / P, EPS, ALU.mult, ALU.add).then_inc(ms_ok, 1)

            def norm_heads(hh):
                dve.wait_ge(root_ok, hh + 1)
                rs = of_heads(o_rs, hh)
                link(nc.vector.reciprocal(rs, rs))
                link(ts_op(rs, rs, 1.0 - LAMBDA_INIT, None, ALU.mult))
                for tt in range(TT):
                    v = a_o[:, tt, hh * BANK:(hh + 1) * BANK].rearrange("p (h n) -> p h n", h=4)
                    t = tt_op(v, v, rs[:, tt, :][:, :, None].broadcast_to([P, 4, P]), ALU.mult)
                t.then_inc(on_ok, 1)

            rope(0)
            rope(1)
            turned(1)
            turned(3)
            front(0)
            front(1)
            back(0)
            front(2)
            back(1)
            front(3)
            back(2)
            back(3)
            rope(2)
            turned(5)
            rope(3)
            mean_square(0)
            turned(7)
            front(4)
            front(5)
            back(4)
            norm_heads(0)
            front(6)
            back(5)
            front(7)
            back(6)
            back(7)
            mean_square(1)
            norm_heads(1)
            layer_norm(0, outp=0)
            xT_copies(1)

            def route(layer):
                dve.wait_ge(bias_in, 16 * (layer + 1))
                dve.wait_ge(score_ok, layer + 1)
                link(tt_op(choice, score, bias_row[:, None, :].broadcast_to([P, TT, NE]), ALU.add))
                groups = choice.rearrange("p a (g e) -> p (a g) e", e=GE)
                for i in range(TT * NG):
                    t = nc.vector.max(best8[:, i, :], groups[:, i, :])
                link(t)
                link(tt_op(g_sum, best8[:, :, 0], best8[:, :, 1], ALU.add))
                gv = g_sum.rearrange("p (a g) -> p a g", a=TT)
                r4, t4 = (v.rearrange("p (a g) k -> p a g k", a=TT) for v in (rank4, tie4))
                other = gv[:, :, None, :].broadcast_to([P, TT, NG, NG])
                own = gv[:, :, :, None].broadcast_to([P, TT, NG, NG])
                tt_op(r4, other, own, ALU.is_gt)
                link(tt_op(t4, other, own, ALU.is_equal))
                lower = const("lower").rearrange("p (g k) -> p g k", g=NG)[:, None, :, :].broadcast_to([P, TT, NG, NG])
                link(tt_op(t4, t4, lower, ALU.mult))
                link(tt_op(rank4, rank4, tie4, ALU.add))
                link(nc.vector.tensor_reduce(g_rank, rank4, AX, ALU.add))
                link(ts_op(g_rank, g_rank, float(TOPG), None, ALU.is_lt))
                link(ts_op(g_pen, g_rank, -1.0, BIG, ALU.add, ALU.mult))
                kg = kept.rearrange("p a (g e) -> p (a g) e", e=GE)
                link(tt_op(kg, groups, g_rank[:, :, None].broadcast_to([P, TT * NG, GE]), ALU.mult))
                link(tt_op(kg, kg, g_pen[:, :, None].broadcast_to([P, TT * NG, GE]), ALU.add))
                for tt in range(TT):
                    t = nc.vector.max(top8[:, tt, :], kept[:, tt, :])
                link(t)
                for tt in range(TT):
                    t = nc.vector.match_replace(out=replaced[:, tt, :], in_to_replace=top8[:, tt, :],
                                                in_values=kept[:, tt, :], imm_value=-3.3e38)
                link(t)
                tt_op(chosen, replaced, kept, ALU.not_equal).then_inc(chosen_ok, 1)
                dve.wait_ge(chosen_ok, layer + 1)
                link(tt_op(gate, score, chosen, ALU.mult))
                link(nc.vector.tensor_reduce(w_sum, gate, AX, ALU.add))
                link(ts_op(w_sum, w_sum, 1e-20, None, ALU.add))
                link(nc.vector.reciprocal(w_sum, w_sum))
                link(ts_op(w_sum, w_sum, ROUTED_SCALE, None, ALU.mult))
                link(tt_op(gate, gate, w_sum[:, :, None].broadcast_to([P, TT, NE]), ALU.mult))
                shared(layer)
                dve.wait_ge(pos_ps, layer + 1)
                stt(out=slot, in0=ps[:, 0, 0:P].rearrange("p (a e) -> p a e", a=TT), scalar=-NO_SLOT, in1=chosen,
                    op0=ALU.add, op1=ALU.mult).then_inc(route_ok, 1)

            def list_overflow(layer):
                for b in range(1, BLOCKS):
                    t = ts_op(flags[:, (b - 1) * NE:b * NE], ps[:, 0, P:P + NE], float(b * SLOTS), None, ALU.is_gt)
                link(t)
                ones = const("ones")[:, 0:1].broadcast_to([P, EXTRA])
                link(nc.vector.tensor_tensor_scan(flags_sum, ones, flags, 0.0, ALU.mult, ALU.add))
                link(tt_op(listed, flags_sum, flags, ALU.subtract))
                link(stt(out=listed, in0=listed, scalar=const("row"), in1=flags, op0=ALU.is_equal, op1=ALU.mult))
                for i, name in enumerate(("ovf_e", "ovf_b")):
                    link(tt_op(listed_id, listed, const(name), ALU.mult))
                    t = nc.vector.tensor_reduce(ovf_cols[:, i:i + 1], listed_id, AX, ALU.add)
                    if i == 0:
                        link(t)
                t.then_inc(ovf_cols_ok, 1)

            def read_list(layer):
                dve.wait_ge(ovf_row_ps, layer + 1)
                nc.vector.tensor_copy(ovf_list[:, 0:1], flags_sum[0:1, EXTRA - 1:EXTRA])
                nc.vector.tensor_copy(ovf_list[:, 1:1 + 2 * OVF], ps[0:1, 0, P + NE:P + NE + 2 * OVF]).then_inc(ovf_ok, 1)

            def shared(layer):
                for tt in range(TT):
                    dve.wait_ge(sh_silu, TT * layer + tt + 1)
                    tt_op(hid[:, tt, :], silu[:, tt, :], ps[:, 5 + 2 * tt, FF:2 * FF], ALU.mult).then_inc(sh_hid, 1)

            def experts(layer):
                split_x(layer)
                route(layer)
                dve.wait_ge(route_ok, layer + 1)
                base = layer * PAIRS
                iota = const("iota")[:, 0:SLOTS][:, None, None, :].broadcast_to([P, TT, 2, SLOTS])

                def one_hot(g, e, u):
                    if not isinstance(g, int) or g >= 2:
                        dve.wait_ge(xg_ps, 3 * g - 3)
                    s = slot[:, :, e:e + 2] if isinstance(e, int) else slot[:, :, bass.ds(e, 2)]
                    tt_op(pick[:, u, :, :].rearrange("p a (e c) -> p a e c", e=2), iota,
                          s[:, :, :, None].broadcast_to([P, TT, 2, SLOTS]), ALU.is_equal).then_inc(pick_ok, 1)

                def step(p, e, u, more=True):
                    g = base + p
                    dve.wait_ge(silu_ok, g + 1)
                    dve.wait_ge(xg_ev, 3 * g + 3)
                    stt(out=hid[:, u, :], in0=silu[:, u, :], scalar=gate_slot[:, u:u + 1], in1=ps[:, 5, FF:2 * FF],
                        op0=ALU.mult, op1=ALU.mult).then_inc(hid_ok, 1)
                    if more:
                        one_hot(g + 2, e + 4, u)
                    for half in range(HALVES):
                        dve.wait_ge(yhi_ok, 2 * g + half + 1)
                        tt_op(y_lo[:, half, :], ps[:, 5 + 2 * half, :], y_hi[:, half, :].bitcast(F32),
                              ALU.subtract).then_inc(ylo_ok, 1)

                one_hot(base, 0, 0)
                one_hot(base + 1, 2, 1)
                list_overflow(layer)
                read_list(layer)
                with dve.Fori(0, PAIRS // 2 - 1) as it:
                    for u in range(2):
                        step(it * 2 + u, it * 4 + 2 * u, u)
                step(PAIRS - 2, 0, 0, more=False)
                step(PAIRS - 1, 0, 1, more=False)

                s = OV[layer]
                n = dve.value_load(ovf_list[0:1, 0:1], min_val=0, max_val=OVF - 1)
                with dve.If(n > 0):
                    nc.vector.memset(pick[:, 0, :, SLOTS:P].bitcast(F32), 0.0)
                    with dve.Fori(0, n) as i:
                        e = dve.value_load(ovf_list[0:1, bass.ds(i + 1, 1)], min_val=0, max_val=NE - 1)
                        b = dve.value_load(ovf_list[0:1, bass.ds(i + (1 + OVF), 1)], min_val=0, max_val=BLOCKS - 1)
                        dve.wait_ge(s["done"], i + 1)
                        sl = slot[:, :, bass.ds(e, 1)].broadcast_to([P, TT, SLOTS])
                        io = cst[:, bass.ds(b * SLOTS + CONST_AT["iota"][0], SLOTS)][:, None, :].broadcast_to([P, TT, SLOTS])
                        tt_op(pick[:, 0, :, 0:SLOTS], io, sl, ALU.is_equal).then_inc(s["pick"], 1)
                        dve.wait_ge(s["silu"], i + 1)
                        stt(out=hid[:, 0, :], in0=silu[:, 0, :], scalar=gate_slot[:, 0:1], in1=ps[:, 5, FF:2 * FF],
                            op0=ALU.mult, op1=ALU.mult).then_inc(s["hid"], 1)
                        dve.wait_ge(s["yhi"], i + 1)
                        for half in range(HALVES):
                            t = tt_op(y_lo[:, half, :], ps[:, 5 + 2 * half, :], y_hi[:, half, :].bitcast(F32), ALU.subtract)
                        t.then_inc(s["ylo"], 1)
                with dve.Else():
                    dve.nop()

            experts(0)
            layer_norm(1)

            xT_copies(2)
            dve.wait_ge(proj_ev, 16)
            for h in range(HEADS):
                t = ts_op(h_b[:, h, :], h_b[:, h, :], lb_rest[:, h:h + 1], lb_low[:, h:h + 1], ALU.mult, ALU.add)
            link(t)
            link(ts_op(h_kT, h_b, -1.0, 1.0, ALU.mult, ALU.add))
            ts_op(h_b, h_b, FORGET_MIN, None, ALU.max).then_inc(forget_ok, 1)
            nc.vector.memset(scoreT, 0.0)
            nc.vector.memset(compact, 0.0).then_inc(scores_clear, 1)
            dve.wait_ge(logf_ok, 1)
            for h in range(HEADS):
                for c in range(SEQ // CHUNK):
                    v = h_b[:, h, c * CHUNK:(c + 1) * CHUNK]
                    t = nc.vector.tensor_tensor_scan(v, const("ones")[:, 0:CHUNK], v, 0.0, ALU.mult, ALU.add)
            link(t)
            b4 = h_b.rearrange("p h (c t) -> p h c t", c=4)

            def exponents(i):
                m, A = LEVELS[i], h_A[i % 2]
                if i >= 2:
                    dve.wait_ge(lev_ps, i - 1)
                last = b4[:, :, :, CHUNK - 1:CHUNK]
                A4 = A.rearrange("p h (c t) -> p h c t", c=4)
                wide = [P, HEADS, CHUNK]
                if m == 128:
                    link(tt_op(c01, last[:, :, 0], last[:, :, 1], ALU.add))
                    tt_op(A4[:, :, 0], c01.broadcast_to(wide), b4[:, :, 0], ALU.subtract)
                    tt_op(A4[:, :, 1], last[:, :, 1].broadcast_to(wide), b4[:, :, 1], ALU.subtract)
                    t = tt_op(A4[:, :, 3], b4[:, :, 3], last[:, :, 2].broadcast_to(wide), ALU.add)
                elif m == 64:
                    t = tt_op(A4[:, :, 0::2], last[:, :, 0::2].broadcast_to([P, HEADS, 2, CHUNK]), b4[:, :, 0::2], ALU.subtract)
                else:
                    a, b = (v.rearrange("p h t -> p (h t)").rearrange("p (n s m) -> p n s m", s=2, m=m) for v in (A, h_b))
                    mid = b[:, :, 0, m - 1:m].broadcast_to([P, HEADS * SEQ // (2 * m), m])
                    tt_op(a[:, :, 1], b[:, :, 1], mid, ALU.subtract)
                    t = tt_op(a[:, :, 0], mid, b[:, :, 0], ALU.subtract)
                t.then_inc(expo_ok, 1)

            def factors(i):
                m, A = LEVELS[i], h_A[i % 2]
                dve.wait_ge(exp_ok, i + 1)
                if i == 0:
                    dve.wait_ge(proj_ev, 20)
                a, q, k = (v.rearrange("p h t -> p (h t)").rearrange("p (n s m) -> p n s m", s=2, m=m) for v in (A, h_qT, h_kT))
                tt_op(a[:, :, 1], a[:, :, 1], q[:, :, 1], ALU.mult)
                tt_op(a[:, :, 0], a[:, :, 0], k[:, :, 0], ALU.mult).then_inc(lev_ok, 1)

            def merge(i):
                dve.wait_ge(lev_ps, i + 1)
                if i > 3:
                    dve.wait_ge(lev_dve, i - 3)
                which = masks[:, (i - 3) * 32:(i - 2) * 32][:, None, :].broadcast_to([P, HEADS * TT, 32])
                nc.vector.copy_predicated(compact, which, ps[:, level_bank(i), :].rearrange("p (k t) -> p k t", k=HEADS * TT))\
                  .then_inc(lev_dve, 1)

            dve.wait_ge(scores_clear, 1)
            exponents(0)
            for i in range(len(LEVELS)):
                if i + 1 < len(LEVELS):
                    exponents(i + 1)
                factors(i)
                if i > 3:
                    merge(i - 1)
            merge(7)
            merge(8)
            dve.wait_ge(lev_dve, 6)
            for q in range(4):
                a = 32 * q
                t = nc.vector.tensor_copy(scoreT[a:a + 32, :, a:a + 32], compact[a:a + 32, :, :])
            t.then_inc(scores_ok, 1)
            dve.wait_ge(sq_ok, 2)
            ts_op(o_sq, o_sq, 1.0 / P, EPS, ALU.mult, ALU.add).then_inc(ms_ok, 1)
            dve.wait_ge(root_ok, 3)
            link(nc.vector.reciprocal(o_rs, o_rs))
            for tt in range(TT):
                for h in range(HEADS):
                    cols = slice(h * P, (h + 1) * P)
                    t = stt(out=h_o[:, tt, cols], in0=ps[:, 2 * tt + h // 4, (h % 4) * P:(h % 4 + 1) * P],
                            scalar=o_rs[:, tt * HEADS + h:tt * HEADS + h + 1], in1=h_gate[:, tt, cols], op0=ALU.mult, op1=ALU.mult)
                t.then_inc(on_ok, 1)
            layer_norm(2, outp=4)
            xT_copies(3)
            experts(1)
            layer_norm(3)


_INS = ["x", "attn_w_in", "attn_w_out", "attn_lambda", "attn_subln", "hgrn_w_in", "hgrn_w_out",
        "hgrn_lower_bounds", "hgrn_norm", "moe_router", "moe_router_bias", "moe_w_gate_up", "moe_w_down",
        "shared_w_gate_up", "shared_w_down", "ln_gain", "ln_bias"]


def kernel(**inputs):
    import concourse.bacc as bacc
    from concourse.bass_utils import run_bass_kernel_spmd

    nc = bacc.Bacc("TRN2", target_bir_lowering=False, num_devices=1)
    floats, masks = constants()
    arrays = {f"in_{name}": np.ascontiguousarray(inputs[name]) for name in _INS}
    arrays["in_constants"], arrays["in_level_masks"] = floats, masks
    args = [nc.dram_tensor(name, a.shape, mybir.dt.from_np(a.dtype), kind="ExternalInput").ap() for name, a in arrays.items()]
    out = nc.dram_tensor("out", (1, SEQ, D), F32, kind="ExternalOutput").ap()
    build_trunk(nc, *args, out)
    return run_bass_kernel_spmd(nc, [arrays], core_ids=[0]).results[0]["out"]
```

```python
import math
from contextlib import ExitStack

import numpy as np

import concourse.bass as bass
from concourse import mybir

ALU = mybir.AluOpType
ACT = mybir.ActivationFunctionType
AX = mybir.AxisListType.X
F32 = mybir.dt.float32
F32R = mybir.dt.float32r
I32 = mybir.dt.int32

P = 128
SEQ, D = 256, 1024
TT = SEQ // P
J = D // P
DEPTH = 2
CHUNK = 64
BANK = 512
HALVES = D // BANK
HEADS = 8
SUB = 64
ROT = SUB // 4
RH = ROT // 2
ROPE_THETA = 500000.0
NE, NG, TOPG, TOPK = 64, 8, 4, 8
GE = NE // NG
FF = D // 4
FT = FF // P
SLOTS = 64
PAIRS = NE // 2
RESIDUAL_AT = 8
SHARED_AT = 18
BLOCKS = SEQ // SLOTS
EXTRA = NE * (BLOCKS - 1)
OVF = SEQ * TOPK // SLOTS
ROUTED_SCALE = 2.5
ALPHA = (2 * DEPTH) ** 0.25
EPS = 1e-5
BIG = 3.0e38
FORGET_MIN = 1e-19
LEVELS = [128, 64, 32, 16, 8, 4, 2, 1]
NO_SLOT = 999.0
LAMBDA_INIT = 0.8 - 0.6 * math.exp(-0.3 * 0)

CONST_WIDTHS = dict(ident=P, before=P, ones=P, cos=TT * RH, sin=TT * RH, amask=P + SEQ,
                    iota=BLOCKS * SLOTS, lower=NG * NG, row=1, ovf_e=EXTRA, ovf_b=EXTRA, eps=1)
CONST_AT, _at = {}, 0
for _name, _width in CONST_WIDTHS.items():
    CONST_AT[_name] = (_at, _at + _width)
    _at += _width
CONSTS = _at
COMPACT = [m for m in LEVELS if m < 32] + [0]


def constants():
    c = np.zeros((P, CONSTS), np.float32)

    def put(name, value):
        a, b = CONST_AT[name]
        c[:, a:b] = value

    t = np.arange(P)
    put("ident", np.eye(P))
    put("before", t[:, None] < t[None, :])
    put("ones", 1.0)
    freq = np.float32(ROPE_THETA) ** (-np.arange(0, ROT, 2, dtype=np.float32) / np.float32(ROT))
    angle = np.arange(SEQ, dtype=np.float32)[:, None] * freq[None, :].astype(np.float32)
    for name, f in (("cos", np.cos), ("sin", np.sin)):
        put(name, f(angle).astype(np.float32).reshape(TT, P, RH).transpose(1, 0, 2).reshape(P, -1))
    am = np.zeros((P, P + SEQ), np.float32)
    q_chunk = t[:, None] // CHUNK
    am[:, :P] = np.where(t[None, :] // CHUNK <= q_chunk, 0, -1e30)
    am[:, P:] = np.where(np.arange(SEQ)[None, :] // CHUNK <= q_chunk + P // CHUNK, 0, -1e30)
    put("amask", am)
    put("iota", (np.arange(BLOCKS * SLOTS) - NO_SLOT)[None, :])
    g = np.arange(NG)
    put("lower", (g[None, :] < g[:, None]).reshape(1, -1))
    put("row", t[:, None])
    k = np.arange(EXTRA)
    put("ovf_e", (k % NE)[None, :])
    put("ovf_b", (k // NE + 1)[None, :])
    put("eps", EPS)
    masks = np.zeros((P, len(COMPACT), 32), np.int32)
    s, q = (t % 32)[:, None], np.arange(32)[None, :]
    for i, m in enumerate(COMPACT):
        masks[:, i] = (s == q) if m == 0 else (s // (2 * m) == q // (2 * m)) & (s % (2 * m) < m) & (q % (2 * m) >= m)
    return c, masks.reshape(P, -1)


ITEMS = []
for _layer, _chunks in ((0, 6), (1, 8)):
    ITEMS += [("in", _layer, c) for c in range(_chunks)]
    ITEMS += [("out", _layer, c) for c in range(HALVES)]
    if _layer == 1:
        ITEMS.append(("ln", _layer, 0))
    ITEMS += [("sgu", _layer, 0), ("sdn", _layer, 0), ("ln", _layer, 1)]
ITEM = {item: k for k, item in enumerate(ITEMS)}
ATTN_COLUMNS = [0, 1024, 2048, 512, 1536, 2560]
HGRN_COLUMNS = [2048, 1024, 1536, 0, 512, 2560, 3072, 3584]


TURN_BANK = [4, 5, 4, 5, 0, 1, 2, 3]


def unit_bank(n):
    return n % 4 if n < 4 or n >= 12 else 6 + n % 2


def level_bank(i):
    return [4, 6, 4, 5, 6, 7, 4, 5, 6][i]


def build_trunk(nc, x_in, attn_w_in, attn_w_out, attn_lambda, attn_subln, hgrn_w_in, hgrn_w_out,
                hgrn_lower_bounds, hgrn_norm, moe_router, moe_router_bias, moe_w_gate_up, moe_w_down,
                shared_w_gate_up, shared_w_down, ln_gain, ln_bias, consts, level_masks, out):
    ctx = ExitStack()

    def sb(name, shape, dt=F32):
        return ctx.enter_context(nc.sbuf_tensor(name, shape, dt))

    def sem(name):
        return ctx.enter_context(nc.semaphore(name))

    with ctx:
        cst = sb("cst", [P, CONSTS])
        masks = sb("masks", [P, len(COMPACT) * 32], I32)
        x = sb("x", [P, TT, D])
        xT = sb("xT", [P, J, SEQ])
        w_gu = sb("w_gu", [P, 2, J * 2 * FF])
        w_dn = sb("w_dn", [P, 2, FT * D])
        odd = sb("odd", [P, 2 * (J * 2 * FF + FT * D)])
        stream = sb("stream", [P, 2, J * BANK])
        x_hi = sb("x_hi", [P, TT, J, P], F32R)
        x_lo = sb("x_lo", [P, TT, J, P], F32R)
        pick = sb("pick", [P, 2, TT, P], F32R)
        place = sb("place", [P, 2, SEQ], F32R)
        alpha_hi, alpha_lo = sb("alpha_hi", [P, P], F32R), sb("alpha_lo", [P, P], F32R)
        y_hi = sb("y_hi", [P, HALVES, BANK], F32R)
        y_lo = sb("y_lo", [P, HALVES, BANK], F32R)
        work = sb("work", [P, 6144])
        w_router = sb("w_router", [P, J, NE])
        bias_row = sb("bias_row", [P, NE])
        small = sb("small", [P, 256])
        ovf_list = sb("ovf_list", [1, 1 + 2 * OVF], I32)
        ps = ctx.enter_context(nc.psum_tensor("ps", [P, 8, BANK], F32))

        def const(name, width=None):
            a, b = CONST_AT[name]
            return cst[:, a:b]

        ident = const("ident")
        GU, DN = J * 2 * FF, FT * D

        def gate_up_of(slot):
            w = w_gu[:, slot, :] if slot < 2 else odd[:, (slot - 2) * GU:(slot - 1) * GU]
            return w

        def down_of(slot):
            return w_dn[:, slot, :] if slot < 2 else odd[:, 2 * GU + (slot - 2) * DN:2 * GU + (slot - 1) * DN]

        def part(tensor, at, *shape):
            v = tensor[:, at:at + int(np.prod(shape))]
            names = "abcd"[:len(shape)]
            return v.rearrange(f"p ({' '.join(names)}) -> p {' '.join(names)}", **dict(zip(names, shape))) if len(shape) > 1 else v

        qkv = part(odd, 0, 3, TT, D)
        q_tok, k_tok, v_tok = qkv[:, 0], qkv[:, 1], qkv[:, 2]
        a_qT, a_kT = part(odd, 6144, HEADS, SEQ), part(odd, 8192, HEADS, SEQ)
        a_o = q_tok
        probs = part(work, 1536, 2, 2, P + SEQ)
        mask_r, ident_r = y_hi[:, 0, 0:P + SEQ], y_hi[:, 1, 0:P]
        diff = part(work, 3072, 2, P + SEQ)
        diffT = part(work, 3840, 2, P + SEQ)
        oT = part(odd, 6144, HEADS, SEQ)
        ln_first = part(odd, 10240, 2 * D)
        h_b, h_qT, h_kT = (part(odd, 2048 * i, HEADS, SEQ) for i in (0, 3, 1))
        h_A = [part(odd, 2048 * i, HEADS, SEQ) for i in (2, 4)]
        h_A.append(w_dn[:, 1, :].rearrange("p (h t) -> p h t", h=HEADS))
        scoreT = part(odd, 10240, HEADS * TT, P)
        h_o = h_A[0].rearrange("p h t -> p (h t)").rearrange("p (a n) -> p a n", a=TT)
        h_v, h_gate = part(work, 0, TT, D), part(work, 2048, TT, D)
        cross, compact = part(work, 4096, HEADS, P), part(work, 5120, HEADS * TT, 32)
        xg = part(work, 0, 2, J, P)
        sh_hidT = part(work, 5632, FT * SEQ)
        silu, hid, hidT = part(work, 2048, 2, FF), part(work, 2560, 2, FF), part(work, 3072, 2, FT, P)
        R0 = 3584
        score, choice, kept, replaced = (part(work, R0 + 128 * i, TT, NE) for i in range(4))
        chosen, gate, slot = (part(work, R0 + 128 * i, TT, NE) for i in range(4, 7))
        best8 = part(work, R0 + 896, TT * NG, 8)
        rank4 = part(work, R0 + 1024, TT * NG, NG)
        tie4 = part(work, R0 + 1152, TT * NG, NG)
        flags, flags_sum = part(work, R0 + 1280, EXTRA), part(work, R0 + 1472, EXTRA)
        listed, listed_id = part(work, R0 + 1664, EXTRA), part(work, R0 + 1856, EXTRA)
        (g_sum, g_rank, g_pen) = (small[:, 16 * i:16 * i + 16] for i in range(3))
        top8 = part(small, 48, TT, 8)
        w_sum = small[:, 64:66]
        gate_slot = part(small, 66, 2)
        ovf_cols = small[:, 68:70]
        stats = part(small, 203, TT, HALVES, 6)
        mean_var = part(small, 227, TT, 2)
        rstd, eps_var = part(small, 231, TT), part(small, 233, TT)
        row_max = part(small, 88, 2, 4)
        row_sum = part(small, 96, 2, 4)
        row_scale = part(small, 104, 4)
        neg_lam = small[:, 108:109]
        o_sq = small[:, 110:126]
        o_rs = small[:, 126:142]
        head_gain = small[:, 142:143]
        lam2 = small[:, 144:146]
        lb_e = part(small, 146, 2, HEADS)
        lb_rest = small[:, 162:170]
        lb_low = small[:, 170:178]
        c01 = part(small, 178, HEADS, 1)
        lb_sum = small[:, 186:194]
        lb_max = small[:, 194:202]
        norm_h = small[:, 202:203]

        lam_row = part(work, 4608, 4, SUB)
        lam_prod = part(work, 4864, 2, SUB)
        lb_raw = work[:, 5120:5120 + P]

        ln_in, ident_in, const_in, x_loaded, vec_in = sem("ln_in"), sem("ident_in"), sem("const_in"), [sem(f"x_loaded{tt}") for tt in range(TT)], sem("vec_in")
        router_in, bias_in = sem("router_in"), sem("bias_in")
        stream_in = [sem("stream_in0"), sem("stream_in1")]
        gu_in = [sem(f"gu_in{s}") for s in range(4)]
        first_in = sem("first_in")
        tail_gu_in, tail_dn_in = ([sem(f"tail_{n}_in{i}") for i in range(2)] for n in ("gu", "dn"))
        dn_in = [sem(f"dn_in{s}") for s in range(4)]
        out_stored = sem("out_stored")
        x_ready, x_split = sem("x_ready"), sem("x_split")
        xT_ps, xT_act, xT_dve = sem("xT_ps"), sem("xT_act"), sem("xT_dve")
        proj_ps, proj_ev = sem("proj_ps"), sem("proj_ev")
        rope_ok, turn_ps, turn_act, turn_dve = sem("rope_ok"), sem("turn_ps"), sem("turn_act"), sem("turn_dve")
        sc_ps, nmax_ok, probs_ok, diff_ok = sem("sc_ps"), sem("nmax_ok"), sem("probs_ok"), sem("diff_ok")
        dT_ps, dT_ev, pv_ps, o_ev = sem("dT_ps"), sem("dT_ev"), sem("pv_ps"), sem("o_ev")
        lam_a, lam_b = sem("lam_a"), sem("lam_b")
        ms_ok, root_ok, on_ok = sem("ms_ok"), sem("root_ok"), sem("on_ok")
        oT_ps, oT_ev, outp_ps = sem("oT_ps"), sem("oT_ev"), sem("outp_ps")
        ln_var, ln_std = sem("ln_var"), sem("ln_std")
        xhi_ok = sem("xhi_ok")
        lb_ps, lb_exp_in, lb_exp_ok = sem("lb_ps"), sem("lb_exp_in"), sem("lb_exp_ok")
        forget_ok, logf_ok = sem("forget_ok"), sem("logf_ok")
        expo_ok, exp_ok, lev_ok, lev_ps = sem("expo_ok"), sem("exp_ok"), sem("lev_ok"), sem("lev_ps")
        lev_act, lev_dve, scores_ok, ho_ps = sem("lev_act"), sem("lev_dve"), sem("scores_ok"), sem("ho_ps")
        logit_ps, score_ok, chosen_ok, pos_ps, route_ok = sem("logit_ps"), sem("score_ok"), sem("chosen_ok"), sem("pos_ps"), sem("route_ok")
        ovf_cols_ok, ovf_row_ps, ovf_ok = sem("ovf_cols_ok"), sem("ovf_row_ps"), sem("ovf_ok")
        sh_ps, sh_silu, sh_hid, shT_ps, shT_ev = sem("sh_ps"), sem("sh_silu"), sem("sh_hid"), sem("shT_ps"), sem("shT_ev")
        pick_ok, xg_ps, xg_ev, gu_ps = sem("pick_ok"), sem("xg_ps"), sem("xg_ev"), sem("gu_ps")
        silu_ok, hid_ok, hidT_ps, hidT_ev = sem("silu_ok"), sem("hid_ok"), sem("hidT_ps"), sem("hidT_ev")
        dn_ps, yhi_ok, ylo_ok, moe_ps = sem("dn_ps"), sem("yhi_ok"), sem("ylo_ok"), sem("moe_ps")
        sdn_ps = sem("sdn_ps")
        mask_ok, alpha_ok, gates_ok = sem("mask_ok"), sem("alpha_ok"), sem("gates_ok")
        scores_clear, sq_ok = sem("scores_clear"), sem("sq_ok")
        dve_chain, act_chain = sem("dve_chain"), sem("act_chain")
        OV = [{n: sem(f"o{layer}_{n}") for n in ("gu_in", "dn_in", "pick", "xps", "xev", "gups", "silu", "hid", "tps", "tev", "dps", "yhi", "ylo", "done")}
              for layer in range(DEPTH)]

        block = ctx.enter_context(nc.Block())

        def rows(w):
            return w.rearrange("(p j) n -> p j n", j=J)

        def expert_gu(layer, e):
            w = moe_w_gate_up[layer]
            w = w[e] if isinstance(e, int) else w[bass.ds(e, 1)].rearrange("a d n -> (a d) n")
            return w.rearrange("(p j) n -> p (j n)", j=J)

        def expert_dn(layer, e):
            w = moe_w_down[layer]
            w = w[e] if isinstance(e, int) else w[bass.ds(e, 1)].rearrange("a d n -> (a d) n")
            return w.rearrange("(p j) n -> p (j n)", j=FT)

        def last_use(k):
            name, layer, c = ITEMS[k]
            return {"in": (proj_ps, 12 * layer + 2 * c + 2), "out": (outp_ps, 4 * layer + 2 * c + 2),
                    "ln": (x_ready, 4 * layer + 2 * c + 2), "sgu": (sh_ps, TT * (layer + 1)), "sdn": (sdn_ps, layer + 1)}[name]

        @block.sync
        def _(sp):
            def load_item(k):
                name, layer, c = ITEMS[k]
                if k >= 2:
                    sp.wait_ge(*last_use(k - 2))
                buf = stream[:, k % 2, :]
                if name == "in":
                    w, col = (attn_w_in, ATTN_COLUMNS[c]) if layer == 0 else (hgrn_w_in, HGRN_COLUMNS[c])
                    dst, src = buf.rearrange("p (j n) -> p j n", j=J), rows(w[0])[:, :, col:col + BANK]
                elif name == "out":
                    w = attn_w_out if layer == 0 else hgrn_w_out
                    dst = buf.rearrange("p (h n) -> p h n", h=HEADS)
                    src = w[0].rearrange("(h p) n -> p h n", p=P)[:, :, c * BANK:(c + 1) * BANK]
                elif name == "ln":
                    for i, v in enumerate((ln_gain, ln_bias)):
                        sp.dma_start(buf[:, i * D:(i + 1) * D], v[layer, c:c + 1, :].broadcast_to([P, D])).then_inc(stream_in[k % 2], 16)
                    return
                elif name == "sgu":
                    dst, src = buf, shared_w_gate_up[layer].rearrange("(p j) n -> p (j n)", j=J)
                else:
                    dst, src = buf[:, 0:DN], shared_w_down[layer].rearrange("(p j) n -> p (j n)", j=FT)
                sp.dma_start(dst, src).then_inc(stream_in[k % 2], 16)

            def load_pair(layer, p, e, u, parts=(0, 1), down_parts=(0, 1)):
                g = layer * PAIRS + p
                if parts and (not isinstance(g, int) or g >= 2):
                    sp.wait_ge(gu_ps, g - 1)
                for i in parts:
                    sp.dma_start(gate_up_of(2 * u + i), expert_gu(layer, e + i)).then_inc(gu_in[2 * u + i], 16)
                if down_parts and (not isinstance(g, int) or g >= 2):
                    sp.wait_ge(dn_ps, 2 * g - 2)
                for i in down_parts:
                    sp.dma_start(down_of(2 * u + i), expert_dn(layer, e + i)).then_inc(dn_in[2 * u + i], 16)

            def load_last_pair(layer):
                g, e = layer * PAIRS + PAIRS - 1, NE - 2
                sp.wait_ge(gu_ps, g - 1)
                for part_, arrived in enumerate((gu_in[2:4], tail_gu_in)):
                    cols = slice(part_ * GU // 2, (part_ + 1) * GU // 2)
                    for i in range(2):
                        sp.dma_start(gate_up_of(2 + i)[:, cols], expert_gu(layer, e + i)[:, cols]).then_inc(arrived[i], 16)
                sp.wait_ge(dn_ps, 2 * g - 2)
                for half, arrived in enumerate((dn_in[2:4], tail_dn_in)):
                    cols = slice(half * BANK, (half + 1) * BANK)
                    for i in range(2):
                        dst, src = (v.rearrange("p (f n) -> p f n", f=FT)[:, :, cols] for v in (down_of(2 + i), expert_dn(layer, e + i)))
                        sp.dma_start(dst, src).then_inc(arrived[i], 16)

            sp.dma_start(cst[:, 0:P], consts[:, 0:P]).then_inc(ident_in, 16)
            first_dst, first_src = (v.rearrange("p (j n) -> p j n", j=J) if i == 0 else v for i, v in
                                    enumerate((stream[:, 0, :], rows(attn_w_in[0])[:, :, 0:BANK])))
            for tt in range(TT):
                sp.dma_start(x[:, tt, :], x_in[0, tt * P:(tt + 1) * P, :]).then_inc(x_loaded[tt], 16)
                js = slice(tt * J // 2, (tt + 1) * J // 2)
                sp.dma_start(first_dst[:, js, :], first_src[:, js, :]).then_inc(first_in if tt == 0 else stream_in[0], 16)
            sp.dma_start(cst[:, P:], consts[:, P:]).then_inc(const_in, 16)
            sp.dma_start(lam_row, attn_lambda.rearrange("a l s -> a (l s)").broadcast_to([P, 4 * SUB]).rearrange("p (l s) -> p l s", l=4)).then_inc(vec_in, 16)
            sp.dma_start(head_gain, attn_subln.rearrange("a n -> n a")).then_inc(vec_in, 16)
            sp.dma_start(norm_h, hgrn_norm.rearrange("a n -> n a")).then_inc(vec_in, 16)
            sp.dma_start(lb_raw[0:DEPTH * HEADS, :], hgrn_lower_bounds.rearrange("a (h p) -> (a h) p", p=P)).then_inc(vec_in, 16)
            load_item(1)
            for i, v in enumerate((ln_gain, ln_bias)):
                sp.dma_start(ln_first[:, i * D:(i + 1) * D], v[0, 0:1, :].broadcast_to([P, D])).then_inc(ln_in, 16)
            sp.dma_start(masks[:], level_masks).then_inc(const_in, 16)
            k = 2
            for layer in range(DEPTH):
                if layer == 1:
                    sp.wait_ge(moe_ps, layer)
                    sp.wait_ge(route_ok, layer)
                sp.dma_start(w_router[:], rows(moe_router[layer])).then_inc(router_in, 16)
                sp.dma_start(bias_row[:], moe_router_bias[layer:layer + 1, :].broadcast_to([P, NE])).then_inc(bias_in, 16)
                prefetch_at = ITEM["out", 0, 0] if layer == 0 else k
                while ITEMS[k] != ("ln", layer, 1):
                    if k == prefetch_at:
                        load_pair(layer, 0, 0, 0, down_parts=(0, 1)[:2 - layer])
                    load_item(k)
                    k += 1
                    if ITEMS[k] == ("out", 1, 1):
                        sp.wait_ge(lev_ps, 6)
                        load_pair(1, 0, 0, 0, parts=(), down_parts=(1,))
                    if ITEMS[k - 1] == (("out", 0, 1), ("ln", 1, 0))[layer]:
                        sp.wait_ge(oT_ev, 4 * (layer + 1))
                        load_pair(layer, 1, 2, 1, parts=(0,), down_parts=(0,))
                    if ITEMS[k] == ("sdn", layer, 0):
                        sp.wait_ge(outp_ps, 4 * (layer + 1))
                        load_pair(layer, 1, 2, 1, parts=(1,), down_parts=())
                        sp.wait_ge(x_ready, 4 * layer + 2)
                        load_pair(layer, 1, 2, 1, parts=(), down_parts=(1,))
                        sp.dma_start(stream[:, k % 2, :], expert_gu(layer, 4)).then_inc(gu_in[0], 16)
                        load_pair(layer, 2, 4, 0, parts=(1,), down_parts=())
                        load_pair(layer, 3, 6, 1, down_parts=())
                        load_pair(layer, 2, 4, 0, parts=())
                        load_pair(layer, 3, 6, 1, parts=())
                        sp.wait_ge(gu_ps, layer * PAIRS + 3)
                with sp.Fori(2, PAIRS // 2 - 1) as it:
                    for u in range(2):
                        load_pair(layer, it * 2 + u, it * 4 + 2 * u, u)
                load_pair(layer, PAIRS - 2, NE - 4, 0)
                load_last_pair(layer)
                load_item(k)
                k += 1
                s = OV[layer]
                sp.wait_ge(ovf_ok, layer + 1)
                n = sp.value_load(ovf_list[0:1, 0:1], min_val=0, max_val=OVF - 1)
                with sp.If(n > 0):
                    sp.wait_ge(dn_ps, 2 * PAIRS * (layer + 1))
                    with sp.Fori(0, n) as i:
                        e = sp.value_load(ovf_list[0:1, bass.ds(i + 1, 1)], min_val=0, max_val=NE - 1)
                        sp.wait_ge(s["done"], i + 1)
                        sp.dma_start(gate_up_of(0), expert_gu(layer, e)).then_inc(s["gu_in"], 16)
                        sp.dma_start(down_of(0), expert_dn(layer, e)).then_inc(s["dn_in"], 16)
                with sp.Else():
                    sp.nop()
                if layer == 0:
                    load_item(k)
                    k += 1
            for tt in range(TT):
                sp.wait_ge(x_ready, 4 * (DEPTH - 1) + 3 + tt)
                sp.dma_start(out[0, tt * P:(tt + 1) * P, :], x[:, tt, :]).then_inc(out_stored, 16)
            sp.wait_ge(out_stored, 16 * TT)

        @block.tensor
        def _(pe):
            def item(name, layer, c):
                k = ITEM[name, layer, c]
                n = sum(2 if ITEMS[i][0] == "ln" else 1 for i in range(k % 2, k + 1, 2))
                pe.wait_ge(stream_in[k % 2], 16 * n)
                return stream[:, k % 2, :]

            def turn_x(b, tt):
                if b == 0:
                    pe.wait_ge(x_loaded[tt], 16)
                else:
                    pe.wait_ge(x_ready, 2 * (b - 1) + tt + 1)
                for j in range(J):
                    t = pe.transpose(ps[:, 2 * tt + j // 4, (j % 4) * P:(j % 4 + 1) * P],
                                     x[:, tt, j:D:J], ident)
                t.then_inc(xT_ps, 1)

            def xT_wait(b, tt):
                pe.wait_ge(xT_act, 2 * b + tt + 1)
                if b == 0 or tt == 1:
                    pe.wait_ge(xT_dve, b + tt + 1)

            def rows_unit(w, tt, n, js=range(J)):
                if n >= 4 and js[0] == 0:
                    pe.wait_ge(proj_ev, n - 3 if n >= 12 else max(n - 1, 4))
                for j in js:
                    t = pe.matmul(ps[:, unit_bank(n), :], xT[:, j, tt * P:(tt + 1) * P], w[:, j, :],
                                  start=(j == 0), stop=(j == J - 1))
                if js[-1] == J - 1:
                    t.then_inc(proj_ps, 1)

            def columns_unit(w, half, n):
                pe.wait_ge(proj_ev, n - 3)
                for i in range(2):
                    for j in range(J):
                        c = (2 * half + i) * P
                        t = pe.matmul(ps[:, n % 4, i * SEQ:(i + 1) * SEQ], w[:, j, c:c + P], xT[:, j, :],
                                      start=(j == 0), stop=(j == J - 1))
                t.then_inc(proj_ps, 1)
                return t

            def turn_heads(o, tt, hh, bank):
                for i in range(4):
                    h = 4 * hh + i
                    t = pe.transpose(ps[:, bank, i * P:(i + 1) * P], o[:, tt, h * P:(h + 1) * P], ident)
                t.then_inc(oT_ps, 1)

            def out_unit(layer, c, tt, heads):
                w = item("out", layer, c).rearrange("p (h n) -> p h n", h=HEADS)
                for h in heads:
                    t = pe.matmul(ps[:, tt * HALVES + c, :], oT[:, h, tt * P:(tt + 1) * P], w[:, h, :],
                                  start=(h == 0), stop=(h == HEADS - 1))
                if heads[-1] == HEADS - 1:
                    t.then_inc(outp_ps, 1)

            pe.wait_ge(ident_in, 16)
            turn_x(0, 0)
            xT_wait(0, 0)
            pe.wait_ge(first_in, 16)
            first_w = stream[:, 0, :].rearrange("p (j n) -> p j n", j=J)
            rows_unit(first_w, 0, 0, range(J // 2))
            turn_x(0, 1)
            rows_unit(item("in", 0, 0).rearrange("p (j n) -> p j n", j=J), 0, 0, range(J // 2, J))
            xT_wait(0, 1)

            def unit(n):
                rows_unit(item("in", 0, n // 2).rearrange("p (j n) -> p j n", j=J), n % 2, n)

            def turn(r):
                group, src = r // 4, (q_tok if r % 4 < 2 else k_tok)
                pe.wait_ge(rope_ok, r // 2 + 1)
                if r in (2, 3):
                    pe.wait_ge(turn_act if r == 2 else turn_dve, 1)
                if r == 4:
                    pe.wait_ge(probs_ok, 4)
                for i in range(2):
                    for tt in range(TT):
                        h = 4 * group + 2 * (r % 2) + i
                        t = pe.transpose(ps[:, TURN_BANK[r], (i * TT + tt) * P:(i * TT + tt + 1) * P],
                                         src[:, tt, h * P:(h + 1) * P], ident)
                t.then_inc(turn_ps, 1)

            def scores(h):
                if h in (0, 4):
                    pe.wait_ge(turn_act, 2 + h // 2)
                    pe.wait_ge(turn_dve, 2 + h // 2)
                if h == 0:
                    pe.wait_ge(proj_ev, 4)
                    pe.wait_ge(mask_ok, 2)
                if h >= 2:
                    pe.wait_ge(probs_ok, h - 1)
                for m in range(2):
                    rows_m = slice(m * SUB, (m + 1) * SUB)
                    b = 2 * (h % 2) + m
                    pe.matmul(ps[:, b, 0:P + SEQ], ident_r, mask_r, start=True, stop=False, skip_group_check=True)
                    pe.matmul(ps[:, b, 0:P], a_qT[rows_m, h, 0:P], a_kT[rows_m, h, 0:P], start=False, stop=True,
                              skip_group_check=True)
                    t = pe.matmul(ps[:, b, P:P + SEQ], a_qT[rows_m, h, P:SEQ], a_kT[rows_m, h, :],
                                  start=False, stop=True, skip_group_check=True)
                t.then_inc(sc_ps, 1)

            def turn_diff(h):
                pe.wait_ge(diff_ok, h + 1)
                if h:
                    pe.wait_ge(dT_ev, h)
                for i in range(3):
                    t = pe.transpose(ps[:, 4, i * P:(i + 1) * P], diff[:, h % 2, i * P:(i + 1) * P], ident)
                t.then_inc(dT_ps, 1)

            def values(h):
                pe.wait_ge(dT_ev, h + 1)
                pe.wait_ge(proj_ev, 6 if h < 4 else 12)
                if h >= 2:
                    pe.wait_ge(o_ev, h - 1)
                v, dT, a = v_tok[:, :, h * P:(h + 1) * P], diffT[:, h % 2, :], SEQ * (h % 2)
                pe.matmul(ps[:, 5, a:a + P], dT[:, 0:P], v[:, 0, :], start=True, stop=True)
                pe.matmul(ps[:, 5, a + P:a + SEQ], dT[:, P:2 * P], v[:, 0, :], start=True, stop=False)
                pe.matmul(ps[:, 5, a + P:a + SEQ], dT[:, 2 * P:3 * P], v[:, 1, :], start=False, stop=True)\
                  .then_inc(pv_ps, 1)

            pe.wait_ge(vec_in, 64)
            pe.transpose(ps[:, 6, 0:DEPTH * HEADS], lb_raw[0:DEPTH * HEADS, :], ident[0:DEPTH * HEADS, 0:DEPTH * HEADS])\
              .then_inc(lb_ps, 1)
            for n in range(1, 4):
                unit(n)
            turn(0)
            turn(1)
            unit(4)
            turn(2)
            turn(3)
            scores(0)
            scores(1)
            for h in range(3):
                unit(5 + h)
                turn_diff(h)
                if h < 2:
                    scores(h + 2)
                values(h)
            unit(8)
            turn(4)
            turn(5)
            unit(9)
            turn_diff(3)
            values(3)
            turn(6)
            turn(7)
            scores(4)
            scores(5)
            unit(10)
            turn_diff(4)
            scores(6)
            unit(11)
            values(4)
            turn_diff(5)
            scores(7)
            values(5)
            pe.wait_ge(on_ok, 1)
            pe.wait_ge(proj_ev, 12)
            for tt in range(TT):
                turn_heads(a_o, tt, 0, 6 + tt)
            turn_diff(6)
            values(6)
            pe.wait_ge(probs_ok, HEADS)
            pe.wait_ge(oT_ev, 2)
            out_unit(0, 0, 0, range(4))
            turn_diff(7)
            out_unit(0, 0, 1, range(4))
            values(7)
            for tt in range(TT):
                out_unit(0, 1, tt, range(4))
            pe.wait_ge(on_ok, 2)
            for tt in range(TT):
                turn_heads(a_o, tt, 1, 6 + tt)
            for c in range(HALVES):
                for tt in range(TT):
                    pe.wait_ge(oT_ev, 3 + tt)
                    out_unit(0, c, tt, range(4, HEADS))

            def gather(g, r, bank=4):
                if r == 0:
                    pe.wait_ge(pick_ok, g + 2)
                if bank == 4:
                    pe.wait_ge(xg_ev, 3 * g + r)
                for i in range(2):
                    j = 2 * r + i
                    for n, (tt, half) in enumerate([(tt, half) for tt in range(TT) for half in (x_hi, x_lo)]):
                        t = pe.matmul(ps[:, bank, i * 2 * P:(i + 1) * 2 * P].rearrange("p (u c) -> p u c", u=2),
                                      half[:, tt, j, :], pick[:, :, tt, :], start=(n == 0), stop=(n == 3))
                t.then_inc(xg_ps, 1)

            def turn_pick(g, u, gates, bank=4):
                if not isinstance(g, int) or g % PAIRS:
                    pe.wait_ge(xg_ev, 3 * g + (4, 2)[u])
                for tt in range(TT):
                    pe.transpose(ps[:, bank, tt * P:(tt + 1) * P], pick[:, u, tt, :].bitcast(F32), ident)
                for tt in range(TT):
                    t = pe.matmul(ps[:, bank, SEQ:SEQ + 2], pick[:, u, tt, :].bitcast(F32), gates(tt),
                                  start=(tt == 0), stop=(tt == TT - 1))
                t.then_inc(xg_ps, 1)

            def gate_up(g, u, turn, weights=gate_up_of, rounds=False, last=False, bank=5):
                if not rounds:
                    pe.wait_ge(xg_ev, 3 * g + (4, 1)[u])
                for i in range(2):
                    pe.wait_ge(gu_in[2 * u + i], turn)
                for j in range(J):
                    if last and j == J // 2:
                        for i in range(2):
                            pe.wait_ge(tail_gu_in[i], 16 * (g // PAIRS + 1))
                    if rounds and j % 2 == 0:
                        pe.wait_ge(xg_ev, 3 * g + j // 2 + 1)
                    for i in range(2):
                        a, b = i * SLOTS, (i + 1) * SLOTS
                        t = pe.matmul(ps[a:b, bank, :], xg[:, u, j, a:b],
                                      weights(2 * u + i)[:, j * BANK:(j + 1) * BANK],
                                      start=(j == 0), stop=(j == J - 1))
                t.then_inc(gu_ps, 1)

            def turn_hidden(g, u, layer, first):
                pe.wait_ge(hid_ok, g + 1)
                if first:
                    pe.wait_ge(shT_ev, TT * layer + 1)
                for f in range(FT):
                    t = pe.transpose(ps[:, 6, f * P:(f + 1) * P], hid[:, u, f:FF:FT], ident)
                t.then_inc(hidT_ps, 1)

            def down(g, u, half, turn, last=False):
                if half == 0:
                    pe.wait_ge(hidT_ev, g + 1)
                    for i in range(2):
                        pe.wait_ge(dn_in[2 * u + i], turn)
                elif last:
                    for i in range(2):
                        pe.wait_ge(tail_dn_in[i], 16 * (g // PAIRS + 1))
                for f in range(FT):
                    for i in range(2):
                        a, b = i * SLOTS, (i + 1) * SLOTS
                        at = f * D + half * BANK
                        t = pe.matmul(ps[a:b, 5 + 2 * half, :], hidT[:, u, f, a:b],
                                      down_of(2 * u + i)[:, at:at + BANK], start=(f == 0), stop=(f == FT - 1))
                t.then_inc(dn_ps, 1)

            def scatter(g, u, half, first=False, last=False):
                pe.wait_ge(ylo_ok, 2 * g + half + 1)
                if half == 0:
                    pe.wait_ge(xg_ev, 3 * g + (5, 3)[u])
                for tt in range(TT):
                    for y in (y_hi, y_lo):
                        pe.matmul(ps[:, tt * HALVES + half, :], place[:, u, tt * P:(tt + 1) * P], y[:, half, :],
                                  start=first and y is y_hi, stop=last and y is y_lo, skip_group_check=True)

            def experts(layer):
                pe.wait_ge(router_in, 16 * (layer + 1))
                for tt in range(TT):
                    turn_x(2 * layer + 1, tt)
                    xT_wait(2 * layer + 1, tt)
                    for j in range(J):
                        t = pe.matmul(ps[:, 4, tt * NE:(tt + 1) * NE], xT[:, j, tt * P:(tt + 1) * P], w_router[:, j, :],
                                      start=(j == 0), stop=(j == J - 1))
                t.then_inc(logit_ps, 1)

                def shared_gate_up(tt, js=range(J)):
                    w = item("sgu", layer, 0)
                    for j in js:
                        t = pe.matmul(ps[:, 5, :], xT[:, j, tt * P:(tt + 1) * P], w[:, j * BANK:(j + 1) * BANK],
                                      start=(j == 0), stop=(j == J - 1))
                    if js[-1] == J - 1:
                        t.then_inc(sh_ps, 1)

                shared_gate_up(0, range(J - 1))
                pe.wait_ge(chosen_ok, layer + 1)
                pos, before, ones = ps[:, 0, 0:P], const("before"), const("ones")
                pe.matmul(pos[:, 0:NE], before, chosen[:, 0, :], start=True, stop=True)
                pe.matmul(pos[:, NE:2 * NE], ones, chosen[:, 0, :], start=True, stop=False)
                pe.matmul(pos[:, NE:2 * NE], before, chosen[:, 1, :], start=False, stop=True)
                count = ps[:, 0, P:P + NE]
                pe.matmul(count, ones, chosen[:, 0, :], start=True, stop=False)
                pe.matmul(count, ones, chosen[:, 1, :], start=False, stop=True).then_inc(pos_ps, 1)
                shared_gate_up(0, range(J - 1, J))
                pe.wait_ge(x_split, TT * (layer + 1))
                base = layer * PAIRS

                def turn_shared(tt):
                    pe.wait_ge(sh_hid, TT * layer + tt + 1)
                    if tt:
                        pe.wait_ge(hidT_ev, base + SHARED_AT)
                    for f in range(FT):
                        t = pe.transpose(ps[:, 6, BANK // 2 + f * P:BANK // 2 + (f + 1) * P], hid[:, 1, f:FF:FT], ident)
                    t.then_inc(shT_ps, 1)

                def turn_list():
                    pe.wait_ge(ovf_cols_ok, layer + 1)
                    for i in range(2):
                        a = P + NE + i * OVF
                        t = pe.matmul(ps[0:1, 0, a:a + OVF], ovf_cols[:, i:i + 1], ident[:, 0:OVF], start=True, stop=True)
                    t.then_inc(ovf_row_ps, 1)

                def shared_down():
                    pe.wait_ge(shT_ev, TT * (layer + 1))
                    w = item("sdn", layer, 0)
                    for tt in range(TT):
                        for half in range(HALVES):
                            for f in range(FT):
                                t = pe.matmul(ps[:, tt * HALVES + half, :], sh_hidT[:, f * SEQ + tt * P:f * SEQ + (tt + 1) * P],
                                              w[:, f * D + half * BANK:f * D + (half + 1) * BANK],
                                              start=False, stop=False, skip_group_check=True)
                    t.then_inc(sdn_ps, 1)

                def residual():
                    pe.wait_ge(alpha_ok, 2)
                    for tt in range(TT):
                        for half in range(HALVES):
                            for a in (alpha_hi, alpha_lo):
                                for part_ in (x_hi, x_lo):
                                    pe.matmul(ps[:, tt * HALVES + half, :].rearrange("t (p j) -> t p j", j=J), a[:],
                                              part_[:, tt, :, 64 * half:64 * (half + 1)].rearrange("t j p -> t p j"),
                                              start=False, stop=False, skip_group_check=True)

                def gates(e):
                    return lambda tt: gate[:, tt, e:e + 2] if isinstance(e, int) else gate[:, tt, bass.ds(e, 2)]

                def first_pairs():
                    g, turn = base, first_turn + 16
                    gate_up(g, 0, turn, rounds=True)
                    gate_up(g + 1, 1, turn, bank=7)
                    pe.wait_ge(gates_ok, layer + 1)
                    turn_pick(g, 0, gates(0))
                    turn_list()
                    turn_shared(0)
                    turn_pick(g + 1, 1, gates(2))
                    turn_hidden(g, 0, layer, True)
                    down(g, 0, 0, turn)
                    pe.wait_ge(hid_ok, g + 2)
                    down(g, 0, 1, turn)
                    gather(g + 2, 0)
                    pe.wait_ge(ovf_ok, layer + 1)
                    for half in range(HALVES):
                        scatter(g, 0, half, first=True)
                    turn_hidden(g + 1, 1, layer, False)
                    gather(g + 2, 1)
                    for half in range(HALVES):
                        down(g + 1, 1, half, turn)
                        gather(g + 2, 2 + half)
                    scatter(g + 1, 1, 0)
                    turn_pick(g + 2, 0, gates(4))

                def step(p, e, u, turn, last=False):
                    g = base + p
                    ahead = u == 1 and not last
                    if isinstance(p, int) and p == 2:
                        k = ITEM["sdn", layer, 0]
                        gate_up(g, u, turn, lambda n: gate_up_of(n) if n else stream[:, k % 2, :])
                    else:
                        gate_up(g, u, turn, last=last)
                    if ahead:
                        gather(g + 1, 0)
                    scatter(g - 1, 1 - u, 1)
                    turn_hidden(g, u, layer, False)
                    if ahead:
                        gather(g + 1, 1)
                    if u == 0:
                        turn_pick(g + 1, 1, gates(e + 2))
                    down(g, u, 0, turn)
                    if ahead:
                        gather(g + 1, 2)
                    down(g, u, 1, turn, last)
                    if ahead:
                        gather(g + 1, 3)
                    scatter(g, u, 0, last=last)
                    if ahead:
                        turn_pick(g + 1, 0, gates(e + 2))

                def steps(a, b):
                    with pe.Fori(a, b) as it:
                        for u in range(2):
                            step(it * 2 + u, it * 4 + 2 * u, u, it * 16 + (first_turn + 16))

                first_turn = 16 * (PAIRS // 2) * layer
                for r in range(4):
                    gather(base, r, bank=(1, 2, 3, 7)[r])
                pe.wait_ge(sh_hid, TT * layer + 1)
                first_pairs()
                for p in (2, 3):
                    step(p, 2 * p, p % 2, first_turn + 16 * (p // 2 + 1))
                steps(2, RESIDUAL_AT // 2)
                residual()
                steps(RESIDUAL_AT // 2, SHARED_AT // 2)
                shared_gate_up(1)
                turn_shared(1)
                shared_down()
                steps(SHARED_AT // 2, PAIRS // 2 - 1)
                for p in range(PAIRS - 2, PAIRS):
                    step(p, 2 * p, p % 2, first_turn + 16 * (p // 2 + 1), last=(p == PAIRS - 1))
                scatter(base + PAIRS - 1, 1, 1, last=True)

                s = OV[layer]
                n = pe.value_load(ovf_list[0:1, 0:1], min_val=0, max_val=OVF - 1)
                with pe.If(n > 0):
                    pe.drain().then_inc(s["done"], 1)
                    with pe.Fori(0, n) as i:
                        e = pe.value_load(ovf_list[0:1, bass.ds(i + 1, 1)], min_val=0, max_val=NE - 1)
                        pe.wait_ge(s["pick"], i + 1)
                        for r in range(2):
                            pe.wait_ge(s["xev"], i * 3 + (r + 1))
                            for c in range(4):
                                j = 4 * r + c
                                for k, (tt, half) in enumerate([(tt, half) for tt in range(TT) for half in (x_hi, x_lo)]):
                                    t = pe.matmul(ps[:, 4, c * P:(c + 1) * P], half[:, tt, j, :], pick[:, 0, tt, :],
                                                  start=(k == 0), stop=(k == 3))
                            t.then_inc(s["xps"], 1)
                        pe.wait_ge(s["xev"], i * 3 + 3)
                        for tt in range(TT):
                            pe.transpose(ps[:, 4, tt * P:(tt + 1) * P], pick[:, 0, tt, :].bitcast(F32), ident)
                        for tt in range(TT):
                            t = pe.matmul(ps[:, 4, SEQ:SEQ + 1], pick[:, 0, tt, :].bitcast(F32), gate[:, tt, bass.ds(e, 1)],
                                          start=(tt == 0), stop=(tt == TT - 1))
                        t.then_inc(s["xps"], 1)
                        pe.wait_ge(s["xev"], i * 3 + 4)
                        pe.wait_ge(s["gu_in"], i * 16 + 16)
                        for j in range(J):
                            t = pe.matmul(ps[:, 5, :], xg[:, 0, j, :], gate_up_of(0)[:, j * BANK:(j + 1) * BANK],
                                          start=(j == 0), stop=(j == J - 1))
                        t.then_inc(s["gups"], 1)
                        pe.wait_ge(s["hid"], i + 1)
                        for f in range(FT):
                            t = pe.transpose(ps[:, 6, f * P:(f + 1) * P], hid[:, 0, f:FF:FT], ident)
                        t.then_inc(s["tps"], 1)
                        pe.wait_ge(s["tev"], i + 1)
                        pe.wait_ge(s["dn_in"], i * 16 + 16)
                        for half in range(HALVES):
                            for f in range(FT):
                                at = f * D + half * BANK
                                t = pe.matmul(ps[:, 5 + 2 * half, :], hidT[:, 0, f, :], down_of(0)[:, at:at + BANK],
                                              start=(f == 0), stop=(f == FT - 1))
                        t.then_inc(s["dps"], 1)
                        pe.wait_ge(s["ylo"], i + 1)
                        for half in range(HALVES):
                            for tt in range(TT):
                                for y in (y_hi, y_lo):
                                    pe.matmul(ps[:, tt * HALVES + half, :], place[:, 0, tt * P:(tt + 1) * P], y[:, half, :],
                                              start=False, stop=(y is y_lo), skip_group_check=True)
                        pe.drain().then_inc(s["done"], 1)
                with pe.Else():
                    pe.nop()
                pe.drain().then_inc(moe_ps, 1)

            experts(0)

            for tt in range(TT):
                turn_x(2, tt)
                xT_wait(2, tt)
                rows_unit(item("in", 1, 0).rearrange("p (j n) -> p j n", j=J), tt, 12 + tt)
            n = 14
            for c in range(1, 5):
                w = item("in", 1, c).rearrange("p (j n) -> p j n", j=J)
                for half in range(2):
                    t = columns_unit(w, half, n)
                    n += 1

            def level(i):
                m = LEVELS[i] if i < len(LEVELS) else 0
                if m:
                    pe.wait_ge(lev_ok, i + 1)
                    A = h_A[i % 3]
                bank = level_bank(i)
                if 2 <= i <= 6:
                    pe.wait_ge(lev_act, {2: 1, 3: 1, 4: 2, 5: 2, 6: 3}[i])
                if i >= 7:
                    pe.wait_ge(lev_dve, i - 6)
                if m == 128:
                    for h in range(HEADS):
                        t = pe.matmul(ps[:, 4 + h // 4, (h % 4) * P:(h % 4 + 1) * P], A[:, h, 0:P], A[:, h, P:SEQ],
                                      start=True, stop=True)
                elif m == 64:
                    for h in range(HEADS):
                        for tt in range(TT):
                            k, a = h * TT + tt, tt * P
                            t = pe.matmul(ps[0:64, 6 + k // 8, (k % 8) * 64:(k % 8 + 1) * 64], A[:, h, a:a + 64],
                                          A[:, h, a + 64:a + P], start=True, stop=True)
                else:
                    for h in range(HEADS):
                        for tt in range(TT):
                            for q in range(4):
                                if m == 32 and q % 2:
                                    continue
                                k, a = h * TT + tt, tt * P + 32 * q
                                lhs = A[:, h, a:a + 32] if m else h_kT[:, h, a:a + 32]
                                rhs = A[:, h, a + 32:a + 64] if m == 32 else A[:, h, a:a + 32] if m else h_qT[:, h, a:a + 32]
                                t = pe.matmul(ps[32 * q:32 * q + 32, bank, 32 * k:32 * k + 32], lhs, rhs,
                                              start=True, stop=True)
                t.then_inc(lev_ps, 1)

            def unit(n, js=range(J)):
                rows_unit(item("in", 1, (n - 12) // 2).rearrange("p (j n) -> p j n", j=J), n % 2, n, js)

            for i in range(9):
                unit(22 + i // 2, range(J // 2, J) if i % 2 else range(0, J // 2))
                level(i)
            unit(26, range(J // 2, J))
            pe.wait_ge(scores_ok, 1)
            pe.wait_ge(lev_act, 3)
            pe.wait_ge(proj_ev, 24)
            for tt in range(TT):
                for h in range(HEADS):
                    o = ps[:, 4 + 2 * tt + h // 4, (h % 4) * P:(h % 4 + 1) * P]
                    v = h_v[:, :, h * P:(h + 1) * P]
                    if tt == 1:
                        pe.matmul(o, cross[:, h, :], v[:, 0, :], start=True, stop=False)
                    t = pe.matmul(o, scoreT[:, h * TT + tt, :], v[:, tt, :], start=(tt == 0), stop=True)
                t.then_inc(ho_ps, 1)

            def turn_gated(hh, tt):
                pe.wait_ge(on_ok, 2 + 2 * hh + tt + 1)
                turn_heads(h_o, tt, hh, 4 + 2 * tt + hh)

            unit(27)
            for tt in range(TT):
                turn_gated(0, tt)
            pe.wait_ge(proj_ev, 27)
            pe.wait_ge(oT_ev, 4 + 2)
            out_unit(1, 0, 0, range(4))
            turn_gated(1, 0)
            out_unit(1, 0, 1, range(4))
            turn_gated(1, 1)
            for tt in range(TT):
                pe.wait_ge(oT_ev, 4 + 3 + tt)
                out_unit(1, 0, tt, range(4, HEADS))
            pe.wait_ge(proj_ev, 28)
            for tt in range(TT):
                out_unit(1, 1, tt, range(HEADS))
            experts(1)

        @block.scalar
        def _(act):
            links = [0]

            def link(t):
                links[0] += 1
                t.then_inc(act_chain, 1)
                act.wait_ge(act_chain, links[0])

            def f(out_, in_, func=ACT.Copy, **kw):
                return nc.scalar.activation(out_, in_, func, **kw)

            def xT_copy(b, tt):
                act.wait_ge(xT_ps, 2 * b + tt + 1)
                n = 1 if b == 0 or tt == 1 else 2
                f(xT[:, 0:4 * n, tt * P:(tt + 1) * P].rearrange("p (a j) t -> p a j t", a=n),
                  ps[:, 2 * tt:2 * tt + n, :].rearrange("p a (j t) -> p a j t", j=4)).then_inc(xT_act, 1)

            def out_copy(n, tt, hh, bank, gain):
                act.wait_ge(oT_ps, n + 1)
                f(oT[:, 4 * hh:4 * hh + 4, tt * P:(tt + 1) * P], ps[:, bank, :].rearrange("p (h t) -> p h t", h=4),
                  scale=gain).then_inc(oT_ev, 1)

            def split_x(tt):
                f(x_hi[:, tt, :, :], x[:, tt, :].rearrange("t (p j) -> t j p", j=J)).then_inc(xhi_ok, 1)

            def layer_norm(n):
                for tt in range(TT):
                    act.wait_ge(ln_var, 2 * n + tt + 1)
                    f(rstd[:, tt:tt + 1], eps_var[:, tt:tt + 1], ACT.Sqrt).then_inc(ln_std, 1)
                    if tt == 1 and n % 2 == 0:
                        split_x(0)
                    if n < 3:
                        xT_copy(n + 1, tt)
                if n % 2 == 0:
                    split_x(1)


            for tt in range(TT):
                xT_copy(0, tt)
            act.wait_ge(lam_a, 1)
            f(lam2, lam2, ACT.Exp).then_inc(lam_b, 1)
            act.wait_ge(lb_exp_in, 1)
            f(lb_e, lb_e, ACT.Exp).then_inc(lb_exp_ok, 1)

            def project(n):
                c, tt = n // 2, n % 2
                act.wait_ge(proj_ps, n + 1)
                f(qkv[:, c % 3, tt, (c // 3) * BANK:(c // 3 + 1) * BANK], ps[:, unit_bank(n), :]).then_inc(proj_ev, 1)

            def turned(r):
                act.wait_ge(turn_ps, r + 1)
                h = 4 * (r // 4)
                dst = a_qT if r % 4 < 2 else a_kT
                f(dst[:, h:h + 2, :], ps[:, TURN_BANK[r], :].rearrange("p (h t) -> p h t", h=2)).then_inc(turn_act, 1)

            def soften(h):
                act.wait_ge(nmax_ok, h + 1)
                for i, (tile, m) in enumerate(((0, 0), (0, 1), (1, 0), (1, 1))):
                    keys = slice(0, P) if tile == 0 else slice(P, P + SEQ)
                    t = f(probs[:, h % 2, m, keys], ps[:, 2 * (h % 2) + m, keys], ACT.Exp, scale=SUB ** -0.5,
                          bias=row_max[:, h % 2, i:i + 1], accum_out=row_sum[:, h % 2, i:i + 1])
                t.then_inc(probs_ok, 1)

            def weights(h):
                act.wait_ge(dT_ps, h + 1)
                f(diffT[:, h % 2, :], ps[:, 4, 0:P + SEQ]).then_inc(dT_ev, 1)

            def head_out(h):
                act.wait_ge(pv_ps, h + 1)
                o = ps[:, 5, SEQ * (h % 2):SEQ * (h % 2 + 1)].rearrange("p (a n) -> p a n", a=TT)
                f(a_o[:, :, h * P:(h + 1) * P], o)
                for tt in range(TT):
                    t = f(part(work, 4608, 2, P)[:, tt, :], o[:, tt, :], ACT.Square, accum_out=o_sq[:, tt * HEADS + h:tt * HEADS + h + 1])
                t.then_inc(o_ev, 1)

            def root(hh):
                act.wait_ge(ms_ok, hh + 1)
                v = o_sq.rearrange("p (a h) -> p a h", a=TT)[:, :, 4 * hh:4 * hh + 4]
                r = o_rs.rearrange("p (a h) -> p a h", a=TT)[:, :, 4 * hh:4 * hh + 4]
                f(r, v, ACT.Sqrt).then_inc(root_ok, 1)

            act.wait_ge(const_in, 16)
            f(ident_r, ident).then_inc(mask_ok, 1)
            f(mask_r, const("amask")).then_inc(mask_ok, 1)
            for n in range(4):
                project(n)
            turned(0)
            project(4)
            turned(2)
            soften(0)
            soften(1)
            for h in range(3):
                project(5 + h)
                weights(h)
                head_out(h)
                if h < 2:
                    soften(h + 2)
            project(8)
            turned(4)
            project(9)
            weights(3)
            head_out(3)
            turned(6)
            root(0)
            soften(4)
            soften(5)
            project(10)
            weights(4)
            soften(6)
            project(11)
            head_out(4)
            weights(5)
            soften(7)
            head_out(5)
            for tt in range(TT):
                out_copy(tt, tt, 0, 6 + tt, head_gain)
            weights(6)
            head_out(6)
            weights(7)
            head_out(7)
            root(1)
            for tt in range(TT):
                out_copy(2 + tt, tt, 1, 6 + tt, head_gain)
            layer_norm(0)

            def experts(layer):
                act.wait_ge(logit_ps, layer + 1)
                f(score, ps[:, 4, 0:P].rearrange("p (a e) -> p a e", a=TT), ACT.Sigmoid).then_inc(score_ok, 1)
                base = layer * PAIRS

                def shared_silu(tt):
                    act.wait_ge(sh_ps, TT * layer + tt + 1)
                    f(silu[:, 1, :], ps[:, 5, 0:FF], ACT.Silu).then_inc(sh_silu, 1)

                def shared_turned(tt):
                    act.wait_ge(shT_ps, TT * layer + tt + 1)
                    f(sh_hidT.rearrange("p (f a c) -> p f a c", f=FT, a=TT)[:, :, tt, :],
                      ps[:, 6, BANK // 2:BANK].rearrange("p (f c) -> p f c", f=FT)).then_inc(shT_ev, 1)

                def gathered(g, r, bank=4):
                    act.wait_ge(xg_ps, 3 * g + r + 1)
                    f(xg[:, :, 2 * r:2 * r + 2, :].rearrange("p u j c -> p j u c"),
                      ps[:, bank, :].rearrange("p (j u c) -> p j u c", j=2, u=2)).then_inc(xg_ev, 1)

                def placed(g, u, bank=4):
                    act.wait_ge(xg_ps, 3 * g + (5, 3)[u])
                    f(place[:, u, :], ps[:, bank, 0:SEQ])
                    f(gate_slot[0:SLOTS, u:u + 1], ps[0:SLOTS, bank, SEQ:SEQ + 1])
                    f(gate_slot[SLOTS:P, u:u + 1], ps[SLOTS:P, bank, SEQ + 1:SEQ + 2]).then_inc(xg_ev, 1)

                def gate_silu(g, u, bank=5):
                    act.wait_ge(gu_ps, g + 1)
                    f(silu[:, u, :], ps[:, bank, 0:FF], ACT.Silu).then_inc(silu_ok, 1)

                def hidden_turned(g, u):
                    act.wait_ge(hidT_ps, g + 1)
                    f(hidT[:, u, :, :], ps[:, 6, 0:SEQ].rearrange("p (f c) -> p f c", f=FT)).then_inc(hidT_ev, 1)

                def high_part(g, half):
                    act.wait_ge(dn_ps, 2 * g + half + 1)
                    f(y_hi[:, half, :], ps[:, 5 + 2 * half, :]).then_inc(yhi_ok, 1)

                def first_pairs():
                    g = base
                    gate_silu(g, 0)
                    gate_silu(g + 1, 1, bank=7)
                    placed(g, 0)
                    shared_turned(0)
                    placed(g + 1, 1)
                    hidden_turned(g, 0)
                    for half in range(HALVES):
                        high_part(g, half)
                    gathered(g + 2, 0)
                    hidden_turned(g + 1, 1)
                    gathered(g + 2, 1)
                    for half in range(HALVES):
                        high_part(g + 1, half)
                        gathered(g + 2, 2 + half)
                    placed(g + 2, 0)

                def step(p, u, last=False):
                    g = base + p
                    ahead = u == 1 and not last
                    gate_silu(g, u)
                    if ahead:
                        gathered(g + 1, 0)
                    hidden_turned(g, u)
                    if ahead:
                        gathered(g + 1, 1)
                    if u == 0:
                        placed(g + 1, 1)
                    for half in range(HALVES):
                        high_part(g, half)
                        if ahead:
                            gathered(g + 1, 2 + half)
                    if ahead:
                        placed(g + 1, 0)

                def steps(a, b):
                    with act.Fori(a, b) as it:
                        for u in range(2):
                            step(it * 2 + u, u)

                shared_silu(0)
                for r in range(4):
                    gathered(base, r, bank=(1, 2, 3, 7)[r])
                first_pairs()
                steps(1, SHARED_AT // 2)
                shared_silu(1)
                shared_turned(1)
                steps(SHARED_AT // 2, PAIRS // 2 - 1)
                step(PAIRS - 2, 0)
                step(PAIRS - 1, 1, last=True)

                s = OV[layer]
                act.wait_ge(ovf_ok, layer + 1)
                n = act.value_load(ovf_list[0:1, 0:1], min_val=0, max_val=OVF - 1)
                with act.If(n > 0):
                    act.wait_ge(s["done"], 1)
                    act.drain().then_inc(s["xev"], 1)
                    with act.Fori(0, n) as i:
                        for r in range(2):
                            act.wait_ge(s["xps"], i * 3 + (r + 1))
                            f(xg[:, 0, 4 * r:4 * r + 4, :], ps[:, 4, :].rearrange("p (j c) -> p j c", j=4)).then_inc(s["xev"], 1)
                        act.wait_ge(s["xps"], i * 3 + 3)
                        f(place[:, 0, :], ps[:, 4, 0:SEQ])
                        f(gate_slot[:, 0:1], ps[:, 4, SEQ:SEQ + 1]).then_inc(s["xev"], 1)
                        act.wait_ge(s["gups"], i + 1)
                        f(silu[:, 0, :], ps[:, 5, 0:FF], ACT.Silu).then_inc(s["silu"], 1)
                        act.wait_ge(s["tps"], i + 1)
                        f(hidT[:, 0, :, :], ps[:, 6, 0:SEQ].rearrange("p (f c) -> p f c", f=FT)).then_inc(s["tev"], 1)
                        act.wait_ge(s["dps"], i + 1)
                        for half in range(HALVES):
                            t = f(y_hi[:, half, :], ps[:, 5 + 2 * half, :])
                        t.then_inc(s["yhi"], 1)
                with act.Else():
                    act.nop()

            experts(0)
            layer_norm(1)

            def project_rows(n):
                c, tt = (0 if n < 14 else 1 if n < 24 else (n - 24) // 2), n % 2
                act.wait_ge(proj_ps, n + 1)
                dst = (h_v if n < 24 else h_gate)[:, tt, c * BANK:(c + 1) * BANK]
                f(dst, ps[:, n % 4, :], ACT.Copy if n < 24 else ACT.Silu).then_inc(proj_ev, 1)

            project_rows(12)
            project_rows(13)
            n = 14
            for i in range(4):
                act.wait_ge(proj_ps, n + 1)
                f(h_b[:, 2 * i:2 * i + 2, :], ps[:, n % 4, :].rearrange("p (h t) -> p h t", h=2), ACT.Sigmoid).then_inc(proj_ev, 1)
                n += 1
            act.wait_ge(forget_ok, 1)
            f(h_b, h_b, ACT.Ln).then_inc(logf_ok, 1)
            def exponentials(i):
                A, m = h_A[i % 3], LEVELS[i]
                act.wait_ge(expo_ok, i + 1)
                quarter = "p h (c t) -> p h c t"
                if m == 128:
                    f(A[:, :, 2 * CHUNK:3 * CHUNK], h_b[:, :, 2 * CHUNK:3 * CHUNK], ACT.Exp)
                    f(A[:, :, 0:2 * CHUNK], A[:, :, 0:2 * CHUNK], ACT.Exp)
                    f(A[:, :, 3 * CHUNK:], A[:, :, 3 * CHUNK:], ACT.Exp).then_inc(exp_ok, 1)
                elif m == 64:
                    a, b = (v.rearrange(quarter, c=4) for v in (A, h_b))
                    f(a[:, :, 1::2, :], b[:, :, 1::2, :], ACT.Exp)
                    f(a[:, :, 0::2, :], a[:, :, 0::2, :], ACT.Exp).then_inc(exp_ok, 1)
                else:
                    f(A, A, ACT.Exp).then_inc(exp_ok, 1)

            def pieces(i):
                act.wait_ge(lev_ps, i + 1)
                if i == 0:
                    for b in range(2):
                        t = f(cross[:, 4 * b:4 * b + 4, :], ps[:, 4 + b, :].rearrange("p (h t) -> p h t", h=4))
                elif i == 1:
                    for b in range(2):
                        t = f(scoreT[0:64, 8 * b:8 * b + 8, 64:P], ps[0:64, 6 + b, :].rearrange("p (k t) -> p k t", k=8))
                else:
                    for q in (0, 2):
                        a = 32 * q
                        t = f(scoreT[a:a + 32, :, a + 32:a + 64],
                              ps[a:a + 32, level_bank(2), :].rearrange("p (k t) -> p k t", k=16))
                t.then_inc(lev_act, 1)

            for i in range(4):
                act.wait_ge(proj_ps, n + 1)
                f(h_qT[:, 2 * i:2 * i + 2, :], ps[:, n % 4, :].rearrange("p (h t) -> p h t", h=2), ACT.Silu).then_inc(proj_ev, 1)
                n += 1
                if i == 1:
                    exponentials(0)
                    exponentials(1)
                    exponentials(2)
            act.wait_ge(scores_clear, 1)
            pieces(0)
            exponentials(3)
            project_rows(22)
            pieces(1)
            exponentials(4)
            pieces(2)
            project_rows(23)
            exponentials(5)
            exponentials(6)
            exponentials(7)
            for n in range(24, 27):
                project_rows(n)
            for tt in range(TT):
                act.wait_ge(ho_ps, tt + 1)
                for h in range(HEADS):
                    t = f(part(odd, 6144 + (tt * HEADS + h) * P, P), ps[:, 4 + 2 * tt + h // 4, (h % 4) * P:(h % 4 + 1) * P], ACT.Square,
                          accum_out=o_sq[:, tt * HEADS + h:tt * HEADS + h + 1])
                t.then_inc(sq_ok, 1)
            act.wait_ge(ms_ok, 3)
            f(o_rs, o_sq, ACT.Sqrt).then_inc(root_ok, 1)
            project_rows(27)
            for tt in range(TT):
                out_copy(4 + tt, tt, 0, 4 + 2 * tt, norm_h)
            for tt in range(TT):
                out_copy(6 + tt, tt, 1, 5 + 2 * tt, norm_h)
            layer_norm(2)
            experts(1)
            layer_norm(3)

        @block.vector
        def _(dve):
            links = [0]

            def link(t):
                links[0] += 1
                t.then_inc(dve_chain, 1)
                dve.wait_ge(dve_chain, links[0])

            tt_op = nc.vector.tensor_tensor
            ts_op = nc.vector.tensor_scalar
            stt = nc.vector.scalar_tensor_tensor

            def wait_item(name, layer, c):
                k = ITEM[name, layer, c]
                n = sum(2 if ITEMS[i][0] == "ln" else 1 for i in range(k % 2, k + 1, 2))
                dve.wait_ge(stream_in[k % 2], 16 * n)
                return stream[:, k % 2, :]

            def xT_copies(b):
                for tt in range(TT) if b == 0 else (1,):
                    dve.wait_ge(xT_ps, 2 * b + tt + 1)
                    nc.vector.tensor_copy(xT[:, 4:8, tt * P:(tt + 1) * P],
                                          ps[:, 2 * tt + 1, :].rearrange("p (j t) -> p j t", j=4)).then_inc(xT_dve, 1)

            def layer_norm(n, outp=None):
                if n == 0:
                    dve.wait_ge(ln_in, 32)
                    w = ln_first
                else:
                    w = wait_item("ln", n // 2, n % 2)

                def add(tt, half):
                    cols = slice(half * BANK, (half + 1) * BANK)
                    link(stt(out=x[:, tt, cols], in0=x[:, tt, cols], scalar=ALPHA, in1=ps[:, tt * HALVES + half, :],
                             op0=ALU.mult, op1=ALU.add))
                    return nc.vector.bn_stats(stats[:, tt, half, :], x[:, tt, cols])

                def variance(tt, t):
                    link(t)
                    link(nc.vector.bn_aggr(mean_var[:, tt, :], stats[:, tt, :, :].rearrange("p a b -> p (a b)")))
                    ts_op(eps_var[:, tt:tt + 1], mean_var[:, tt, 1:2], EPS, None, ALU.add).then_inc(ln_var, 1)

                def finish(tt, source=None):
                    source = x[:, tt, :] if source is None else source
                    link(stt(out=x[:, tt, :], in0=source, scalar=mean_var[:, tt, 0:1], in1=w[:, 0:D],
                             op0=ALU.subtract, op1=ALU.mult))
                    dve.wait_ge(ln_std, 2 * n + tt + 1)
                    link(nc.vector.reciprocal(rstd[:, tt:tt + 1], rstd[:, tt:tt + 1]))
                    stt(out=x[:, tt, :], in0=x[:, tt, :], scalar=rstd[:, tt:tt + 1], in1=w[:, D:2 * D],
                        op0=ALU.mult, op1=ALU.add).then_inc(x_ready, 1)

                if outp is None:
                    dve.wait_ge(moe_ps, n // 2 + 1)
                    for tt in range(TT):
                        for half in range(HALVES):
                            t = nc.vector.bn_stats(stats[:, tt, half, :], ps[:, tt * HALVES + half, :])
                        variance(tt, t)
                        finish(tt, ps[:, tt * HALVES:(tt + 1) * HALVES, :].rearrange("p a b -> p (a b)"))
                else:
                    for half in range(HALVES):
                        for tt in range(TT):
                            dve.wait_ge(outp_ps, outp + half * TT + tt + 1)
                            t = add(tt, half)
                            if half:
                                variance(tt, t)
                                finish(tt)

            def split_x(layer, tt):
                dve.wait_ge(xhi_ok, TT * layer + tt + 1)
                tt_op(x_lo[:, tt, :, :], x[:, tt, :].rearrange("t (p j) -> t j p", j=J),
                      x_hi[:, tt, :, :].bitcast(F32), ALU.subtract).then_inc(x_split, 1)

            xT_copies(0)
            dve.wait_ge(vec_in, 64)
            dve.wait_ge(const_in, 32)
            ts_op(alpha_hi[:], ident, ALPHA, None, ALU.mult).then_inc(alpha_ok, 1)
            dve.wait_ge(alpha_ok, 1)
            stt(out=alpha_lo[:], in0=ident, scalar=ALPHA, in1=alpha_hi[:].bitcast(F32), op0=ALU.mult, op1=ALU.subtract).then_inc(alpha_ok, 1)
            link(tt_op(lam_prod, lam_row[:, 0::2, :], lam_row[:, 1::2, :], ALU.mult))
            nc.vector.tensor_reduce(lam2, lam_prod, AX, ALU.add).then_inc(lam_a, 1)
            dve.wait_ge(lam_b, 1)
            link(tt_op(neg_lam, lam2[:, 1:2], lam2[:, 0:1], ALU.subtract))
            link(ts_op(neg_lam, neg_lam, -LAMBDA_INIT, None, ALU.add))

            dve.wait_ge(lb_ps, 1)
            link(nc.vector.tensor_copy(lb_e.rearrange("p a h -> p (a h)"), ps[:, 6, 0:DEPTH * HEADS]))
            link(tt_op(lb_max, lb_e[:, 0, :], lb_e[:, 1, :], ALU.max))
            tt_op(lb_e, lb_e, lb_max[:, None, :].broadcast_to([P, DEPTH, HEADS]), ALU.subtract).then_inc(lb_exp_in, 1)
            dve.wait_ge(lb_exp_ok, 1)
            link(tt_op(lb_sum, lb_e[:, 0, :], lb_e[:, 1, :], ALU.add))
            link(nc.vector.reciprocal(lb_sum, lb_sum))
            link(tt_op(lb_e, lb_e, lb_sum[:, None, :].broadcast_to([P, DEPTH, HEADS]), ALU.mult))
            link(tt_op(lb_low, lb_e[:, 0, :], lb_e[:, 1, :], ALU.add))
            link(tt_op(lb_low, lb_low, lb_e[:, 0, :], ALU.subtract))
            link(ts_op(lb_rest, lb_low, -1.0, 1.0, ALU.mult, ALU.add))

            rope_tmp = [part(work, 128 * i, TT, HEADS, RH) for i in range(4)]
            cos = const("cos").rearrange("p (a r) -> p a r", a=TT)[:, :, None, :].broadcast_to([P, TT, HEADS, RH])
            sin = const("sin").rearrange("p (a r) -> p a r", a=TT)[:, :, None, :].broadcast_to([P, TT, HEADS, RH])

            def rope(i):
                dve.wait_ge(proj_ev, (2, 4, 8, 10)[i])
                if i:
                    dve.wait_ge(rope_ok, i)
                v = (q_tok, k_tok)[i % 2].rearrange("p a (h s) -> p a h s", s=SUB)[:, :, HEADS * (i // 2):HEADS * (i // 2 + 1), :]
                x1, x2 = v[:, :, :, 0:RH], v[:, :, :, RH:ROT]
                for t_, a_, b_ in zip(rope_tmp, (x1, x2, x2, x1), (cos, sin, cos, sin)):
                    t = tt_op(t_, a_, b_, ALU.mult)
                link(t)
                tt_op(x1, rope_tmp[0], rope_tmp[1], ALU.subtract)
                tt_op(x2, rope_tmp[2], rope_tmp[3], ALU.add).then_inc(rope_ok, 1)

            def turned(r):
                dve.wait_ge(turn_ps, r + 1)
                h = 4 * (r // 4) + 2
                dst = a_qT if r % 4 < 2 else a_kT
                nc.vector.tensor_copy(dst[:, h:h + 2, :],
                                      ps[:, TURN_BANK[r], :].rearrange("p (h t) -> p h t", h=2)).then_inc(turn_dve, 1)

            def front(h):
                u = h % 2
                dve.wait_ge(sc_ps, h + 1)
                nc.vector.tensor_reduce(row_max[:, u, 0:2], ps[:, 2 * u:2 * u + 2, 0:P], AX, ALU.max)
                link(nc.vector.tensor_reduce(row_max[:, u, 2:4], ps[:, 2 * u:2 * u + 2, P:P + SEQ], AX, ALU.max))
                ts_op(row_max[:, u, :], row_max[:, u, :], -SUB ** -0.5, None, ALU.mult).then_inc(nmax_ok, 1)

            def back(h):
                u = h % 2
                dve.wait_ge(probs_ok, h + 1)
                if h:
                    dve.wait_ge(diff_ok, h)
                link(nc.vector.reciprocal(row_scale, row_sum[:, u, :]))
                link(ts_op(row_scale[:, 1:4:2], row_scale[:, 1:4:2], neg_lam, None, ALU.mult))
                keys = (slice(0, P), slice(P, P + SEQ))
                for tile in range(2):
                    t = ts_op(probs[:, u, 1, keys[tile]], probs[:, u, 1, keys[tile]], row_scale[:, 2 * tile + 1:2 * tile + 2], None, ALU.mult)
                link(t)
                if h >= 2:
                    dve.wait_ge(dT_ps, h - 1)
                for tile in range(2):
                    t = stt(out=diff[:, u, keys[tile]], in0=probs[:, u, 0, keys[tile]], scalar=row_scale[:, 2 * tile:2 * tile + 1],
                            in1=probs[:, u, 1, keys[tile]], op0=ALU.mult, op1=ALU.add)
                t.then_inc(diff_ok, 1)

            def of_heads(v, hh):
                return v.rearrange("p (a h) -> p a h", a=TT)[:, :, 4 * hh:4 * hh + 4]

            def mean_square(hh):
                dve.wait_ge(o_ev, 4 * hh + 4)
                ts_op(of_heads(o_sq, hh), of_heads(o_sq, hh), 1.0 / P, EPS, ALU.mult, ALU.add).then_inc(ms_ok, 1)

            def norm_heads(hh):
                dve.wait_ge(root_ok, hh + 1)
                rs = of_heads(o_rs, hh)
                link(nc.vector.reciprocal(rs, rs))
                link(ts_op(rs, rs, 1.0 - LAMBDA_INIT, None, ALU.mult))
                for tt in range(TT):
                    v = a_o[:, tt, hh * BANK:(hh + 1) * BANK].rearrange("p (h n) -> p h n", h=4)
                    t = tt_op(v, v, rs[:, tt, :][:, :, None].broadcast_to([P, 4, P]), ALU.mult)
                t.then_inc(on_ok, 1)

            rope(0)
            rope(1)
            turned(1)
            turned(3)
            front(0)
            front(1)
            back(0)
            front(2)
            back(1)
            front(3)
            back(2)
            back(3)
            rope(2)
            turned(5)
            rope(3)
            mean_square(0)
            turned(7)
            front(4)
            front(5)
            back(4)
            norm_heads(0)
            front(6)
            back(5)
            front(7)
            back(6)
            back(7)
            mean_square(1)
            norm_heads(1)
            layer_norm(0, outp=0)

            def route(layer):
                dve.wait_ge(bias_in, 16 * (layer + 1))
                dve.wait_ge(score_ok, layer + 1)
                link(tt_op(choice, score, bias_row[:, None, :].broadcast_to([P, TT, NE]), ALU.add))
                groups = choice.rearrange("p a (g e) -> p (a g) e", e=GE)
                for i in range(TT * NG):
                    t = nc.vector.max(best8[:, i, :], groups[:, i, :])
                link(t)
                link(tt_op(g_sum, best8[:, :, 0], best8[:, :, 1], ALU.add))
                gv = g_sum.rearrange("p (a g) -> p a g", a=TT)
                r4, t4 = (v.rearrange("p (a g) k -> p a g k", a=TT) for v in (rank4, tie4))
                other = gv[:, :, None, :].broadcast_to([P, TT, NG, NG])
                own = gv[:, :, :, None].broadcast_to([P, TT, NG, NG])
                tt_op(r4, other, own, ALU.is_gt)
                link(tt_op(t4, other, own, ALU.is_equal))
                lower = const("lower").rearrange("p (g k) -> p g k", g=NG)[:, None, :, :].broadcast_to([P, TT, NG, NG])
                link(tt_op(t4, t4, lower, ALU.mult))
                link(tt_op(rank4, rank4, tie4, ALU.add))
                link(nc.vector.tensor_reduce(g_rank, rank4, AX, ALU.add))
                link(ts_op(g_rank, g_rank, float(TOPG), None, ALU.is_lt))
                link(ts_op(g_pen, g_rank, -1.0, BIG, ALU.add, ALU.mult))
                kg = kept.rearrange("p a (g e) -> p (a g) e", e=GE)
                link(tt_op(kg, groups, g_rank[:, :, None].broadcast_to([P, TT * NG, GE]), ALU.mult))
                link(tt_op(kg, kg, g_pen[:, :, None].broadcast_to([P, TT * NG, GE]), ALU.add))
                for tt in range(TT):
                    t = nc.vector.max(top8[:, tt, :], kept[:, tt, :])
                link(t)
                for tt in range(TT):
                    t = nc.vector.match_replace(out=replaced[:, tt, :], in_to_replace=top8[:, tt, :],
                                                in_values=kept[:, tt, :], imm_value=-3.3e38)
                link(t)
                tt_op(chosen, replaced, kept, ALU.not_equal).then_inc(chosen_ok, 1)
                dve.wait_ge(chosen_ok, layer + 1)
                link(tt_op(gate, score, chosen, ALU.mult))
                link(nc.vector.tensor_reduce(w_sum, gate, AX, ALU.add))
                link(ts_op(w_sum, w_sum, 1e-20, None, ALU.add))
                dve.wait_ge(pos_ps, layer + 1)
                stt(out=slot, in0=ps[:, 0, 0:P].rearrange("p (a e) -> p a e", a=TT), scalar=-NO_SLOT, in1=chosen,
                    op0=ALU.add, op1=ALU.mult).then_inc(route_ok, 1)

            def scale_gates():
                link(nc.vector.reciprocal(w_sum, w_sum))
                link(ts_op(w_sum, w_sum, ROUTED_SCALE, None, ALU.mult))
                tt_op(gate, gate, w_sum[:, :, None].broadcast_to([P, TT, NE]), ALU.mult).then_inc(gates_ok, 1)

            def list_overflow(layer):
                for b in range(1, BLOCKS):
                    t = ts_op(flags[:, (b - 1) * NE:b * NE], ps[:, 0, P:P + NE], float(b * SLOTS), None, ALU.is_gt)
                link(t)
                ones = const("ones")[:, 0:1].broadcast_to([P, EXTRA])
                link(nc.vector.tensor_tensor_scan(flags_sum, ones, flags, 0.0, ALU.mult, ALU.add))
                link(tt_op(listed, flags_sum, flags, ALU.subtract))
                link(stt(out=listed, in0=listed, scalar=const("row"), in1=flags, op0=ALU.is_equal, op1=ALU.mult))
                for i, name in enumerate(("ovf_e", "ovf_b")):
                    link(tt_op(listed_id, listed, const(name), ALU.mult))
                    t = nc.vector.tensor_reduce(ovf_cols[:, i:i + 1], listed_id, AX, ALU.add)
                    if i == 0:
                        link(t)
                t.then_inc(ovf_cols_ok, 1)

            def read_list(layer):
                dve.wait_ge(ovf_row_ps, layer + 1)
                nc.vector.tensor_copy(ovf_list[:, 0:1], flags_sum[0:1, EXTRA - 1:EXTRA])
                nc.vector.tensor_copy(ovf_list[:, 1:1 + 2 * OVF], ps[0:1, 0, P + NE:P + NE + 2 * OVF]).then_inc(ovf_ok, 1)

            def shared(layer, tt):
                dve.wait_ge(sh_silu, TT * layer + tt + 1)
                tt_op(hid[:, 1, :], silu[:, 1, :], ps[:, 5, FF:2 * FF], ALU.mult).then_inc(sh_hid, 1)

            def experts(layer):
                split_x(layer, 0)
                xT_copies(2 * layer + 1)
                split_x(layer, 1)
                route(layer)
                dve.wait_ge(route_ok, layer + 1)
                base = layer * PAIRS
                iota = const("iota")[:, 0:SLOTS][:, None, None, :].broadcast_to([P, TT, 2, SLOTS])

                def one_hot(g, e, u):
                    if u == 0 and (not isinstance(g, int) or g):
                        dve.wait_ge(xg_ps, 3 * g)
                    s = slot[:, :, e:e + 2] if isinstance(e, int) else slot[:, :, bass.ds(e, 2)]
                    tt_op(pick[:, u, :, :].rearrange("p a (e c) -> p a e c", e=2), iota,
                          s[:, :, :, None].broadcast_to([P, TT, 2, SLOTS]), ALU.is_equal).then_inc(pick_ok, 1)

                def hidden(g, u, bank=5):
                    dve.wait_ge(silu_ok, g + 1)
                    dve.wait_ge(xg_ev, 3 * g + (5, 3)[u])
                    stt(out=hid[:, u, :], in0=silu[:, u, :], scalar=gate_slot[:, u:u + 1], in1=ps[:, bank, FF:2 * FF],
                        op0=ALU.mult, op1=ALU.mult).then_inc(hid_ok, 1)

                def low_part(g, half):
                    dve.wait_ge(yhi_ok, 2 * g + half + 1)
                    tt_op(y_lo[:, half, :], ps[:, 5 + 2 * half, :], y_hi[:, half, :].bitcast(F32),
                          ALU.subtract).then_inc(ylo_ok, 1)

                def first_pairs():
                    hidden(base, 0)
                    hidden(base + 1, 1, bank=7)
                    one_hot(base + 2, 4, 0)
                    one_hot(base + 3, 6, 1)
                    for g in (base, base + 1):
                        for half in range(HALVES):
                            low_part(g, half)

                def step(p, e, u, more=True):
                    g = base + p
                    if u == 1 and more:
                        one_hot(g + 1, e + 2, 0)
                        one_hot(g + 2, e + 4, 1)
                    hidden(g, u)
                    for half in range(HALVES):
                        low_part(g, half)

                def steps(a, b):
                    with dve.Fori(a, b) as it:
                        for u in range(2):
                            step(it * 2 + u, it * 4 + 2 * u, u)

                one_hot(base, 0, 0)
                one_hot(base + 1, 2, 1)
                scale_gates()
                shared(layer, 0)
                list_overflow(layer)
                read_list(layer)
                first_pairs()
                steps(1, SHARED_AT // 2)
                shared(layer, 1)
                steps(SHARED_AT // 2, PAIRS // 2 - 1)
                step(PAIRS - 2, 0, 0, more=False)
                step(PAIRS - 1, 0, 1, more=False)

                s = OV[layer]
                n = dve.value_load(ovf_list[0:1, 0:1], min_val=0, max_val=OVF - 1)
                with dve.If(n > 0):
                    nc.vector.memset(pick[:, 0, :, SLOTS:P].bitcast(F32), 0.0)
                    with dve.Fori(0, n) as i:
                        e = dve.value_load(ovf_list[0:1, bass.ds(i + 1, 1)], min_val=0, max_val=NE - 1)
                        b = dve.value_load(ovf_list[0:1, bass.ds(i + (1 + OVF), 1)], min_val=0, max_val=BLOCKS - 1)
                        dve.wait_ge(s["done"], i + 1)
                        sl = slot[:, :, bass.ds(e, 1)].broadcast_to([P, TT, SLOTS])
                        io = cst[:, bass.ds(b * SLOTS + CONST_AT["iota"][0], SLOTS)][:, None, :].broadcast_to([P, TT, SLOTS])
                        tt_op(pick[:, 0, :, 0:SLOTS], io, sl, ALU.is_equal).then_inc(s["pick"], 1)
                        dve.wait_ge(s["silu"], i + 1)
                        stt(out=hid[:, 0, :], in0=silu[:, 0, :], scalar=gate_slot[:, 0:1], in1=ps[:, 5, FF:2 * FF],
                            op0=ALU.mult, op1=ALU.mult).then_inc(s["hid"], 1)
                        dve.wait_ge(s["yhi"], i + 1)
                        for half in range(HALVES):
                            t = tt_op(y_lo[:, half, :], ps[:, 5 + 2 * half, :], y_hi[:, half, :].bitcast(F32), ALU.subtract)
                        t.then_inc(s["ylo"], 1)
                with dve.Else():
                    dve.nop()

            experts(0)
            layer_norm(1)

            xT_copies(2)
            dve.wait_ge(proj_ev, 18)
            for h in range(HEADS):
                t = ts_op(h_b[:, h, :], h_b[:, h, :], lb_rest[:, h:h + 1], lb_low[:, h:h + 1], ALU.mult, ALU.add)
            link(t)
            link(ts_op(h_kT, h_b, -1.0, 1.0, ALU.mult, ALU.add))
            ts_op(h_b, h_b, FORGET_MIN, None, ALU.max).then_inc(forget_ok, 1)
            nc.vector.memset(scoreT, 0.0)
            nc.vector.memset(compact, 0.0).then_inc(scores_clear, 1)
            dve.wait_ge(logf_ok, 1)
            for h in range(HEADS):
                for c in range(SEQ // CHUNK):
                    v = h_b[:, h, c * CHUNK:(c + 1) * CHUNK]
                    t = nc.vector.tensor_tensor_scan(v, const("ones")[:, 0:CHUNK], v, 0.0, ALU.mult, ALU.add)
            link(t)
            b4 = h_b.rearrange("p h (c t) -> p h c t", c=4)

            def exponents(i):
                m, A = LEVELS[i], h_A[i % 3]
                if i >= 3:
                    dve.wait_ge(lev_ps, i - 2)
                last = b4[:, :, :, CHUNK - 1:CHUNK]
                A4 = A.rearrange("p h (c t) -> p h c t", c=4)
                wide = [P, HEADS, CHUNK]
                if m == 128:
                    link(tt_op(c01, last[:, :, 0], last[:, :, 1], ALU.add))
                    tt_op(A4[:, :, 0], c01.broadcast_to(wide), b4[:, :, 0], ALU.subtract)
                    tt_op(A4[:, :, 1], last[:, :, 1].broadcast_to(wide), b4[:, :, 1], ALU.subtract)
                    t = tt_op(A4[:, :, 3], b4[:, :, 3], last[:, :, 2].broadcast_to(wide), ALU.add)
                elif m == 64:
                    t = tt_op(A4[:, :, 0::2], last[:, :, 0::2].broadcast_to([P, HEADS, 2, CHUNK]), b4[:, :, 0::2], ALU.subtract)
                else:
                    a, b = (v.rearrange("p h t -> p (h t)").rearrange("p (n s m) -> p n s m", s=2, m=m) for v in (A, h_b))
                    mid = b[:, :, 0, m - 1:m].broadcast_to([P, HEADS * SEQ // (2 * m), m])
                    tt_op(a[:, :, 1], b[:, :, 1], mid, ALU.subtract)
                    t = tt_op(a[:, :, 0], mid, b[:, :, 0], ALU.subtract)
                t.then_inc(expo_ok, 1)

            def factors(i):
                m, A = LEVELS[i], h_A[i % 3]
                dve.wait_ge(exp_ok, i + 1)
                if i == 0:
                    dve.wait_ge(proj_ev, 22)
                a, q, k = (v.rearrange("p h t -> p (h t)").rearrange("p (n s m) -> p n s m", s=2, m=m) for v in (A, h_qT, h_kT))
                tt_op(a[:, :, 1], a[:, :, 1], q[:, :, 1], ALU.mult)
                tt_op(a[:, :, 0], a[:, :, 0], k[:, :, 0], ALU.mult).then_inc(lev_ok, 1)

            def merge(i):
                dve.wait_ge(lev_ps, i + 1)
                if i > 3:
                    dve.wait_ge(lev_dve, i - 3)
                which = masks[:, (i - 3) * 32:(i - 2) * 32][:, None, :].broadcast_to([P, HEADS * TT, 32])
                nc.vector.copy_predicated(compact, which, ps[:, level_bank(i), :].rearrange("p (k t) -> p k t", k=HEADS * TT))\
                  .then_inc(lev_dve, 1)

            dve.wait_ge(scores_clear, 1)
            exponents(0)
            exponents(1)
            exponents(2)
            for i in range(len(LEVELS)):
                factors(i)
                if 3 <= i + 2 < len(LEVELS):
                    exponents(i + 2)
                if i > 3:
                    merge(i - 1)
            merge(7)
            merge(8)
            dve.wait_ge(lev_dve, 6)
            for q in range(4):
                a = 32 * q
                t = nc.vector.tensor_copy(scoreT[a:a + 32, :, a:a + 32], compact[a:a + 32, :, :])
            t.then_inc(scores_ok, 1)
            dve.wait_ge(sq_ok, 2)
            ts_op(o_sq, o_sq, 1.0 / P, EPS, ALU.mult, ALU.add).then_inc(ms_ok, 1)
            dve.wait_ge(root_ok, 3)
            link(nc.vector.reciprocal(o_rs, o_rs))
            for tt in range(TT):
                for hh in range(2):
                    r = o_rs[:, tt * HEADS + 4 * hh:tt * HEADS + 4 * hh + 4][:, :, None].broadcast_to([P, 4, P])
                    t = tt_op(h_o[:, tt, hh * BANK:(hh + 1) * BANK].rearrange("p (h n) -> p h n", h=4),
                              ps[:, 4 + 2 * tt + hh, :].rearrange("p (h n) -> p h n", h=4), r, ALU.mult)
            link(t)
            for n in range(24, 28):
                dve.wait_ge(proj_ev, n + 1)
                v = (slice(None), n % 2, slice((n - 24) // 2 * BANK, ((n - 24) // 2 + 1) * BANK))
                tt_op(h_o[v], h_o[v], h_gate[v], ALU.mult).then_inc(on_ok, 1)
            layer_norm(2, outp=4)
            experts(1)
            layer_norm(3)


_INS = ["x", "attn_w_in", "attn_w_out", "attn_lambda", "attn_subln", "hgrn_w_in", "hgrn_w_out",
        "hgrn_lower_bounds", "hgrn_norm", "moe_router", "moe_router_bias", "moe_w_gate_up", "moe_w_down",
        "shared_w_gate_up", "shared_w_down", "ln_gain", "ln_bias"]


def kernel(**inputs):
    import concourse.bacc as bacc
    from concourse.bass_utils import run_bass_kernel_spmd

    nc = bacc.Bacc("TRN2", target_bir_lowering=False, num_devices=1)
    floats, masks = constants()
    arrays = {f"in_{name}": np.ascontiguousarray(inputs[name]) for name in _INS}
    arrays["in_constants"], arrays["in_level_masks"] = floats, masks
    args = [nc.dram_tensor(name, a.shape, mybir.dt.from_np(a.dtype), kind="ExternalInput").ap() for name, a in arrays.items()]
    out = nc.dram_tensor("out", (1, SEQ, D), F32, kind="ExternalOutput").ap()
    build_trunk(nc, *args, out)
    return run_bass_kernel_spmd(nc, [arrays], core_ids=[0]).results[0]["out"]
```
